# Optimizing a Trainium2 kernel written in Bass

```python
import math
import jax, jax.numpy as jnp
from jax import lax
import numpy as np

D_MODEL = 1024
BATCH = 1
SEQ = 512
DEPTH = 1

D_BRANCH = 512
N_BRANCHES = 3
EPS = 1e-6
GMLP_CHUNK = 128
GMLP_GROUPS = 4
GMLP_GDIM = D_BRANCH // GMLP_GROUPS
GLA_HEADS = 4
GLA_DK = D_BRANCH // 2 // GLA_HEADS
GLA_DV = D_BRANCH // GLA_HEADS
GLA_GATE_RANK = 16
GLA_GATE_TAU = 16.0
GLA_CHUNK = 64
DSA_HEADS = 4
DSA_HDIM = D_BRANCH // DSA_HEADS
DSA_IDX_HEADS = 4
DSA_IDX_DIM = 64
DSA_QBLOCK = 128
DSA_TOPK_MAX = 256
N_BUCKETS = 32
MAX_DISTANCE = 128
N_GROUPS = 4
EXPERTS_PER_GROUP = 4
N_EXPERTS = N_GROUPS * EXPERTS_PER_GROUP
D_EXPERT = 256
TOPK_IN_GROUP = 2

IN_SIZES = (
    D_BRANCH, D_BRANCH,
    GLA_HEADS * GLA_DK, GLA_HEADS * GLA_DK,
    GLA_HEADS * GLA_DV, GLA_HEADS * GLA_DV,
    GLA_GATE_RANK,
    DSA_HEADS * DSA_HDIM, DSA_HEADS * DSA_HDIM, DSA_HEADS * DSA_HDIM,
    DSA_IDX_HEADS * DSA_IDX_DIM, DSA_IDX_DIM, DSA_IDX_HEADS,
    N_BRANCHES * D_MODEL,
)
N_IN = sum(IN_SIZES)


def rms_norm(x, g):
    xf = x.astype(jnp.float32)
    y = xf * lax.rsqrt(jnp.mean(xf * xf, axis=-1, keepdims=True) + EPS)
    return (y * g.astype(jnp.float32)).astype(x.dtype)

def layer_norm(x, g, b):
    xf = x.astype(jnp.float32)
    mu = jnp.mean(xf, axis=-1, keepdims=True)
    var = jnp.mean(jnp.square(xf - mu), axis=-1, keepdims=True)
    y = (xf - mu) * lax.rsqrt(var + EPS)
    return (y * g.astype(jnp.float32) + b.astype(jnp.float32)).astype(x.dtype)

def t5_bucket(rel):
    n = jnp.maximum(rel, 0)
    max_exact = N_BUCKETS // 2
    large = max_exact + (
        jnp.log(jnp.maximum(n, max_exact).astype(jnp.float32) / max_exact)
        / math.log(MAX_DISTANCE / max_exact) * (N_BUCKETS - max_exact)
    ).astype(jnp.int32)
    large = jnp.minimum(large, N_BUCKETS - 1)
    return jnp.where(n < max_exact, n, large)

def gmlp_branch(u, v, ln_g, ln_b, w_s, b_s):
    bsz, s, _ = v.shape
    v = layer_norm(v, ln_g, ln_b)
    vc = v.reshape(bsz, s // GMLP_CHUNK, GMLP_CHUNK, GMLP_GROUPS, GMLP_GDIM)
    causal = jnp.tril(jnp.ones((GMLP_CHUNK, GMLP_CHUNK), dtype=bool))
    w = jnp.where(causal[None], w_s, jnp.zeros_like(w_s))
    mixed = jnp.einsum('gts,bcsgd->bctgd', w, vc) + b_s.T[:, :, None]
    return u * mixed.reshape(bsz, s, D_BRANCH)

def gla_scan(q, k, v, g):
    bsz, s, h, _ = q.shape
    out_dtype = v.dtype
    q = q.astype(jnp.float32) * (GLA_DK ** -0.5)

    def to_chunks(t):
        t = t.astype(jnp.float32)
        return t.reshape(bsz, s // GLA_CHUNK, GLA_CHUNK, h, t.shape[-1]).transpose(1, 0, 3, 2, 4)

    causal = jnp.tril(jnp.ones((GLA_CHUNK, GLA_CHUNK), dtype=bool))[None, None, :, :, None]

    def step(state, inp):
        qc, kc, vc, gc = inp
        b = jnp.cumsum(gc, axis=2)
        b_last = b[:, :, -1:, :]
        o_inter = jnp.einsum('bhtd,bhde->bhte', qc * jnp.exp(b), state)
        diff = b[:, :, :, None, :] - b[:, :, None, :, :]
        decay = jnp.where(causal, jnp.exp(jnp.minimum(diff, 0.0)), 0.0)
        attn = jnp.einsum('bhtd,bhsd,bhtsd->bhts', qc, kc, decay)
        o = o_inter + jnp.einsum('bhts,bhse->bhte', attn, vc)
        new_state = (jnp.exp(b_last[:, :, 0, :])[..., None] * state
                     + jnp.einsum('bhsd,bhse->bhde', kc * jnp.exp(b_last - b), vc))
        return new_state, o

    state0 = jnp.zeros((bsz, h, GLA_DK, GLA_DV), jnp.float32)
    _, o = lax.scan(step, state0, (to_chunks(q), to_chunks(k), to_chunks(v), to_chunks(g)))
    return o.transpose(1, 0, 3, 2, 4).reshape(bsz, s, h, GLA_DV).astype(out_dtype)

def dsa_attention(q, k, v, iq, ik, iw, rel_bias):
    bsz, s, h, hd = q.shape
    n_blocks = s // DSA_QBLOCK
    topk = min(DSA_TOPK_MAX, s // 4)
    key_pos = jnp.arange(s, dtype=jnp.int32)
    gather = jax.vmap(lambda arr, idx: arr[idx])

    def block(i):
        start = i * DSA_QBLOCK
        qb = lax.dynamic_slice_in_dim(q, start, DSA_QBLOCK, axis=1)
        iqb = lax.dynamic_slice_in_dim(iq, start, DSA_QBLOCK, axis=1)
        iwb = lax.dynamic_slice_in_dim(iw, start, DSA_QBLOCK, axis=1)
        qpos = start + jnp.arange(DSA_QBLOCK, dtype=jnp.int32)
        raw = jnp.einsum('bthd,bsd->bths', iqb, ik)
        score = jnp.einsum('bths,bth->bts', jax.nn.relu(raw), iwb).astype(jnp.float32)
        admissible = key_pos[None, :] <= qpos[:, None]
        score = jnp.where(admissible[None], score, -jnp.inf)
        _, top_idx = lax.top_k(score, topk)
        valid = top_idx <= qpos[None, :, None]
        kg = gather(k, top_idx)
        vg = gather(v, top_idx)
        logits = jnp.einsum('bthd,btkhd->btkh', qb, kg).astype(jnp.float32) * (hd ** -0.5)
        bias = rel_bias[t5_bucket(qpos[None, :, None] - top_idx)].astype(jnp.float32)
        logits = jnp.where(valid[..., None], logits + bias, -1e30)
        p = jax.nn.softmax(logits, axis=2).astype(v.dtype)
        return jnp.einsum('btkh,btkhd->bthd', p, vg)

    out = lax.map(block, jnp.arange(n_blocks))
    return out.transpose(1, 0, 2, 3, 4).reshape(bsz, s, h * hd)

def hybrid_mixer(h, w_in, gmlp_ln_g, gmlp_ln_b, gmlp_w_s, gmlp_b_s, gla_w_gate2, gla_b_gate,
                 gla_norm_g, dsa_qnorm_g, dsa_knorm_g, rel_bias, w_branch, b_branch_gate, w_out):
    bsz, s, _ = h.shape
    proj = h @ w_in
    splits = np.cumsum(IN_SIZES)[:-1].tolist()
    (a_u, a_v, g_q, g_k, g_v, g_r, g_a, d_q, d_k, d_v, d_iq, d_ik, d_iw, gates) = jnp.split(
        proj, splits, axis=-1)

    y_a = gmlp_branch(jax.nn.gelu(a_u), jax.nn.gelu(a_v), gmlp_ln_g, gmlp_ln_b, gmlp_w_s, gmlp_b_s)

    log_alpha = jax.nn.log_sigmoid((g_a @ gla_w_gate2 + gla_b_gate).astype(jnp.float32)) / GLA_GATE_TAU
    o_b = gla_scan(g_q.reshape(bsz, s, GLA_HEADS, GLA_DK), g_k.reshape(bsz, s, GLA_HEADS, GLA_DK),
                   g_v.reshape(bsz, s, GLA_HEADS, GLA_DV),
                   log_alpha.reshape(bsz, s, GLA_HEADS, GLA_DK))
    o_b = rms_norm(o_b, gla_norm_g) * jax.nn.silu(g_r.reshape(bsz, s, GLA_HEADS, GLA_DV))
    y_b = o_b.reshape(bsz, s, D_BRANCH)

    q = rms_norm(d_q.reshape(bsz, s, DSA_HEADS, DSA_HDIM), dsa_qnorm_g)
    k = rms_norm(d_k.reshape(bsz, s, DSA_HEADS, DSA_HDIM), dsa_knorm_g)
    y_c = dsa_attention(q, k, d_v.reshape(bsz, s, DSA_HEADS, DSA_HDIM),
                        d_iq.reshape(bsz, s, DSA_IDX_HEADS, DSA_IDX_DIM), d_ik, d_iw, rel_bias)

    ys = jnp.stack([y_a, y_b.astype(y_a.dtype), y_c.astype(y_a.dtype)], axis=0)
    up = jnp.einsum('nbse,ned->bsnd', ys, w_branch)
    gate = jax.nn.sigmoid(gates.reshape(bsz, s, N_BRANCHES, D_MODEL) + b_branch_gate)
    merged = jnp.sum(gate * up, axis=2)
    return (merged @ w_out).astype(h.dtype)

def hier_moe(h, w_group, b_group, w_router, b_router, w_exp_gate, w_exp_up, w_exp_down):
    bsz, s, d = h.shape
    hf = h.reshape(-1, d)
    grp_prob = jax.nn.softmax((hf @ w_group + b_group).astype(jnp.float32), axis=-1)
    p_g, g_idx = lax.top_k(grp_prob, 1)
    g_onehot = jax.nn.one_hot(g_idx[:, 0], N_GROUPS, dtype=jnp.float32)
    exp_logits = (hf @ w_router + b_router).astype(jnp.float32).reshape(-1, N_GROUPS, EXPERTS_PER_GROUP)
    sel_logits = jnp.einsum('tge,tg->te', exp_logits, g_onehot)
    top_vals, e_idx = lax.top_k(sel_logits, TOPK_IN_GROUP)
    weights = p_g * jax.nn.softmax(top_vals, axis=-1)
    eid = g_idx * EXPERTS_PER_GROUP + e_idx
    combine = jnp.einsum('tk,tke->te', weights,
                         jax.nn.one_hot(eid, N_EXPERTS, dtype=jnp.float32)).astype(hf.dtype)
    y = jnp.zeros_like(hf)
    for gi in range(N_GROUPS):
        sl = slice(gi * EXPERTS_PER_GROUP, (gi + 1) * EXPERTS_PER_GROUP)
        hg = jnp.einsum('td,edf->etf', hf, w_exp_gate[sl])
        hu = jnp.einsum('td,edf->etf', hf, w_exp_up[sl])
        act = jax.nn.silu(hg) * hu * combine[:, sl].T[:, :, None]
        y = y + jnp.einsum('etf,efd->td', act, w_exp_down[sl]).astype(hf.dtype)
    return y.reshape(bsz, s, d)

def first_inputs(seed: int = 0) -> dict:
    key = jax.random.key(seed)
    ks = jax.random.split(key, 28)
    L = DEPTH

    def nrm(k, shape, scale):
        return jax.random.normal(k, shape, jnp.float32) * scale

    return {
        "x": nrm(ks[0], (BATCH, SEQ, D_MODEL), 1.0),
        "c": nrm(ks[1], (BATCH, D_MODEL), 1.0),
        "w_mod": nrm(ks[2], (L, D_MODEL, 6 * D_MODEL), 0.5 * D_MODEL ** -0.5),
        "b_mod": nrm(ks[3], (L, 6 * D_MODEL), 0.02),
        "g_norm1": 1.0 + nrm(ks[4], (L, D_MODEL), 0.1),
        "g_norm2": 1.0 + nrm(ks[5], (L, D_MODEL), 0.1),
        "w_in": nrm(ks[6], (L, D_MODEL, N_IN), D_MODEL ** -0.5),
        "gmlp_ln_g": 1.0 + nrm(ks[7], (L, D_BRANCH), 0.1),
        "gmlp_ln_b": nrm(ks[8], (L, D_BRANCH), 0.02),
        "gmlp_w_s": nrm(ks[9], (L, GMLP_GROUPS, GMLP_CHUNK, GMLP_CHUNK), GMLP_CHUNK ** -0.5),
        "gmlp_b_s": 1.0 + nrm(ks[10], (L, GMLP_GROUPS, GMLP_CHUNK), 0.1),
        "gla_w_gate2": nrm(ks[11], (L, GLA_GATE_RANK, GLA_HEADS * GLA_DK), GLA_GATE_RANK ** -0.5),
        "gla_b_gate": nrm(ks[12], (L, GLA_HEADS * GLA_DK), 0.1),
        "gla_norm_g": 1.0 + nrm(ks[13], (L, GLA_DV), 0.1),
        "dsa_qnorm_g": 1.0 + nrm(ks[14], (L, DSA_HDIM), 0.1),
        "dsa_knorm_g": 1.0 + nrm(ks[15], (L, DSA_HDIM), 0.1),
        "rel_bias": nrm(ks[16], (N_BUCKETS, DSA_HEADS), 0.5),
        "w_branch": nrm(ks[17], (L, N_BRANCHES, D_BRANCH, D_MODEL), D_BRANCH ** -0.5),
        "b_branch_gate": nrm(ks[18], (L, N_BRANCHES, D_MODEL), 0.1),
        "w_out": nrm(ks[19], (L, D_MODEL, D_MODEL), D_MODEL ** -0.5),
        "w_group": nrm(ks[20], (L, D_MODEL, N_GROUPS), D_MODEL ** -0.5),
        "b_group": nrm(ks[21], (L, N_GROUPS), 0.01),
        "w_router": nrm(ks[22], (L, D_MODEL, N_EXPERTS), D_MODEL ** -0.5),
        "b_router": nrm(ks[23], (L, N_EXPERTS), 0.01),
        "w_exp_gate": nrm(ks[24], (L, N_EXPERTS, D_MODEL, D_EXPERT), D_MODEL ** -0.5),
        "w_exp_up": nrm(ks[25], (L, N_EXPERTS, D_MODEL, D_EXPERT), D_MODEL ** -0.5),
        "w_exp_down": nrm(ks[26], (L, N_EXPERTS, D_EXPERT, D_MODEL), D_EXPERT ** -0.5),
    }

def first_block(x, c, w_mod, b_mod, g_norm1, g_norm2, w_in, gmlp_ln_g, gmlp_ln_b, gmlp_w_s, gmlp_b_s,
              gla_w_gate2, gla_b_gate, gla_norm_g, dsa_qnorm_g, dsa_knorm_g, rel_bias, w_branch,
              b_branch_gate, w_out, w_group, b_group, w_router, b_router, w_exp_gate, w_exp_up,
              w_exp_down):
    c_act = jax.nn.silu(c)
    for l in range(DEPTH):
        mod = c_act @ w_mod[l] + b_mod[l]
        sh1, sc1, gt1, sh2, sc2, gt2 = [m[:, None, :] for m in jnp.split(mod, 6, axis=-1)]
        h = rms_norm(x, g_norm1[l]) * (1.0 + sc1) + sh1
        mix = hybrid_mixer(h, w_in[l], gmlp_ln_g[l], gmlp_ln_b[l], gmlp_w_s[l], gmlp_b_s[l],
                           gla_w_gate2[l], gla_b_gate[l], gla_norm_g[l], dsa_qnorm_g[l],
                           dsa_knorm_g[l], rel_bias, w_branch[l], b_branch_gate[l], w_out[l])
        x = (x + gt1 * mix).astype(x.dtype)
        h2 = rms_norm(x, g_norm2[l]) * (1.0 + sc2) + sh2
        ffn = hier_moe(h2, w_group[l], b_group[l], w_router[l], b_router[l],
                       w_exp_gate[l], w_exp_up[l], w_exp_down[l])
        x = (x + gt2 * ffn).astype(x.dtype)
    return x


MIX_WIDTH = D_MODEL
HEAD_DIM = 64
NSA_HEADS = 8
NSA_KV_GROUPS = 2
HEADS_PER_GROUP = NSA_HEADS // NSA_KV_GROUPS
NSA_WIDTH = NSA_HEADS * HEAD_DIM
KV_WIDTH = NSA_KV_GROUPS * HEAD_DIM
CONV_WIDTH = MIX_WIDTH - NSA_WIDTH
CONV_GROUPS = CONV_WIDTH // HEAD_DIM
CONV_K = 3
CMP_STRIDE = 16
CMP_BLOCK = 2 * CMP_STRIDE
CMP_HIDDEN = 128
SLC_BLOCK = 64
SLC_TOPK = 8
WINDOW = 256
Q_BLOCK = 64
FORCE_BONUS = 1.0e4
MEM_HEADS = 4
MEM_HEAD_DIM = 64
MEM_WIDTH = MEM_HEADS * MEM_HEAD_DIM
MEM_LEN = 256
FFN_HIDDEN = -(-8 * D_MODEL // (3 * 256)) * 256
RMS_EPS = 1e-6
NEG_INF = -1e30
IN_SIZES_2 = (NSA_WIDTH,) + (KV_WIDTH,) * 6 + (3 * NSA_HEADS,) + (CONV_WIDTH,) * 3
IN_WIDTH = sum(IN_SIZES_2)
IN_SPLITS = tuple(int(s) for s in np.cumsum(IN_SIZES_2)[:-1])


def rmsnorm(x, g):
    xf = x.astype(jnp.float32)
    y = xf * lax.rsqrt(jnp.mean(xf * xf, axis=-1, keepdims=True) + RMS_EPS)
    return (y * g.astype(jnp.float32)).astype(x.dtype)

def t5_bucket_2(dist):
    n = jnp.maximum(dist, 0)
    max_exact = N_BUCKETS // 2
    nf = jnp.maximum(n, 1).astype(jnp.float32)
    large = max_exact + (jnp.log(nf / max_exact) / math.log(MAX_DISTANCE / max_exact)
                         * (N_BUCKETS - max_exact)).astype(jnp.int32)
    large = jnp.minimum(large, N_BUCKETS - 1)
    return jnp.where(n < max_exact, n, large)

def masked_softmax(logits, mask, axis):
    maskf = mask.astype(jnp.float32)
    logits = jnp.where(mask, logits, NEG_INF)
    m = jnp.max(logits, axis=axis, keepdims=True)
    e = jnp.exp(logits - m) * maskf
    return e / jnp.maximum(jnp.sum(e, axis=axis, keepdims=True), 1e-30)

def compress_blocks(kv, pe, w1, w2):
    B, S, G, Dh = kv.shape
    ch = kv.reshape(B, S // CMP_STRIDE, CMP_STRIDE, G, Dh)
    blocks = jnp.concatenate([ch[:, :-1], ch[:, 1:]], axis=2)
    blocks = blocks + pe[None, None, :, None, :]
    n = blocks.shape[1]
    flat = blocks.transpose(0, 1, 3, 2, 4).reshape(B, n, G, CMP_BLOCK * Dh)
    return jax.nn.gelu(flat @ w1) @ w2

def nsa_attention(q, k_c, v_c, k_s, v_s, k_w, v_w, gates, rel_bias, pe, ck1, ck2, cv1, cv2):
    B, S, G, HPG, Dh = q.shape
    scale = Dh ** -0.5
    kcmp = compress_blocks(k_c, pe, ck1, ck2)
    vcmp = compress_blocks(v_c, pe, cv1, cv2)
    n_cmp = kcmp.shape[1]
    cmp_end = jnp.arange(n_cmp, dtype=jnp.int32) * CMP_STRIDE + CMP_BLOCK - 1
    n_slc = S // SLC_BLOCK
    topk = min(SLC_TOPK, n_slc)
    cs = np.arange(n_cmp) * CMP_STRIDE
    ss = np.arange(n_slc) * SLC_BLOCK
    ov = np.clip(np.minimum(cs[:, None] + CMP_BLOCK, ss[None, :] + SLC_BLOCK)
                 - np.maximum(cs[:, None], ss[None, :]), 0, None) / CMP_BLOCK
    ov = jnp.asarray(ov, dtype=jnp.float32)
    ks_blk = k_s.reshape(B, n_slc, SLC_BLOCK, G, Dh).transpose(0, 3, 1, 2, 4)
    vs_blk = v_s.reshape(B, n_slc, SLC_BLOCK, G, Dh).transpose(0, 3, 1, 2, 4)
    gather_blocks = jax.vmap(jax.vmap(lambda kb, ix: kb[ix]))
    rb_sel = rel_bias.reshape(G, HPG, N_BUCKETS).transpose(0, 2, 1)
    g_index = jnp.arange(G)[None, None, :, None, None]
    kw_pad = jnp.pad(k_w, ((0, 0), (WINDOW, 0), (0, 0), (0, 0)))
    vw_pad = jnp.pad(v_w, ((0, 0), (WINDOW, 0), (0, 0), (0, 0)))
    kw_len = WINDOW + Q_BLOCK
    dist_w = jnp.arange(Q_BLOCK)[:, None] + WINDOW - jnp.arange(kw_len)[None, :]
    band = (dist_w >= 0) & (dist_w < WINDOW)
    bias_w = rel_bias[:, t5_bucket_2(dist_w)].reshape(G, HPG, Q_BLOCK, kw_len).transpose(2, 0, 1, 3)

    def chunk(args):
        c, q_c, g_c = args
        t = c * Q_BLOCK + jnp.arange(Q_BLOCK, dtype=jnp.int32)
        dist_c = t[:, None] - cmp_end[None, :]
        bias_c = rel_bias[:, t5_bucket_2(dist_c)].reshape(G, HPG, Q_BLOCK, n_cmp).transpose(2, 0, 1, 3)
        lg = jnp.einsum('bqghd,bngd->bqghn', q_c, kcmp).astype(jnp.float32) * scale + bias_c
        p_cmp = masked_softmax(lg, (dist_c >= 0)[:, None, None, :], -1)
        o_cmp = jnp.einsum('bqghn,bngd->bqghd', p_cmp, vcmp.astype(jnp.float32))
        imp = jnp.einsum('bqghn,nj->bqgj', p_cmp, ov)
        blk = jnp.arange(n_slc, dtype=jnp.int32)[None, :]
        cur = (t // SLC_BLOCK)[:, None]
        valid = blk <= cur
        forced = (blk == 0) | (blk == cur) | (blk == cur - 1)
        score = jnp.where(valid[:, None, :], imp + jnp.where(forced, FORCE_BONUS, 0.0)[:, None, :], NEG_INF)
        top_val, top_idx = lax.top_k(score, topk)
        sel_ok = top_val > 0.5 * NEG_INF
        idx_bg = top_idx.transpose(0, 2, 1, 3)
        k_sel = gather_blocks(ks_blk, idx_bg)
        v_sel = gather_blocks(vs_blk, idx_bg)
        pos = top_idx[..., None] * SLC_BLOCK + jnp.arange(SLC_BLOCK, dtype=jnp.int32)
        dist_s = t[None, :, None, None, None] - pos
        mask_s = sel_ok[..., None] & (dist_s >= 0)
        bias_s = jnp.moveaxis(rb_sel[g_index, t5_bucket_2(dist_s)], -1, 3)
        lg = jnp.einsum('bqghd,bgqkjd->bqghkj', q_c, k_sel).astype(jnp.float32) * scale + bias_s
        p_sel = masked_softmax(lg, mask_s[:, :, :, None], (-2, -1))
        o_sel = jnp.einsum('bqghkj,bgqkjd->bqghd', p_sel, v_sel.astype(jnp.float32))
        kw_c = lax.dynamic_slice_in_dim(kw_pad, c * Q_BLOCK, kw_len, axis=1)
        vw_c = lax.dynamic_slice_in_dim(vw_pad, c * Q_BLOCK, kw_len, axis=1)
        s_pos = c * Q_BLOCK - WINDOW + jnp.arange(kw_len, dtype=jnp.int32)
        mask_w = band & (s_pos >= 0)[None, :]
        lg = jnp.einsum('bqghd,bkgd->bqghk', q_c, kw_c).astype(jnp.float32) * scale + bias_w
        p_win = masked_softmax(lg, mask_w[:, None, None, :], -1)
        o_win = jnp.einsum('bqghk,bkgd->bqghd', p_win, vw_c.astype(jnp.float32))
        out = g_c[..., 0:1] * o_cmp + g_c[..., 1:2] * o_sel + g_c[..., 2:3] * o_win
        return out.astype(q.dtype)

    nc = S // Q_BLOCK
    q_chunks = jnp.moveaxis(q.reshape(B, nc, Q_BLOCK, G, HPG, Dh), 1, 0)
    g_chunks = jnp.moveaxis(gates.reshape(B, nc, Q_BLOCK, G, HPG, 3), 1, 0)
    out = lax.map(chunk, (jnp.arange(nc, dtype=jnp.int32), q_chunks, g_chunks))
    return jnp.moveaxis(out, 0, 1).reshape(B, S, G, HPG, Dh)

def hybrid_mixer_2(h, w_in, w_out, gn_nsa, gn_conv, conv_w, rel_bias, pe, ck1, ck2, cv1, cv2):
    B, S, _ = h.shape
    proj = h @ w_in
    q, kc, vc, ks, vs, kw, vw, gl, cb, cc, cx = jnp.split(proj, IN_SPLITS, axis=-1)
    G, HPG, Dh = NSA_KV_GROUPS, HEADS_PER_GROUP, HEAD_DIM
    kvr = lambda a: a.reshape(B, S, G, Dh)
    gates = jax.nn.sigmoid(gl.astype(jnp.float32)).reshape(B, S, G, HPG, 3)
    o_nsa = nsa_attention(q.reshape(B, S, G, HPG, Dh), kvr(kc), kvr(vc), kvr(ks), kvr(vs),
                          kvr(kw), kvr(vw), gates, rel_bias, pe, ck1, ck2, cv1, cv2)
    o_nsa = o_nsa.reshape(B, S, NSA_WIDTH)
    u = cc * cx
    u_pad = jnp.pad(u, ((0, 0), (CONV_K - 1, 0), (0, 0)))
    y = sum(conv_w[k] * u_pad[:, CONV_K - 1 - k: CONV_K - 1 - k + S] for k in range(CONV_K))
    o_conv = cb * y
    merged = jnp.concatenate([rmsnorm(o_nsa, gn_nsa), rmsnorm(o_conv, gn_conv)], axis=-1)
    return merged @ w_out

def memory_attention(h, mem_n, wq, wkv, wo):
    B, S, _ = h.shape
    M = mem_n.shape[1]
    q = (h @ wq).reshape(B, S, MEM_HEADS, MEM_HEAD_DIM)
    k, v = jnp.split(mem_n @ wkv, 2, axis=-1)
    k = k.reshape(B, M, MEM_HEADS, MEM_HEAD_DIM)
    v = v.reshape(B, M, MEM_HEADS, MEM_HEAD_DIM)
    lg = jnp.einsum('bshd,bmhd->bhsm', q, k).astype(jnp.float32) * (MEM_HEAD_DIM ** -0.5)
    p = jax.nn.softmax(lg, axis=-1)
    o = jnp.einsum('bhsm,bmhd->bshd', p, v.astype(jnp.float32)).reshape(B, S, MEM_WIDTH)
    return o.astype(h.dtype) @ wo

def swiglu(h, wg, wu, wd):
    return (jax.nn.silu(h @ wg) * (h @ wu)) @ wd

def second_inputs(seed: int = 0) -> dict:
    key = jax.random.key(seed)
    ks = jax.random.split(key, 24)
    f32 = jnp.float32
    nrm = lambda k, shape, fan_in: jax.random.normal(k, shape, f32) * fan_in ** -0.5
    gain = lambda k, shape: 1.0 + 0.05 * jax.random.normal(k, shape, f32)
    return {
        "x": jax.random.normal(ks[0], (BATCH, SEQ, D_MODEL), f32),
        "mem": jax.random.normal(ks[1], (BATCH, MEM_LEN, D_MODEL), f32),
        "rel_bias": 0.3 * jax.random.normal(ks[2], (NSA_HEADS, N_BUCKETS), f32),
        "norms": gain(ks[3], (DEPTH, 6, D_MODEL)),
        "mem_norm": gain(ks[4], (DEPTH, D_MODEL)),
        "gn_nsa": gain(ks[5], (DEPTH, NSA_WIDTH)),
        "gn_conv": gain(ks[6], (DEPTH, CONV_WIDTH)),
        "w_in": nrm(ks[7], (DEPTH, D_MODEL, IN_WIDTH), D_MODEL),
        "w_out": nrm(ks[8], (DEPTH, MIX_WIDTH, D_MODEL), MIX_WIDTH),
        "cmp_pe": 0.1 * jax.random.normal(ks[9], (DEPTH, CMP_BLOCK, HEAD_DIM), f32),
        "cmp_k_w1": nrm(ks[10], (DEPTH, CMP_BLOCK * HEAD_DIM, CMP_HIDDEN), CMP_BLOCK * HEAD_DIM),
        "cmp_k_w2": nrm(ks[11], (DEPTH, CMP_HIDDEN, HEAD_DIM), CMP_HIDDEN),
        "cmp_v_w1": nrm(ks[12], (DEPTH, CMP_BLOCK * HEAD_DIM, CMP_HIDDEN), CMP_BLOCK * HEAD_DIM),
        "cmp_v_w2": nrm(ks[13], (DEPTH, CMP_HIDDEN, HEAD_DIM), CMP_HIDDEN),
        "conv_w": nrm(ks[14], (DEPTH, CONV_K, CONV_WIDTH), CONV_K),
        "mem_wq": nrm(ks[15], (DEPTH, D_MODEL, MEM_WIDTH), D_MODEL),
        "mem_wkv": nrm(ks[16], (DEPTH, D_MODEL, 2 * MEM_WIDTH), D_MODEL),
        "mem_wo": nrm(ks[17], (DEPTH, MEM_WIDTH, D_MODEL), MEM_WIDTH),
        "ffn_wg": nrm(ks[18], (DEPTH, D_MODEL, FFN_HIDDEN), D_MODEL),
        "ffn_wu": nrm(ks[19], (DEPTH, D_MODEL, FFN_HIDDEN), D_MODEL),
        "ffn_wd": nrm(ks[20], (DEPTH, FFN_HIDDEN, D_MODEL), FFN_HIDDEN),
    }

def second_block(x, mem, rel_bias, norms, mem_norm, gn_nsa, gn_conv, w_in, w_out, cmp_pe,
              cmp_k_w1, cmp_k_w2, cmp_v_w1, cmp_v_w2, conv_w, mem_wq, mem_wkv, mem_wo,
              ffn_wg, ffn_wu, ffn_wd):
    for l in range(DEPTH):
        h = hybrid_mixer_2(rmsnorm(x, norms[l, 0]), w_in[l], w_out[l], gn_nsa[l], gn_conv[l], conv_w[l],
                         rel_bias, cmp_pe[l], cmp_k_w1[l], cmp_k_w2[l], cmp_v_w1[l], cmp_v_w2[l])
        x = x + rmsnorm(h, norms[l, 1])
        h = memory_attention(rmsnorm(x, norms[l, 2]), rmsnorm(mem, mem_norm[l]),
                             mem_wq[l], mem_wkv[l], mem_wo[l])
        x = x + rmsnorm(h, norms[l, 3])
        h = swiglu(rmsnorm(x, norms[l, 4]), ffn_wg[l], ffn_wu[l], ffn_wd[l])
        x = x + rmsnorm(h, norms[l, 5])
    return x


def setup_inputs(seed=0):
    out = dict(first_inputs(seed))
    for name, value in second_inputs(seed + 1).items():
        if name != "x":
            out[name + "_2"] = value
    return out


def reference(
    x, c, w_mod, b_mod, g_norm1, g_norm2, w_in, gmlp_ln_g, gmlp_ln_b, gmlp_w_s, gmlp_b_s,
    gla_w_gate2, gla_b_gate, gla_norm_g, dsa_qnorm_g, dsa_knorm_g, rel_bias, w_branch,
    b_branch_gate, w_out, w_group, b_group, w_router, b_router, w_exp_gate, w_exp_up,
    w_exp_down, mem_2, rel_bias_2, norms_2, mem_norm_2, gn_nsa_2, gn_conv_2, w_in_2, w_out_2,
    cmp_pe_2, cmp_k_w1_2, cmp_k_w2_2, cmp_v_w1_2, cmp_v_w2_2, conv_w_2, mem_wq_2, mem_wkv_2,
    mem_wo_2, ffn_wg_2, ffn_wu_2, ffn_wd_2,
):
    x = first_block(
        x, c, w_mod, b_mod, g_norm1, g_norm2, w_in, gmlp_ln_g, gmlp_ln_b, gmlp_w_s, gmlp_b_s,
        gla_w_gate2, gla_b_gate, gla_norm_g, dsa_qnorm_g, dsa_knorm_g, rel_bias, w_branch,
        b_branch_gate, w_out, w_group, b_group, w_router, b_router, w_exp_gate, w_exp_up,
        w_exp_down,
    )
    return second_block(
        x, mem_2, rel_bias_2, norms_2, mem_norm_2, gn_nsa_2, gn_conv_2, w_in_2, w_out_2,
        cmp_pe_2, cmp_k_w1_2, cmp_k_w2_2, cmp_v_w1_2, cmp_v_w2_2, conv_w_2, mem_wq_2, mem_wkv_2,
        mem_wo_2, ffn_wg_2, ffn_wu_2, ffn_wd_2,
    )


_drawn_inputs = setup_inputs


def setup_inputs(seed=0):
    import zlib

    import numpy as np

    out = dict(_drawn_inputs(seed))
    spreads = {}
    factors = {'gmlp_ln_g': 5.03,
     'gmlp_ln_b': 32.152,
     'gmlp_b_s': 3.288,
     'gla_b_gate': 6.562,
     'gla_norm_g': 3.509,
     'dsa_qnorm_g': 8.0,
     'dsa_knorm_g': 8.0,
     'rel_bias': 2.714,
     'b_branch_gate': 4.902,
     'b_group': 49.258,
     'b_router': 55.357}
    for name, (base, spread) in spreads.items():
        noise = np.random.default_rng([zlib.crc32(name.encode()), seed]).standard_normal(out[name].shape)
        drawn = base * np.exp(spread * noise) if base else spread * noise
        out[name] = __import__('jax').numpy.asarray(drawn.astype(out[name].dtype))
    for name, factor in factors.items():
        out[name] = (out[name] * factor).astype(out[name].dtype)
    return out
```

```python
from contextlib import ExitStack

import numpy as np
import concourse.bass as bass
from concourse import mybir
from concourse.alu_op_type import AluOpType as ALU

ACT = mybir.ActivationFunctionType
F32 = mybir.dt.float32
F32R = mybir.dt.float32r
U32 = mybir.dt.uint32
AX = mybir.AxisListType

P = 128
S = 512
ST = S // P
D = 1024
KD = D // P
NEG = -1e30
NOT_ADMITTED = -3e38
PIECE = 16
RAW_SLOTS = 3
SPLIT_SLOTS = 2
BANKS = 6
MEM = 256
HID = 2816
NBUCKET = 32
TOPK = 128
NCMP = S // 16 - 1
LEVELS = 8
EXPERTS, EPG = 16, 4

COLS = {"c": 8, "b_mod": 48, "g1": 8, "g2": 8, "gla_b": 2, "gla_g": 1, "qn": 1, "kn": 1,
        "b_gate": 24, "norms": 48, "mem_norm": 8, "gn_nsa": 4, "gn_conv": 4, "conv_w": 12, "eps": 1}
ROWS = {"ln_g": 512, "ln_b": 512, "b_s": 512, "b_router": 20}
CONST = {"ident": 128, "ones": 128, "causal": 128, "noadm": 128, "band": 128, "levels": 8 * 128, "cmpmask": ST * 32}


def offsets(sizes):
    at, out = 0, {}
    for name, n in sizes.items():
        out[name] = at
        at += n
    return out, at


COL, NCOL = offsets(COLS)
ROW, NROW = offsets(ROWS)
CON, NCONST = offsets(CONST)

REV = 384
FWD = 1024
VEC = REV + FWD

STREAM = ([("mod0", 8), ("av", 2), ("au", 2), ("gqk", 2), ("misc", 2), ("gv", 2), ("gr", 2),
           ("merge0", 6), ("dq", 2), ("dk", 2), ("dv", 2), ("merge1", 6), ("mod1", 16), ("merge2", 6), ("wout", 4)]
          + [(f"moe{g}", 12) for g in range(4)]
          + [("kcvc", 1), ("kskw", 1), ("vsvw", 1), ("conv", 6), ("q", 2), ("gl", 1), ("wout2", 4),
             ("memk", 1), ("memv", 1), ("memq", 1), ("memo", 1), ("ffn0", 12), ("ffn1", 12), ("ffn2", 9)])
NPIECES = sum(n for _, n in STREAM)
KIND = []
for _name, _n in STREAM:
    for _ in range(_n):
        KIND.append("mod" if _name.startswith("mod") else "split")

SPLITS, NSPLITS = offsets({"h1": 8, "ya": 4, "yb": 4, "yc": 4, "merged": 8, "h2": 8,
                           "moe0": 8, "moe1": 8, "moe2": 8, "moe3": 8, "n0": 8, "conv": 4, "nsa": 4,
                           "mem": 8, "n2": 8, "mo": 2, "n4": 8, "ffn0": 8, "ffn1": 8, "ffn2": 6})
FFN_TILES = [8, 8, 6]


def build(nc, stream, xT, memT, cols_d, rows_d, const_d, wsT, gate2_d, relT, onehot, router_d,
          cw1_d, cw2_d, peT, out):
    ctx = ExitStack()
    with ctx:
        sems = {}

        def sem(name):
            if name not in sems:
                sems[name] = ctx.enter_context(nc.semaphore("s_" + name))
            return sems[name]

        def sb(name, shape, dt=F32):
            return ctx.enter_context(nc.sbuf_tensor("b_" + name, shape, dt))

        raw = sb("raw", [P, RAW_SLOTS, PIECE * P])
        whi = sb("whi", [P, SPLIT_SLOTS, PIECE * P], F32R)
        wlo = sb("wlo", [P, SPLIT_SLOTS, PIECE * P], F32R)
        hhi = sb("hhi", [P, KD, S], F32R)
        hlo = sb("hlo", [P, KD, S], F32R)
        ahi = sb("ahi", [P, KD, S], F32R)
        alo = sb("alo", [P, KD, S], F32R)
        X = sb("x", [P, KD, S])
        Y = sb("y", [P, KD, S])
        con = sb("con", [P, NCONST])
        cols = sb("cols", [P, NCOL])
        mod = sb("mod", [P, 48])
        cact = sb("cact", [P, 8])
        gain = sb("gain", [P, 8])
        g2 = sb("gate2", [16, 256])
        router = sb("router", [P, 8, 20])
        small = sb("small", [P, 544])
        ARENA = 11264
        arena = sb("arena", [P, ARENA])
        ps = ctx.enter_context(nc.psum_tensor("ps", [P, BANKS + 2, 512], F32))
        vec_d = nc.dram_tensor("bias_vectors", (12, VEC), F32, kind="Internal").ap()
        near_d = nc.dram_tensor("bias_near", (12, P, REV), F32, kind="Internal").ap()
        comp_d = nc.dram_tensor("bias_compressed", (8, NCMP, FWD), F32, kind="Internal").ap()

        def ar(off, n):
            assert off + n <= ARENA, (off, n)
            return arena[:, off:off + n]

        def tiles(ap, n):
            return ap.rearrange("p (a n) -> p a n", a=n)

        Xf = X[:, :, :].rearrange("p k s -> p (k s)")
        Yf = Y[:, :, :].rearrange("p k s -> p (k s)")
        ident = con[:, CON["ident"]:CON["ident"] + P]
        ones = con[:, CON["ones"]:CON["ones"] + P]
        causal = con[:, CON["causal"]:CON["causal"] + P]
        noadm = con[:, CON["noadm"]:CON["noadm"] + P]
        band = con[:, CON["band"]:CON["band"] + P]
        levelmask = tiles(con[:, CON["levels"]:CON["levels"] + LEVELS * P], LEVELS)
        cmpmask = tiles(con[:, CON["cmpmask"]:CON["cmpmask"] + ST * 32], ST)
        eps = cols[:, COL["eps"]:COL["eps"] + 1]

        def col(name, i=0, n=1):
            return cols[:, COL[name] + i:COL[name] + i + n]

        bn = small[:, 0:24].rearrange("p (c n) -> p c n", c=4)
        mv = small[:, 24:32].rearrange("p (c n) -> p c n", c=4)
        lnr = small[:, 32:36]
        iwt = small[:, 36:52].rearrange("p (a h) -> p a h", a=ST)
        max8 = small[:, 52:60]
        cnt = small[:, 60:61]
        stat = small[:, 64:80]
        kcmp = small[:, 80:112]
        glt = small[:, 112:208].rearrange("p (a h) -> p a h", a=ST)
        pehid = small[:, 208:210]
        scol = small[:, 216:344]
        sq = [ar(8704, 512), ar(9216, 512)]
        rstd = ar(9728, 512)
        tmp = [ar(10240, 512), ar(10752, 512)]
        accmod = ar(8192, 512)
        vecs = arena[0:12, 0:VEC]
        ebl = stat[:, 0:8]
        gv_ = tiles(ar(0, 2048), ST)
        gu_ = tiles(ar(2048, 2048), ST)
        wsm = tiles(ar(4096, 512), 4)
        rows = Yf[:, 0:NROW]
        qg = tiles(ar(4608, 1024), 2)
        kg = tiles(ar(5632, 1024), 2)
        vg = tiles(Xf[:, 0:2048], ST)
        rg = tiles(Xf[:, 2048:4096], 4)
        bcum = ar(0, 1024)
        edec = ar(1024, 1024)
        qs = tiles(ar(2048, 1024), 2)
        ksc = tiles(ar(3072, 1024), 2)
        ktok = tiles(ar(1024, 1024), ST)
        state = tiles(ar(4096, 768), 3)
        attn = ar(8192, 2048)
        og = tiles(ar(0, 2048), 4)
        iq = tiles(ar(6656, 1024), 2)
        ik = ar(7680, 512)
        misc = ar(8192, 512)
        dq = tiles(ar(0, 2048), 4)
        dk = tiles(ar(2048, 2048), 4)
        dv = tiles(Xf[:, 0:2048], ST)
        selmask = [None, ar(4096, 256), ar(4352, 384), ar(4736, 512)]
        work = ar(5248, 512)
        eqm = Xf[:, 3072:3584]
        cum = Xf[:, 3584:4096]
        bt1 = tiles(Xf[:, 2048:3072], 4)
        p1 = [Xf[:, 3072:3584], Xf[:, 3584:4096], ar(6272, 512), ar(6784, 512)]
        pt1 = [ar(5248, 512), ar(5760, 512), ar(7296, 512)]
        combT = arena[0:16, 0:512]
        sil = [ar(512, 512), ar(1024, 512)]
        combs = [ar(1536, 512), ar(2048, 512)]
        kc2 = ar(0, 1024).rearrange("p (g t) -> p g t", g=2)
        vc2 = ar(1024, 1024).rearrange("p (g t) -> p g t", g=2)
        kcvc = tiles(ar(2048, 1024), 2)
        ks2 = ar(4096, 512)
        kw2 = ar(4608, 512)
        vsw = tiles(ar(5120, 1024), ST)
        cw1 = tiles(ar(6144, 4096), 2)
        chid = ar(3072, 128)
        cw2 = ar(3200, 128)
        pe_s = ar(3328, 16)
        vcmp = small[0:NCMP, 216:344]
        convc = ar(8192, 512)
        convo = tiles(ar(6144, 2048), 4)
        glf = ar(8192, 512)
        q2 = tiles(ar(0, 2048), 4)
        bt2 = tiles(ar(2048, 2048), 8)
        bct = Yf[:, 0:2048].rearrange("p (j t) -> p j t", j=4)
        p2 = [ar(8192, 512), ar(10240, 512), ar(10752, 512), rstd]
        pt2 = [ar(8704, 512), ar(9216, 512), Yf[:, 2048:2560]]
        onsa = tiles(ar(6144, 2048), 4)
        memx = tiles(ar(0, 2048), 8)
        mk = tiles(ar(2048, 512), 2)
        mv_ = tiles(ar(2560, 512), 2)
        mq = tiles(ar(3072, 1024), 2)
        om = tiles(ar(4096, 1024), 2)
        p3 = [ar(5120, 512), ar(5632, 512), ar(6144, 512), ar(6656, 512)]
        pt3 = [ar(7168, 512), ar(7680, 512), ar(8192, 512)]
        probs = {"dsa": p1, "nsa": p2, "mem": p3}
        probsT = {"dsa": pt1, "nsa": pt2, "mem": pt3}


        done = {}
        marks = [0]
        opened = []
        bank_of = {}
        handed = {}
        piece_end = []
        squares = []
        here = {"piece": -1, "tile": PIECE}

        def mark(ins, *keys):
            marks[0] += 1
            ins.then_inc(sem("matmuls_done"), 1)
            for k in keys:
                done[k] = marks[0]

        jobs1 = [("dsa", T, h, T + 1, (T + 1) * P) for T in range(ST) for h in range(4)]
        jobs2 = []
        for T in range(ST):
            jobs2 += [("cmp", T, (0, g), 4, NCMP) for g in range(2)]
            for j in range(4):
                for g in range(2):
                    n = min(T, 2) + 1
                    jobs2.append(("win", T, (j, g), n, n * P))
                    jobs2.append(("sel", T, (j, g), T + 1, (T + 1) * P))
        jobs3 = [("mem", T, h, 2, MEM) for T in range(ST) for h in range(4)]
        TLAG = 3

        def heads(ap):
            return tiles(ap[:, 0:P], 4)[:, :, 0:NCMP]

        block = ctx.enter_context(nc.Block())

        @block.tensor
        def _(pe):
            def open_bank(key, frees):
                n = len(opened)
                if n >= BANKS:
                    pe.wait_ge(sem(opened[n - BANKS][0]), opened[n - BANKS][1])
                handed[frees] = handed.get(frees, 0) + 1
                opened.append((frees, handed[frees]))
                bank_of[key] = n % BANKS
                return ps[:, n % BANKS, :]

            def open_output(key, frees):
                n = handed.get(frees, 0)
                if n >= 2:
                    pe.wait_ge(sem(frees), n - 1)
                handed[frees] = n + 1
                bank_of[key] = BANKS + n % 2
                return ps[:, BANKS + n % 2, :]

            def weight_tile():
                if here["tile"] == PIECE:
                    here["tile"] = 0
                    here["piece"] += 1
                    pe.wait_ge(sem("weights_split"), here["piece"] + 1)
                n, slot = here["tile"], here["piece"] % SPLIT_SLOTS
                here["tile"] += 1
                return slot, n * P

            def piece_over(ins, *keys):
                mark(ins, *keys)
                piece_end.append(marks[0])

            def three(o, ahi_, alo_, bhi_, blo_, start, stop):
                pe.matmul(o, ahi_, bhi_, start=start, stop=False)
                pe.matmul(o, ahi_, blo_, start=False, stop=False)
                return pe.matmul(o, alo_, bhi_, start=False, stop=stop)

            def linear(key, outs, nk, hi, lo, k0, frees, split_key=None, n=S):
                for m in outs:
                    o = open_bank((key, m), frees(m) if callable(frees) else frees)
                    for k in range(nk):
                        if split_key and m == outs[0]:
                            pe.wait_ge(sem("lo"), SPLITS[split_key] + k + 1)
                        slot, c = weight_tile()
                        ins = three(o[:, 0:n], whi[:, slot, c:c + P], wlo[:, slot, c:c + P],
                                    hi[:, k0 + k, 0:n], lo[:, k0 + k, 0:n], k == 0, k == nk - 1)
                        keys = [(key, m)] if k == nk - 1 else []
                        if here["tile"] == PIECE:
                            piece_over(ins, *keys)
                        elif keys:
                            mark(ins, *keys)

            def rest_unused(key):
                piece_end.append(done[key])
                here["tile"] = PIECE

            def linear_tokens(key, width, hi, lo, frees, split_key=None, nt=ST):
                per = PIECE * P // width
                o = [open_bank((key, t), frees) for t in range(nt)]
                for k0 in range(0, KD, per):
                    here["piece"] += 1
                    pe.wait_ge(sem("weights_split"), here["piece"] + 1)
                    slot = here["piece"] % SPLIT_SLOTS
                    for t in range(nt):
                        for k in range(k0, k0 + per):
                            if split_key and t == 0:
                                pe.wait_ge(sem("lo"), SPLITS[split_key] + k + 1)
                            c = (k - k0) * width
                            ts = slice(t * P, t * P + P)
                            ins = three(o[t][:, 0:width], hi[:, k, ts], lo[:, k, ts],
                                        whi[:, slot, c:c + width], wlo[:, slot, c:c + width],
                                        k == 0, k == KD - 1)
                        if t == nt - 1:
                            piece_over(ins, *([(key, t)] if k == KD - 1 else []))
                        elif k == KD - 1:
                            mark(ins, (key, t))

            def norm_sum(key, n, width=S):
                o = open_bank(key, "mean_square_read")
                for k in range(n):
                    pe.wait_ge(sem("squares"), len(squares) + 1)
                    ins = pe.matmul(o[:, 0:width], ones, sq[len(squares) % 2][:, 0:width],
                                    start=k == 0, stop=k == n - 1)
                    mark(ins, *([key] if k == n - 1 else []))
                    squares.append(marks[0])

            def mod_products(lo_, hi_):
                for n in range(lo_, hi_):
                    pe.wait_ge(sem("mod_used"), 2 * n + 2)
                    o = open_bank(("mod", n), "mod_read")
                    for m in range(4):
                        ins = pe.matmul(o[:, m:m + 1], accmod[:, m * P:(m + 1) * P], ones[:, 0:1],
                                        start=True, stop=True)
                    mark(ins, ("mod", n))

            pe.wait_ge(sem("tables_in"), 16 * 2)
            for i, (c0, n) in enumerate(((0, REV), (REV, 512), (REV + 512, 512))):
                o = open_bank(("vec", i), "vec_read")
                mark(pe.matmul(o[0:12, 0:n], Yf[0:33, 2048:2060], Yf[0:33, 2060 + c0:2060 + c0 + n],
                               start=True, stop=True), ("vec", i))
            pe.wait_ge(sem("const_in"), 16)
            norm_sum("sum_h1", KD)
            mod_products(0, 4)

            linear_tokens("av", 512, hhi, hlo, "gelu_v", "h1")
            linear("au", range(4), KD, hhi, hlo, 0, "gelu_u")
            linear("gqk", range(4), KD, hhi, hlo, 0, "gla_qk")
            linear("misc", range(4), KD, hhi, hlo, 0, "misc_read")
            pe.wait_ge(sem("misc_read"), 4)
            pe.wait_ge(sem("gate2_in"), 16)
            for a in range(2):
                o = open_bank(("z", a), "z_read")
                mark(pe.matmul(o[:, 0:S], g2[:, a * P:(a + 1) * P], misc[0:16, :], start=True, stop=True), ("z", a))
            o = open_bank("iw", "iw_read")
            for T in range(ST):
                ins = pe.transpose(o[:, T * P:(T + 1) * P], misc[:, T * P:(T + 1) * P], ident)
            mark(ins, "iw")
            linear_tokens("gv", 512, hhi, hlo, "gla_v")
            for g in range(4):
                if g == 0:
                    pe.wait_ge(sem("ln_done"), 4)
                    pe.wait_ge(sem("spatial_masked"), 1)
                o = open_bank(("mix", g), "mix_read")
                for c in range(ST):
                    ins = pe.matmul(o[:, c * P:(c + 1) * P], gv_[:, c, g * P:(g + 1) * P], wsm[:, g, :],
                                    start=True, stop=True)
                mark(ins, ("mix", g))
            linear("gr", range(4), KD, hhi, hlo, 0, "gla_r")

            def merge(n, hi, lo, k0, split_key):
                for half in range(2):
                    m = 4 * half
                    linear(("gate", n), range(m, m + 2), KD, hhi, hlo, 0, "gate_read")
                    if half == 0:
                        pe.wait_ge(sem("lo"), SPLITS[split_key] + 4)
                    linear(("up", n), range(m, m + 4), 4, hi, lo, k0, "up_read")
                    linear(("gate", n), range(m + 2, m + 4), KD, hhi, hlo, 0, "gate_read")

            def attn_of(h, c):
                at_ = ((h % 2) * 8 + 2 * c + h // 2) * P
                return attn[:, at_:at_ + P]

            def level(lv):
                if lv < LEVELS - 1:
                    pe.wait_ge(sem("level_scaled"), 2 * (lv + 1))
                qk_q, qk_k = (qs, ksc) if lv < LEVELS - 1 else (qg, kg)
                for n in range(4):
                    o = open_bank(("level", lv, n), "level_read")
                    r = slice(64 * (n % 2), 64 * (n % 2) + 64)
                    for i in range(4):
                        cs = slice((2 * (n // 2) + i // 2) * P, (2 * (n // 2) + i // 2 + 1) * P)
                        ins = pe.matmul(o[:, i * P:(i + 1) * P], qk_k[r, i % 2, cs], qk_q[r, i % 2, cs],
                                        start=True, stop=True)
                    mark(ins, ("level", lv, n))

            merge(0, ahi, alo, 0, "ya")
            for lv in range(LEVELS):
                level(lv)
            pe.wait_ge(sem("khat"), 1)
            for c in range(ST - 1):
                o = open_bank(("khat", c), "ktok")
                for a in range(2):
                    ins = pe.transpose(o[:, a * P:(a + 1) * P], ksc[:, a, c * P:(c + 1) * P], ident)
                mark(ins, ("khat", c))
            for c in range(ST - 1):
                pe.wait_ge(sem("ktok"), c + 1)
                o = open_bank(("upd", c), "state")
                for h in range(4):
                    r = slice(64 * (h % 2), 64 * (h % 2) + 64)
                    c0 = (h // 2) * P
                    ins = pe.matmul(o[r, c0:c0 + P], ktok[:, c, c0 + 64 * (h % 2):c0 + 64 * (h % 2) + 64],
                                    vg[:, c, h * P:(h + 1) * P], start=True, stop=True)
                mark(ins, ("upd", c))
            pe.wait_ge(sem("state"), 3)
            pe.wait_ge(sem("level_read"), 4 * LEVELS)
            for h in range(4):
                r = slice(64 * (h % 2), 64 * (h % 2) + 64)
                o = open_bank(("og", h), "og_read")
                for c in range(ST):
                    cs = slice(c * P, (c + 1) * P)
                    ins = pe.matmul(o[:, cs], vg[:, c, h * P:(h + 1) * P], attn_of(h, c),
                                    start=True, stop=c == 0)
                    if c:
                        ins = pe.matmul(o[:, cs], state[r, c - 1, (h // 2) * P:(h // 2 + 1) * P],
                                        qs[r, h // 2, cs], start=False, stop=True)
                mark(ins, ("og", h))
            for h in range(4):
                norm_sum(("sum_og", h), 1)

            linear("dq", range(4), KD, hhi, hlo, 0, "dq_read")
            linear("dk", range(4), KD, hhi, hlo, 0, "dk_read")
            linear_tokens("dv", 512, hhi, hlo, "dv_read")
            for T in range(1, ST):
                for h in range(4):
                    r = slice(64 * (h % 2), 64 * (h % 2) + 64)
                    o = open_bank(("idx", T, h), "index_read")
                    mark(pe.matmul(o[:, 0:(T + 1) * P], iq[r, h // 2, T * P:(T + 1) * P], ik[r, 0:(T + 1) * P],
                                   start=True, stop=True), ("idx", T, h))
            for h in range(4):
                norm_sum(("sum_dq", h), 1)
                norm_sum(("sum_dk", h), 1)
            merge(1, ahi, alo, 4, "yb")
            mod_products(4, 12)

            def attention(jobs, name, logits, values, out_key, out_open):
                outs = {}
                for i in range(len(jobs) + TLAG + 1):
                    if i < len(jobs):
                        o = open_bank((name, i), name + "_logits_read")
                        mark(logits(o, jobs[i]), (name, i))
                    if 0 <= i - TLAG < len(jobs):
                        n = i - TLAG
                        kind, T, h, nt, w = jobs[n]
                        pe.wait_ge(sem(name + "_probs"), n + 1)
                        o = open_bank((name + "T", n), name + "_probsT")
                        pb = probs[name][n % len(probs[name])]
                        for j in range(nt):
                            c, wj = (32 * j, NCMP) if kind == "cmp" else (j * P, P)
                            ins = pe.transpose(o[0:wj, j * P:(j + 1) * P], pb[:, c:c + wj], ident)
                        mark(ins, (name + "T", n))
                    if i > TLAG:
                        n = i - TLAG - 1
                        key = out_key(jobs[n])
                        if key not in outs:
                            outs[key] = open_output(key, out_open)
                        pe.wait_ge(sem(name + "_probsT"), n + 1)
                        ins = values(outs[key], jobs[n], probsT[name][n % len(probsT[name])])
                        mark(ins, key, (name + "V", n))

            def dsa_logits(o, job):
                _, T, h, nt, w = job
                return pe.matmul(o[:, 0:w], dq[:, h, T * P:(T + 1) * P], dk[:, h, 0:w], start=True, stop=True)

            def dsa_values(o, job, pt):
                _, T, h, nt, w = job
                for j in range(nt):
                    ins = pe.matmul(o[:, h * P:(h + 1) * P], dv[:, j, h * P:(h + 1) * P], pt[:, j * P:(j + 1) * P],
                                    start=j == 0, stop=j == nt - 1)
                return ins

            pe.wait_ge(sem("rstd_used"), 1 + 4 + 8)
            attention(jobs1, "dsa", dsa_logits, dsa_values, lambda job: ("dsa_out", job[1]), "dsa_out_read")
            merge(2, ahi, alo, 0, "yc")
            linear("wout", range(KD), KD, hhi, hlo, 0, "wout_read", "merged")

            norm_sum("sum_h2", KD)
            o = open_bank("router", "router_read")
            for T in range(ST):
                for k in range(KD):
                    if T == 0:
                        pe.wait_ge(sem("lo"), SPLITS["h2"] + k + 1)
                    for part in (hhi, hlo):
                        ins = pe.matmul(o[:, T * 32:T * 32 + 20], part[:, k, T * P:(T + 1) * P].bitcast(F32),
                                        router[:, k, :], start=k == 0 and part is hhi,
                                        stop=k == KD - 1 and part is hlo)
            mark(ins, "router")
            pe.wait_ge(sem("combined"), 1)
            o = open_bank("combT", "combT_read")
            for T in range(ST):
                ins = pe.transpose(o[0:16, T * P:(T + 1) * P], scol[:, T * 16:(T + 1) * 16], ident)
            mark(ins, "combT")
            pe.wait_ge(sem("combT_read"), 1)
            for g in range(EXPERTS // EPG):
                for e in range(EPG * g, EPG * g + EPG):
                    linear(("eg", e), range(2), KD, hhi, hlo, 0, "silu_read")
                    linear(("eu", e), range(2), KD, hhi, hlo, 0, "eu_read")
                    o = open_bank(("comb", e), "comb_read")
                    mark(pe.matmul(o[:, :], ident[0:16, e:e + 1].to_broadcast([16, P]), combT[:, :],
                                   start=True, stop=True), ("comb", e))
                linear(("ed", g), range(KD), KD, ahi, alo, 0, "ed_read", f"moe{g}")

            norm_sum("sum_n0", KD)
            linear("kcvc", range(2), KD, hhi, hlo, 0, "kcvc_read", "n0")
            linear("kskw", range(2), KD, hhi, hlo, 0, "kskw_read")
            linear_tokens("vsvw", 256, hhi, hlo, "vsvw_read")
            pe.wait_ge(sem("comp_in"), 16 * 3)
            for i in range(2):
                o = open_bank(("pe", i), "pe_read")
                for m in range(PIECE):
                    ins = pe.matmul(o[:, 0:1], cw1[:, i, m * P:(m + 1) * P], pe_s[:, m:m + 1],
                                    start=m == 0, stop=m == PIECE - 1)
                mark(ins, ("pe", i))
            pe.wait_ge(sem("pairs_in"), 16 * 8)
            for i, src in enumerate((kc2, vc2)):
                o = open_bank(("hid", i), "chid")
                for m in range(PIECE):
                    for g in range(2):
                        ins = pe.matmul(o[:, g * 32:g * 32 + NCMP], cw1[:, i, m * P:(m + 1) * P],
                                        src[:, g, 2 * m:2 * m + 16 * (NCMP - 1) + 1:16],
                                        start=m == 0 and g == 0, stop=m == PIECE - 1 and g == 1)
                mark(ins, ("hid", i))
            pe.wait_ge(sem("chid"), 2)
            o = open_bank("kcmp", "kcmp_read")
            for g in range(2):
                ins = pe.matmul(o[64 * g:64 * g + 64, 0:NCMP], cw2[:, 0:64], chid[:, g * 32:g * 32 + NCMP],
                                start=True, stop=True)
            mark(ins, "kcmp")
            o = open_bank("vcmp", "vcmp_read")
            for g in range(2):
                ins = pe.matmul(o[0:NCMP, g * 64:g * 64 + 64], chid[:, 64 + g * 32:64 + g * 32 + NCMP],
                                cw2[:, 64:128], start=True, stop=True)
            mark(ins, "vcmp")
            linear("conv", range(12), KD, hhi, hlo, 0, lambda m: "cc_read" if m % 3 == 0 else "conv_read")
            norm_sum("sum_conv", 4)
            linear("q2", range(4), KD, hhi, hlo, 0, "q2_read")
            linear("gl", range(1), KD, hhi, hlo, 0, "gl_read")
            rest_unused(("gl", 0))
            pe.wait_ge(sem("gl_read"), 1)
            o = open_bank("glT", "glT_read")
            for T in range(ST):
                ins = pe.transpose(o[:, T * P:T * P + 32], glf[0:32, T * P:(T + 1) * P], ident[0:32, 0:32])
            mark(ins, "glT")

            def nsa_logits(o, job):
                kind, T, (j, g), nt, w = job
                r = slice(64 * g, 64 * g + 64)
                if kind == "cmp":
                    for j in range(4):
                        pe.matmul(o[:, 32 * j:32 * j + NCMP], q2[r, j, T * P:(T + 1) * P], kcmp[r, 0:NCMP],
                                  start=True, stop=False)
                        rb = slice(64 * g, 64 * g + NCMP)
                        ins = pe.matmul(o[:, 32 * j:32 * j + NCMP], bct[rb, j, T * P:(T + 1) * P],
                                        ident[rb, 64 * g:64 * g + NCMP], start=False, stop=True)
                    return ins
                key, j0 = (ks2, 0) if kind == "sel" else (kw2, T + 1 - nt)
                return pe.matmul(o[:, 0:w], q2[r, j, T * P:(T + 1) * P], key[r, j0 * P:j0 * P + w],
                                 start=True, stop=True)

            def nsa_values(o, job, pt):
                kind, T, (j, g), nt, w = job
                r = slice(64 * g, 64 * g + 64)
                if kind == "cmp":
                    for j in range(4):
                        ins = pe.matmul(o[r, j * P:(j + 1) * P], vcmp[:, 64 * g:64 * g + 64],
                                        pt[0:NCMP, j * P:(j + 1) * P], start=j == 0, stop=False)
                    return ins
                c0 = (0 if kind == "sel" else P) + 64 * g
                for n in range(nt):
                    ins = pe.matmul(o[r, j * P:(j + 1) * P], vsw[:, T + 1 - nt + n, c0:c0 + 64],
                                    pt[:, n * P:(n + 1) * P], start=False, stop=kind == "sel" and j == 3 and n == nt - 1)
                return ins

            pe.wait_ge(sem("q2_read"), 4)
            pe.wait_ge(sem("bias_cmp_in"), 16 * 8)
            pe.wait_ge(sem("kcmp_read"), 1)
            pe.wait_ge(sem("vcmp_read"), 1)
            attention(jobs2, "nsa", nsa_logits, nsa_values, lambda job: ("nsa_out", job[1]), "nsa_out_read")
            norm_sum("sum_nsa", 4)
            pe.wait_ge(sem("lo"), SPLITS["nsa"] + 4)
            linear("wout2", range(KD), KD, ahi, alo, 0, "wout2_read")
            norm_sum("sum_w2", KD)

            norm_sum("sum_mem", KD, MEM)
            linear("memk", range(2), KD, ahi, alo, 0, "memk_read", "mem", n=MEM)
            linear_tokens("memv", 256, ahi, alo, "memv_read", nt=2)
            norm_sum("sum_n2", KD)
            linear("memq", range(2), KD, hhi, hlo, 0, "memq_read", "n2")

            def mem_logits(o, job):
                _, T, h, nt, w = job
                r = slice(64 * (h % 2), 64 * (h % 2) + 64)
                return pe.matmul(o[:, 0:w], mq[r, h // 2, T * P:(T + 1) * P], mk[r, h // 2, :], start=True, stop=True)

            def mem_values(o, job, pt):
                _, T, h, nt, w = job
                r = slice(64 * (h % 2), 64 * (h % 2) + 64)
                for j in range(nt):
                    ins = pe.matmul(o[r, (h // 2) * P:(h // 2 + 1) * P], mv_[:, j, 64 * h:64 * h + 64],
                                    pt[:, j * P:(j + 1) * P], start=j == 0, stop=j == nt - 1)
                return ins

            pe.wait_ge(sem("memq_read"), 2)
            pe.wait_ge(sem("memk_read"), 2)
            pe.wait_ge(sem("memv_read"), 2)
            attention(jobs3, "mem", mem_logits, mem_values, lambda job: ("mem_out", job[1]), "mem_out_read")
            pe.wait_ge(sem("lo"), SPLITS["mo"] + 2)
            linear("memo", range(KD), 2, ahi, alo, 0, "memo_read")
            norm_sum("sum_mo", KD)

            norm_sum("sum_n4", KD)
            for g, nt in enumerate(FFN_TILES):
                for m in range(0, nt, 2):
                    linear(("fg", g), range(m, m + 2), KD, hhi, hlo, 0, "silu_read", "n4" if g == 0 and m == 0 else None)
                    linear(("fu", g), range(m, m + 2), KD, hhi, hlo, 0, "fu_read")
                linear(("fd", g), range(KD), nt, ahi, alo, 0, "fd_read", f"ffn{g}")
            norm_sum("sum_fd", KD)
            assert here["piece"] + 1 == KIND.count("split") == len(piece_end), (here, KIND.count("split"), len(piece_end))

        def bank(key, w=512):
            return ps[:, bank_of[key], 0:w]

        def finished(eng, key):
            eng.wait_ge(sem("matmuls_done"), done[key])

        PRODUCED = ("h1", "ya", "yb", "merged", "h2", "moe0", "moe1", "moe2", "moe3", "n0", "conv", "nsa", "mem",
                    "n2", "n4")
        SIZE = {k: (list(SPLITS.values()) + [NSPLITS])[n + 1] - SPLITS[k] for n, k in enumerate(SPLITS)}
        UNSPLIT, at = {}, 0
        for k in SPLITS:
            if k in PRODUCED:
                UNSPLIT[k] = at
                at += SIZE[k]

        @block.scalar
        def _(act):
            count = {}

            def run(ins, name, wait=False):
                count[name] = count.get(name, 0) + 1
                ins.then_inc(sem(name), 1)
                if wait:
                    act.wait_ge(sem(name), count[name])

            def squares_of(n, src, ready=None, width=S):
                for k in range(n):
                    i = count.get("squares", 0)
                    if i >= 2:
                        act.wait_ge(sem("matmuls_done"), squares[i - 2])
                    if ready:
                        act.wait_ge(sem(ready[0]), ready[1] + k)
                    run(nc.scalar.activation(sq[i % 2][:, 0:width], src(k), ACT.Square), "squares")

            def rstd_of(key, dim, width=S):
                n = count.get("rstd", 0)
                finished(act, key)
                if n:
                    act.wait_ge(sem("rstd_used"), n)
                run(nc.scalar.activation(rstd[:, 0:width], bank(key, width), ACT.Ln, bias=eps, scale=1.0 / dim),
                    "mean_square_read", True)
                run(nc.scalar.activation(rstd[:, 0:width], rstd[:, 0:width], ACT.Exp, scale=-0.5), "rstd")

            def hi_of(key, i, dst, src=None, bias=None, ready=None, free=None):
                n = SPLITS[key] + i
                assert n == count.get("hi", 0), (key, i, count.get("hi"))
                if ready:
                    act.wait_ge(sem(ready[0]), ready[1])
                else:
                    act.wait_ge(sem("unsplit"), UNSPLIT[key] + i + 1)
                if free:
                    finished(act, free)
                src = tmp[n % 2] if src is None else src
                if bias is None:
                    run(nc.scalar.activation(dst, src, ACT.Copy), "hi")
                else:
                    run(nc.scalar.activation(dst, src, ACT.Identity, bias=bias), "hi")

            def evacuate(key, dst, name, func=ACT.Copy, scale=1.0, bias=0.0, w=512, src=None):
                finished(act, key)
                src = bank(key, w) if src is None else src
                run(nc.scalar.activation(dst, src, func, scale=scale, bias=bias), name)

            act.wait_ge(sem("cols_in"), 16)
            run(nc.scalar.activation(cact[:, :], col("c", 0, 8), ACT.Silu), "c_act")
            for i, (c0, n) in enumerate(((0, REV), (REV, 512), (REV + 512, 512))):
                evacuate(("vec", i), vecs[:, c0:c0 + n], "vec_read", src=ps[0:12, bank_of[("vec", i)], 0:n])
            act.wait_ge(sem("vec_read"), 3)
            act.dma_start(vec_d, vecs).then_inc(sem("vec_out"), 16)
            act.wait_ge(sem("vec_out"), 16)
            act.dma_start(near_d[:, :, 0:REV - 1], bass.AP(tensor=vec_d.tensor, offset=vec_d.offset,
                                                           ap=[[VEC, 12], [0, P], [1, REV - 1]])).then_inc(sem("near_out"), 16)
            act.dma_start(comp_d[:, :, 0:FWD - 32], bass.AP(tensor=vec_d.tensor, offset=vec_d.offset + 4 * VEC + REV,
                                                            ap=[[VEC, 8], [0, NCMP], [1, FWD - 32]])).then_inc(sem("comp_out"), 16)
            act.wait_ge(sem("x_in"), 16)
            squares_of(KD, lambda k: X[:, k, :])
            rstd_of("sum_h1", D)
            for k in range(KD):
                hi_of("h1", k, hhi[:, k, :], bias=mod[:, k:k + 1])
            for T in range(ST):
                evacuate(("av", T), gv_[:, T, :], "gelu_v", ACT.Gelu_apprx_tanh)
            for m in range(4):
                evacuate(("au", m), gu_[:, m, :], "gelu_u", ACT.Gelu_apprx_tanh)
            for m in range(4):
                evacuate(("gqk", m), qg[:, m, :] if m < 2 else kg[:, m - 2, :], "gla_qk", scale=0.125 if m < 2 else 1.0)
            for m in range(4):
                finished(act, ("misc", m))
                evacuate(("misc", m), [iq[:, 0, :], iq[:, 1, :], ik, misc][m], "misc_read")
            act.wait_ge(sem("ln_stats"), 4)
            run(nc.scalar.activation(lnr, mv[:, :, 1], ACT.Ln, bias=eps), "ln_log", True)
            run(nc.scalar.activation(lnr, lnr, ACT.Exp, scale=-0.5), "ln_rstd")
            act.wait_ge(sem("lo"), SPLITS["h1"] + KD)
            for T in range(ST):
                evacuate(("gv", T), vg[:, T, :], "gla_v")
            for g in range(4):
                hi_of("ya", g, ahi[:, g, :])
            for m in range(4):
                evacuate(("gr", m), rg[:, m, :], "gla_r", ACT.Silu)

            def gates(n, ms):
                for m in ms:
                    if m >= 2:
                        if n == 0:
                            act.wait_ge(sem("up_read"), 8 * n + m - 1)
                        elif n == 1:
                            act.wait_ge(sem("merged_in"), m - 1)
                        else:
                            act.wait_ge(sem("unsplit"), UNSPLIT["merged"] + m - 1)
                    evacuate((("gate", n), m), tmp[m % 2], "gate_read", ACT.Sigmoid, bias=col("b_gate", 8 * n + m))

            act.wait_ge(sem("lo"), SPLITS["ya"] + 4)
            act.wait_ge(sem("z_read"), 2)
            run(nc.scalar.activation(edec, ar(8704, 1024), ACT.Abs), "softplus", True)
            run(nc.scalar.activation(edec, edec, ACT.Exp, scale=-1.0), "softplus", True)
            run(nc.scalar.activation(edec, edec, ACT.Ln, bias=ones[:, 0:1]), "softplus")
            gates(0, range(KD))
            for lv in range(LEVELS - 1):
                act.wait_ge(sem("decay_diff"), lv + 1)
                half = 1 << lv
                e = edec.rearrange("p (n b) -> p n b", b=2 * half)
                run(nc.scalar.activation(e[:, :, 0:half], e[:, :, 0:half], ACT.Exp, scale=-1.0), "decay_lower")
                run(nc.scalar.activation(e[:, :, half:2 * half], e[:, :, half:2 * half], ACT.Exp), "decay")
            act.wait_ge(sem("level_scaled"), 2 * (LEVELS - 1))
            run(nc.scalar.activation(ebl, bcum.rearrange("p (n b) -> p n b", b=P)[:, :, P - 1], ACT.Exp), "decay_last")
            run(nc.scalar.activation(edec, bcum, ACT.Exp), "decay")
            act.wait_ge(sem("decay_diff"), LEVELS)
            run(nc.scalar.activation(edec, edec, ACT.Exp), "decay")
            act.wait_ge(sem("khat"), 1)
            for c in range(ST - 1):
                evacuate(("khat", c), ktok[:, c, :], "ktok", w=256)
            for h in range(4):
                evacuate(("og", h), og[:, h, :], "og_read")
            for h in range(4):
                finished(act, ("og", 3))
                act.wait_ge(sem("og_read"), h + 1)
                squares_of(1, lambda k: og[:, h, :])
                rstd_of(("sum_og", h), P)
                hi_of("yb", h, ahi[:, 4 + h, :])
            act.wait_ge(sem("lo"), SPLITS["yb"] + 4)
            act.wait_ge(sem("near_out"), 16)
            for h in range(4):
                src = bass.AP(tensor=near_d.tensor, offset=near_d.offset + h * P * REV + 127, ap=[[REV - 1, P], [1, 256]])
                act.dma_start(bt1[:, h, :], src).then_inc(sem("bias1_in"), 16)
            for m in range(4):
                evacuate(("dq", m), dq[:, m, :], "dq_read")
            for m in range(4):
                evacuate(("dk", m), dk[:, m, :], "dk_read")
            for T in range(ST):
                evacuate(("dv", T), dv[:, T, :], "dv_read")
            for h in range(4):
                act.wait_ge(sem("dq_read"), h + 1)
                act.wait_ge(sem("dk_read"), h + 1)
                squares_of(1, lambda k: dq[:, h, :])
                rstd_of(("sum_dq", h), P)
                squares_of(1, lambda k: dk[:, h, :])
                rstd_of(("sum_dk", h), P)
            gates(1, range(KD))

            def attention(jobs, name, out_of):
                for i in range(len(jobs) + TLAG + 2):
                    if i < len(jobs):
                        kind, T, h, nt, w = jobs[i]
                        st = stat[:, 4 * (i % 4):4 * (i % 4) + 4]
                        pb = probs[name][i % len(probs[name])]
                        if kind != "cmp":
                            act.wait_ge(sem(name + "_max"), sum(job[0] != "cmp" for job in jobs[:i + 1]))
                        if kind == "cmp":
                            act.wait_ge(sem(name + "_logits_read"), i + 1)
                            run(nc.scalar.activation(heads(pb), heads(pb), ACT.Exp), name + "_exp")
                        elif kind == "mem":
                            run(nc.scalar.activation(pb[:, 0:w], bank((name, i), w), ACT.Exp, bias=st[:, 0:1],
                                                     accum_out=st[:, 2:3]), name + "_logits_read")
                        else:
                            run(nc.scalar.activation(pb[:, 0:w], pb[:, 0:w], ACT.Exp, bias=st[:, 0:1],
                                                     accum_out=st[:, 2:3]), name + "_exp")
                    if 0 <= i - TLAG < len(jobs):
                        n = i - TLAG
                        kind, T, h, nt, w = jobs[n]
                        ring = probsT[name]
                        if n >= len(ring):
                            finished(act, (name + "V", n - len(ring)))
                        rows_ = NCMP if kind == "cmp" else P
                        evacuate((name + "T", n), ring[n % len(ring)][0:rows_, 0:nt * P], name + "_probsT",
                                 src=ps[0:rows_, bank_of[(name + "T", n)], 0:nt * P])
                    n = i - TLAG - 2
                    if n >= 0 and (n + 1 == len(jobs) or jobs[n + 1][1] != jobs[n][1]):
                        out_of(jobs[n][1])

            def dsa_out(T):
                n = SPLITS["yc"] + T
                act.wait_ge(sem("lo"), n - 1)
                evacuate(("dsa_out", T), tmp[n % 2], "dsa_out_read")
                t4 = tmp[n % 2].rearrange("p (h t) -> p h t", h=4)
                hi_of("yc", T, ahi[:, 0:4, T * P:(T + 1) * P], src=t4, ready=("dsa_out_read", T + 1))

            attention(jobs1, "dsa", dsa_out)
            finished(act, ("dsa_out", ST - 1))
            act.wait_ge(sem("dsa_probs"), len(jobs1))
            act.dma_start(X[:, :, :], xT).then_inc(sem("x_in"), 16)
            act.wait_ge(sem("lo"), SPLITS["yc"] + 4)
            gates(2, range(KD))
            for k in range(KD):
                hi_of("merged", k, hhi[:, k, :], src=Y[:, k, :], free=(("gate", 2), 7))
            squares_of(KD, lambda k: X[:, k, :], ("wout_read", 1))
            rstd_of("sum_h2", D)
            for k in range(KD):
                hi_of("h2", k, hhi[:, k, :], bias=mod[:, 24 + k:25 + k])
            act.wait_ge(sem("route_max"), 1)
            gl_e = small[:, 344:360]
            run(nc.scalar.activation(gl_e, gl_e, ACT.Exp), "route_exp")
            act.wait_ge(sem("route_diff"), 1)
            run(nc.scalar.activation(stat[:, 8:12], stat[:, 8:12], ACT.Exp), "route_exp")
            for g in range(EXPERTS // EPG):
                for e in range(EPG * g, EPG * g + EPG):
                    for m in range(2):
                        if 2 * e + m >= 2:
                            act.wait_ge(sem("eu_read"), 2 * e + m - 1)
                        evacuate((("eg", e), m), sil[m], "silu_read", ACT.Silu)
                    if e >= 2:
                        act.wait_ge(sem("unsplit"), UNSPLIT["moe0"] + 2 * (e - 1))
                    evacuate(("comb", e), combs[e % 2], "comb_read")
                    for m in range(2):
                        i = 2 * (e % EPG) + m
                        hi_of(f"moe{g}", i, ahi[:, i, :], free=(("ed", g - 1), 7) if g else None)
            squares_of(KD, lambda k: X[:, k, :], ("ffn1_added", 1))
            rstd_of("sum_n0", D)
            for k in range(KD):
                hi_of("n0", k, hhi[:, k, :])
            act.wait_ge(sem("lo"), SPLITS["n0"] + KD)
            act.dma_start(cw1[:, :, :], cw1_d).then_inc(sem("comp_in"), 16)
            act.dma_start(cw2, cw2_d).then_inc(sem("comp_in"), 16)
            act.dma_start(pe_s, peT).then_inc(sem("comp_in"), 16)
            act.wait_ge(sem("comp_out"), 16)
            for h in range(8):
                src = bass.AP(tensor=comp_d.tensor, offset=comp_d.offset + h * NCMP * FWD + 480,
                              ap=[[FWD - 16, NCMP], [1, S]])
                act.dma_start(bct[64 * (h // 4):64 * (h // 4) + NCMP, h % 4, :], src).then_inc(sem("bias_cmp_in"), 16)
            for m in range(2):
                evacuate(("kcvc", m), kcvc[:, m, :], "kcvc_read")
            act.wait_ge(sem("kcvc_read"), 2)
            for i, dst in enumerate((kc2, vc2)):
                for g in range(2):
                    r = slice(64 * g, 64 * g + 64)
                    act.dma_start(dst[0:64, g, :], kcvc[r, i, :]).then_inc(sem("pairs_in"), 16)
                    act.dma_start(dst[64:128, g, 0:S - 1], kcvc[r, i, 1:S]).then_inc(sem("pairs_in"), 16)
            for m in range(2):
                evacuate(("kskw", m), [ks2, kw2][m], "kskw_read")
            for T in range(ST):
                evacuate(("vsvw", T), vsw[:, T, :], "vsvw_read", w=256)
            for i in range(2):
                evacuate(("pe", i), pehid[:, i:i + 1], "pe_read", w=1)
            act.wait_ge(sem("pe_read"), 2)
            for i in range(2):
                finished(act, ("hid", i))
                src = ps[:, bank_of[("hid", i)], 0:64].rearrange("p (g n) -> p g n", g=2)[:, :, 0:NCMP]
                dst = chid[:, 64 * i:64 * i + 64].rearrange("p (g n) -> p g n", g=2)[:, :, 0:NCMP]
                run(nc.scalar.activation(dst, src, ACT.Gelu_apprx_tanh, bias=pehid[:, i:i + 1]), "chid")
            evacuate("kcmp", kcmp[:, 0:NCMP], "kcmp_read", w=NCMP)
            evacuate("vcmp", vcmp, "vcmp_read", src=ps[0:NCMP, bank_of["vcmp"], 0:128])
            for h in range(8):
                src = bass.AP(tensor=near_d.tensor, offset=near_d.offset + (4 + h) * P * REV + 127,
                              ap=[[REV - 1, P], [1, 256]])
                act.dma_start(bt2[:, h, :], src).then_inc(sem("bias2_in"), 16)
            for j in range(4):
                if j:
                    act.wait_ge(sem("conv_read"), 2 * j - 1)
                evacuate(("conv", 3 * j), convc, "cc_read")
            squares_of(4, lambda k: convo[:, k, :], ("conv_out", 1))
            rstd_of("sum_conv", 512)
            for k in range(4):
                hi_of("conv", k, ahi[:, 4 + k, :])
            for m in range(4):
                evacuate(("q2", m), q2[:, m, :], "q2_read", scale=0.125)
            evacuate(("gl", 0), glf, "gl_read", ACT.Sigmoid)

            def nsa_out(T):
                evacuate(("nsa_out", T), onsa[:, :, T * P:(T + 1) * P], "nsa_out_read",
                         src=bank(("nsa_out", T)).rearrange("p (a t) -> p a t", a=4))

            act.wait_ge(sem("lo"), SPLITS["conv"] + 4)
            attention(jobs2, "nsa", nsa_out)
            act.wait_ge(sem("nsa_out_read"), ST)
            squares_of(4, lambda k: onsa[:, k, :])
            rstd_of("sum_nsa", 512)
            for k in range(4):
                hi_of("nsa", k, ahi[:, k, :])
            finished(act, ("nsa_out", ST - 1))
            act.dma_start(memx, memT).then_inc(sem("mem_in"), 16)
            for k in range(KD):
                evacuate(("wout2", k), Y[:, k, :], "wout2_read")
            squares_of(KD, lambda k: Y[:, k, :], ("wout2_read", 1))
            rstd_of("sum_w2", D)
            act.wait_ge(sem("mem_in"), 16)
            squares_of(KD, lambda k: memx[:, k, :], width=MEM)
            rstd_of("sum_mem", D, MEM)
            for k in range(KD):
                hi_of("mem", k, ahi[:, k, 0:MEM], src=tmp[(SPLITS["mem"] + k) % 2][:, 0:MEM])
            for m in range(2):
                evacuate(("memk", m), mk[:, m, :], "memk_read", w=MEM)
            for T in range(2):
                evacuate(("memv", T), mv_[:, T, :], "memv_read", w=MEM)
            squares_of(KD, lambda k: X[:, k, :], ("res1", 1))
            rstd_of("sum_n2", D)
            for k in range(KD):
                hi_of("n2", k, hhi[:, k, :])
            for m in range(2):
                evacuate(("memq", m), mq[:, m, :], "memq_read", scale=0.125)

            def mem_out(T):
                evacuate(("mem_out", T), om[:, :, T * P:(T + 1) * P], "mem_out_read",
                         src=bank(("mem_out", T), 256).rearrange("p (a t) -> p a t", a=2))

            attention(jobs3, "mem", mem_out)
            for k in range(2):
                hi_of("mo", k, ahi[:, k, :], src=om[:, k, :], ready=("mem_out_read", ST))
            for k in range(KD):
                evacuate(("memo", k), Y[:, k, :], "memo_read")
            squares_of(KD, lambda k: Y[:, k, :], ("memo_read", 1))
            rstd_of("sum_mo", D)
            squares_of(KD, lambda k: X[:, k, :], ("res3", 1))
            rstd_of("sum_n4", D)
            for k in range(KD):
                hi_of("n4", k, hhi[:, k, :])
            n = 0
            for g, nt in enumerate(FFN_TILES):
                for m in range(nt):
                    i = 2 * EXPERTS + n
                    if n < 2:
                        act.wait_ge(sem("eu_read"), 2 * EXPERTS)
                    else:
                        act.wait_ge(sem("fu_read"), n - 1)
                    evacuate((("fg", g), m), sil[n % 2], "silu_read", ACT.Silu)
                    hi_of(f"ffn{g}", m, ahi[:, m, :], ready=("fu_read", n + 1),
                          free=(("fd", g - 1), 7) if g else None)
                    n += 1
            squares_of(KD, lambda k: Y[:, k, :], ("fd_read", 17))
            rstd_of("sum_fd", D)

        @block.vector
        def _(dve):
            count = {}

            def run(ins, name="step", wait=True):
                count[name] = count.get(name, 0) + 1
                ins.then_inc(sem("dve_" + name if name == "step" else name), 1)
                if wait:
                    dve.wait_ge(sem("dve_" + name if name == "step" else name), count[name])

            V = nc.vector

            def lo_of(key, i, dst, dst_hi, src=None, bias=None):
                n = SPLITS[key] + i
                assert n == count.get("lo", 0)
                dve.wait_ge(sem("hi"), n + 1)
                src = tmp[n % 2] if src is None else src
                hi32 = dst_hi.bitcast(F32)
                if bias is None:
                    run(V.tensor_tensor(dst, src, hi32, ALU.subtract), "lo")
                else:
                    run(V.scalar_tensor_tensor(dst, src, bias, hi32, op0=ALU.add, op1=ALU.subtract), "lo")

            def split(key, n, produce, hi, lo, k0=0, bias=None, w=S, signal="unsplit"):
                for i in range(n + 1):
                    if i < n:
                        produce(i, tmp[(SPLITS[key] + i) % 2][:, 0:w])
                    if i:
                        j = i - 1
                        lo_of(key, j, lo[:, k0 + j, 0:w], hi[:, k0 + j, 0:w], tmp[(SPLITS[key] + j) % 2][:, 0:w],
                              bias(j) if bias else None)

            def wait_rstd():
                count["norms"] = count.get("norms", 0) + 1
                dve.wait_ge(sem("rstd"), count["norms"])

            def normed(n, src, g, w=S):
                def produce(i, dst):
                    run(V.scalar_tensor_tensor(dst, src(i), g(i), rstd[:, 0:w], op0=ALU.mult, op1=ALU.mult),
                        "unsplit")
                    if i == n - 1:
                        run(V.memset(small[:, 360:361], 0.0), "rstd_used")
                return produce

            def modulation(lo_, hi_, pieces):
                for n in range(lo_, hi_):
                    if n:
                        finished(dve, ("mod", n - 1))
                    for half in range(2):
                        i = pieces[2 * (n - lo_) + half]
                        dve.wait_ge(sem(f"raw_in{i % RAW_SLOTS}"), 16 * (i // RAW_SLOTS + 1))
                        for k in range(4):
                            w_ = raw[:, i % RAW_SLOTS, k * 512:(k + 1) * 512]
                            c_ = cact[:, 4 * half + k:4 * half + k + 1]
                            name = "mod_used" if k == 3 else "step"
                            if half == 0 and k == 0:
                                run(V.tensor_scalar(accmod, w_, c_, None, ALU.mult), name)
                            else:
                                run(V.scalar_tensor_tensor(accmod, w_, c_, accmod, op0=ALU.mult, op1=ALU.add), name)
                    finished(dve, ("mod", n))
                    run(V.tensor_tensor(mod[:, 4 * n:4 * n + 4], bank(("mod", n), 4), col("b_mod", 4 * n, 4), ALU.add),
                        "mod_read")

            first = {}
            for i, (name, n) in enumerate(STREAM):
                first[name] = sum(x for _, x in STREAM[:i])

            dve.wait_ge(sem("c_act"), 1)
            modulation(0, 4, range(first["mod0"], first["mod0"] + 8))
            run(V.scalar_tensor_tensor(gain[:, :], mod[:, 8:16], 1.0, col("g1", 0, 8), op0=ALU.add, op1=ALU.mult))
            wait_rstd()
            split("h1", KD, normed(KD, lambda k: X[:, k, :], lambda k: gain[:, k:k + 1]), hhi, hlo,
                  bias=lambda k: mod[:, k:k + 1])
            dve.wait_ge(sem("ws_in"), 16)
            run(V.tensor_tensor(wsm, wsm, causal.unsqueeze(1).to_broadcast([P, 4, P]), ALU.mult), "spatial_masked")
            for c in range(ST):
                dve.wait_ge(sem("gelu_v"), c + 1)
                run(V.bn_stats(bn[:, c, :], gv_[:, c, :]))
                run(V.bn_aggr(mv[:, c, :], bn[:, c, :]), "ln_stats")
            dve.wait_ge(sem("ln_rstd"), 1)
            dve.wait_ge(sem("rows_in"), 16)
            for c in range(ST):
                v = gv_[:, c, :]
                run(V.tensor_scalar(v, v, mv[:, c, 0:1], lnr[:, c:c + 1], ALU.subtract, ALU.mult))
                run(V.tensor_tensor(v, v, rows[:, ROW["ln_g"]:ROW["ln_g"] + 512], ALU.mult))
                run(V.tensor_tensor(v, v, rows[:, ROW["ln_b"]:ROW["ln_b"] + 512], ALU.add), "ln_done")
            run(V.tensor_copy(scol[:, 0:20], rows[:, ROW["b_router"]:ROW["b_router"] + 20]))
            zb = ar(8704, 1024)
            for a in range(2):
                finished(dve, ("z", a))
                run(V.tensor_scalar(zb[:, a * S:(a + 1) * S], bank(("z", a)), col("gla_b", a), None, ALU.add), "z_read")
            finished(dve, "iw")
            run(V.tensor_copy(iwt, tiles(bank("iw"), 4)[:, :, 16:20]), "iw_read")

            def mixed(g, dst):
                finished(dve, ("mix", g))
                dve.wait_ge(sem("gelu_u"), 4)
                b_ = rows[:, ROW["b_s"] + g * P:ROW["b_s"] + (g + 1) * P].unsqueeze(1).to_broadcast([P, ST, P])
                run(V.tensor_tensor(tiles(dst, ST), tiles(bank(("mix", g)), ST), b_, ALU.add), "mix_read")
                run(V.tensor_tensor(dst, dst, gu_[:, g, :], ALU.mult), "unsplit")

            split("ya", 4, mixed, ahi, alo)
            dve.wait_ge(sem("softplus"), 3)
            run(V.scalar_tensor_tensor(edec, zb, 0.0, edec, op0=ALU.min, op1=ALU.subtract))
            run(V.tensor_scalar(edec, edec, 1.0 / 16.0, None, ALU.mult))
            for n in range(8):
                c_ = slice(n * P, (n + 1) * P)
                run(V.tensor_tensor_scan(bcum[:, c_], ones, edec[:, c_], 0.0, ALU.mult, ALU.add), wait=n == 7)

            def ups(n):
                for m in range(KD):
                    finished(dve, (("up", n), m))
                    dve.wait_ge(sem("gate_read"), 8 * n + m + 1)
                    if n == 0:
                        run(V.tensor_tensor(Y[:, m, :], bank((("up", n), m)), tmp[m % 2], ALU.mult), "up_read")
                    else:
                        run(V.tensor_tensor(tmp[m % 2], bank((("up", n), m)), tmp[m % 2], ALU.mult), "up_read")
                        run(V.tensor_tensor(Y[:, m, :], Y[:, m, :], tmp[m % 2], ALU.add),
                            "merged_in" if n == 1 else "unsplit")

            def difference(lv):
                half = 1 << lv
                b_ = bcum.rearrange("p (n b) -> p n b", b=2 * half)
                ref = b_[:, :, half - 1:half].to_broadcast([P, 1024 // (2 * half), 2 * half])
                run(V.tensor_tensor(edec.rearrange("p (n b) -> p n b", b=2 * half), b_, ref, ALU.subtract), "decay_diff")

            difference(0)
            finished(dve, "iw")
            run(V.memset(attn, 0.0))
            dve.wait_ge(sem("gla_qk"), 4)
            ups(0)

            def flat(t):
                return t.rearrange("p a t -> p (a t)")

            for lv in range(LEVELS):
                if lv < LEVELS - 1:
                    dve.wait_ge(sem("decay"), lv + 1)
                    dve.wait_ge(sem("decay_lower"), lv + 1)
                    if lv:
                        finished(dve, ("level", lv - 1, ST - 1))
                    run(V.tensor_tensor(flat(qs), flat(qg), edec, ALU.mult), "level_scaled", False)
                    run(V.tensor_tensor(flat(ksc), flat(kg), edec, ALU.mult), "level_scaled")
                if lv < LEVELS - 2:
                    difference(lv + 1)
                for n in range(4):
                    finished(dve, ("level", lv, n))
                    mask = levelmask[:, lv, :].bitcast(U32).unsqueeze(1).to_broadcast([P, 4, P])
                    at_ = (n % 2) * 1024 + (n // 2) * 512
                    run(V.copy_predicated(attn[:, at_:at_ + 512].rearrange("p (h t) -> p h t", h=4), mask,
                                          tiles(bank(("level", lv, n)), 4)), "level_read")
            dve.wait_ge(sem("decay"), LEVELS)
            run(V.tensor_tensor(flat(qs), flat(qg), edec, ALU.mult))
            b_ = bcum.rearrange("p (n b) -> p n b", b=P)
            run(V.tensor_tensor(edec.rearrange("p (n b) -> p n b", b=P), b_[:, :, P - 1:P].to_broadcast([P, 8, P]), b_,
                                ALU.subtract), "decay_diff")
            dve.wait_ge(sem("decay"), LEVELS + 1)
            run(V.tensor_tensor(flat(ksc), flat(kg), edec, ALU.mult), "khat")
            dve.wait_ge(sem("decay_last"), 1)
            for c in range(ST - 1):
                finished(dve, ("upd", c))
                if c == 0:
                    run(V.tensor_copy(state[:, 0, :], bank(("upd", 0), 256)), "state")
                else:
                    for a in range(2):
                        a_ = slice(a * P, (a + 1) * P)
                        run(V.scalar_tensor_tensor(state[:, c, a_], state[:, c - 1, a_], ebl[:, 4 * a + c:4 * a + c + 1],
                                                   bank(("upd", c), 256)[:, a_], op0=ALU.mult, op1=ALU.add),
                            "state" if a else "step")

            def gla_out(h, dst):
                wait_rstd()
                run(V.scalar_tensor_tensor(dst, og[:, h, :], col("gla_g"), rstd, op0=ALU.mult, op1=ALU.mult), "rstd_used")
                dve.wait_ge(sem("gla_r"), h + 1)
                run(V.tensor_tensor(dst, dst, rg[:, h, :], ALU.mult), "unsplit")

            split("yb", 4, gla_out, ahi, alo, 4)
            for T in range(1, ST):
                w = (T + 1) * P
                sc = selmask[T]
                for h in range(4):
                    finished(dve, ("idx", T, h))
                    dst = sc if h == 0 else work[:, 0:w]
                    run(V.tensor_scalar(dst, bank(("idx", T, h), w), 0.0, iwt[:, T, h:h + 1], ALU.max, ALU.mult),
                        "index_read")
                    if h:
                        run(V.tensor_tensor(sc, sc, work[:, 0:w], ALU.add))
                run(V.tensor_tensor(sc[:, T * P:w], sc[:, T * P:w], noadm, ALU.add))
            for h in range(4):
                for t, g in ((dq, "qn"), (dk, "kn")):
                    wait_rstd()
                    run(V.scalar_tensor_tensor(t[:, h, :], t[:, h, :], col(g), rstd, op0=ALU.mult, op1=ALU.mult),
                        "rstd_used")
            for T in range(1, ST):
                w = (T + 1) * P
                sc, wk, eq_, cu = selmask[T], work[:, 0:w], eqm[:, 0:w], cum[:, 0:w]
                for r in range(TOPK // 8):
                    run(V.max(max8, wk if r else sc))
                    if r < TOPK // 8 - 1:
                        run(V.match_replace(wk, max8, wk if r else sc, -3.4e38))
                thr = max8[:, 7:8]
                run(V.tensor_scalar(wk, sc, thr, None, ALU.is_gt))
                run(V.tensor_reduce(cnt, wk, AX.X, ALU.add))
                run(V.tensor_scalar(cnt, cnt, -1.0, float(TOPK), ALU.mult, ALU.add))
                run(V.tensor_scalar(eq_, sc, thr, None, ALU.is_equal))
                run(V.tensor_tensor_scan(cu, eq_, eq_, 0.0, ALU.bypass, ALU.add) if False else
                    V.tensor_tensor_scan(cu, ones[:, 0:1].to_broadcast([P, w]), eq_, 0.0, ALU.mult, ALU.add))
                run(V.scalar_tensor_tensor(eq_, cu, cnt, eq_, op0=ALU.is_le, op1=ALU.mult))
                run(V.tensor_tensor(wk, wk, eq_, ALU.add))
                run(V.tensor_scalar(sc, wk, -1.0, -NEG, ALU.add, ALU.mult))
            ups(1)
            modulation(4, 12, range(first["mod1"], first["mod1"] + 16))

            def attention(jobs, name, bias_of, gate_of=None, after=None):
                ring = probs[name]
                exp_done = name + ("_logits_read" if name == "mem" else "_exp")

                def then():
                    dve.wait_ge(sem("dve_step"), count["step"])

                for i in range(len(jobs) + 1):
                    if i < len(jobs):
                        kind, T, h, nt, w = jobs[i]
                        st = stat[:, 4 * (i % 4):4 * (i % 4) + 4]
                        pb = ring[i % len(ring)]
                        if i >= len(ring):
                            finished(dve, (name + "T", i - len(ring)))
                        finished(dve, (name, i))
                        if kind == "cmp":
                            lg = heads(bank((name, i)))
                            m4 = small[:, 4 * h[1]:4 * h[1] + 4]
                            run(V.tensor_reduce(m4, lg, AX.X, ALU.max))
                            run(V.tensor_tensor(heads(pb), lg, m4.unsqueeze(2).to_broadcast([P, 4, NCMP]),
                                                ALU.subtract), name + "_logits_read", False)
                        elif kind == "mem":
                            run(V.tensor_reduce(st[:, 0:1], bank((name, i), w), AX.X, ALU.max, negate=True),
                                name + "_max", False)
                        else:
                            bias_of(jobs[i], bank((name, i)), pb)
                    if i:
                        n = i - 1
                        kind1, T1, h1, nt1, w1 = jobs[n]
                        st1 = stat[:, 4 * (n % 4):4 * (n % 4) + 4]
                        pb1 = ring[n % len(ring)]
                        dve.wait_ge(sem(exp_done), n + 1)
                        if kind1 == "cmp":
                            s4 = small[:, 8 + 4 * h1[1]:12 + 4 * h1[1]]
                            pv = heads(pb1)
                            run(V.tensor_tensor(pv, pv, cmpmask[:, T1, 0:NCMP].unsqueeze(1).to_broadcast([P, 4, NCMP]),
                                                ALU.mult))
                            run(V.tensor_reduce(s4, pv, AX.X, ALU.add))
                            run(V.tensor_scalar(s4, s4, 1e-30, None, ALU.max))
                            run(V.reciprocal(s4, s4))
                            run(V.tensor_tensor(s4, s4, gate_of(jobs[n]), ALU.mult))
                        else:
                            run(V.reciprocal(st1[:, 3:4], st1[:, 2:3]), "step", False)
                    if i < len(jobs) and kind not in ("cmp", "mem"):
                        run(V.tensor_reduce(st[:, 0:1], pb[:, 0:w], AX.X, ALU.max, negate=True), name + "_max", False)
                    if i:
                        then()
                        if kind1 == "cmp":
                            run(V.tensor_tensor(pv, pv, s4.unsqueeze(2).to_broadcast([P, 4, NCMP]), ALU.mult),
                                name + "_probs", False)
                        elif gate_of:
                            run(V.tensor_scalar(pb1[:, 0:w1], pb1[:, 0:w1], st1[:, 3:4], gate_of(jobs[n]),
                                                ALU.mult, ALU.mult), name + "_probs", False)
                        else:
                            run(V.tensor_scalar(pb1[:, 0:w1], pb1[:, 0:w1], st1[:, 3:4], None, ALU.mult),
                                name + "_probs", False)
                    if after:
                        after(i)

            def with_bias(bt, scale, o, pb, nt, sem_name):
                w = nt * P
                if nt == 1:
                    run(V.scalar_tensor_tensor(pb[:, 0:P], o[:, 0:P], scale, bt[:, P:2 * P], op0=ALU.mult, op1=ALU.add),
                        sem_name)
                    return
                if nt > 2:
                    run(V.tensor_scalar(pb[:, 0:w - 2 * P], o[:, 0:w - 2 * P], scale, bt[:, 0:1], ALU.mult, ALU.add),
                        "step", False)
                run(V.scalar_tensor_tensor(pb[:, w - 2 * P:w], o[:, w - 2 * P:w], scale, bt, op0=ALU.mult, op1=ALU.add),
                    sem_name)
                dve.wait_ge(sem("dve_step"), count["step"])

            def dsa_bias(job, o, pb):
                _, T, h, nt, w = job
                with_bias(bt1[:, h, :], P ** -0.5, o, pb, nt, "dsa_logits_read")
                if T:
                    run(V.tensor_tensor(pb[:, 0:w], pb[:, 0:w], selmask[T], ALU.add))

            dve.wait_ge(sem("bias1_in"), 16 * 4)
            def dsa_low(i):
                T = (i - 9) // 4
                if i < 9 or (i - 9) % 4:
                    return
                n = SPLITS["yc"] + T
                t4 = tmp[n % 2].rearrange("p (h t) -> p h t", h=4)
                ts = slice(T * P, (T + 1) * P)
                lo_of("yc", T, alo[:, 0:4, ts], ahi[:, 0:4, ts], t4)

            attention(jobs1, "dsa", dsa_bias, after=dsa_low)
            dsa_low(17)
            dsa_low(21)
            ups(2)
            for k in range(KD):
                lo_of("merged", k, hlo[:, k, :], hhi[:, k, :], Y[:, k, :])
            dve.wait_ge(sem("x_in"), 32)
            for k in range(KD):
                finished(dve, ("wout", k))
                run(V.scalar_tensor_tensor(X[:, k, :], bank(("wout", k)), mod[:, 16 + k:17 + k], X[:, k, :],
                                           op0=ALU.mult, op1=ALU.add), "wout_read")
            run(V.scalar_tensor_tensor(gain[:, :], mod[:, 32:40], 1.0, col("g2", 0, 8), op0=ALU.add, op1=ALU.mult))
            wait_rstd()
            split("h2", KD, normed(KD, lambda k: X[:, k, :], lambda k: gain[:, k:k + 1]), hhi, hlo,
                  bias=lambda k: mod[:, 24 + k:25 + k])

            finished(dve, "router")
            lg = small[:, 368:368 + 80].rearrange("p (a n) -> p a n", a=ST)
            gl_e = small[:, 344:360].rearrange("p (a n) -> p a n", a=ST)
            bias_ = scol[:, 0:20].unsqueeze(1).to_broadcast([P, ST, 20])
            run(V.tensor_tensor(lg, tiles(bank("router", 128), ST)[:, :, 0:20], bias_, ALU.add), "router_read")
            r1 = small[:, 448:452].unsqueeze(2)
            r2 = small[:, 452:456].unsqueeze(2)
            run(V.tensor_reduce(small[:, 448:452], lg[:, :, 0:4], AX.X, ALU.max))
            run(V.tensor_tensor(gl_e, lg[:, :, 0:4], r1.to_broadcast([P, ST, 4]), ALU.subtract), "route_max")
            dve.wait_ge(sem("route_exp"), 1)
            pg = small[:, 456:460]
            run(V.tensor_reduce(pg, gl_e, AX.X, ALU.add))
            run(V.reciprocal(pg, pg))

            def first_of(dst, src, best):
                run(V.tensor_tensor(dst, src, best.to_broadcast([P, ST, 4]), ALU.is_equal))
                seen = small[:, 460:464].unsqueeze(2)
                run(V.tensor_scalar(seen, dst[:, :, 0:1], -1.0, 1.0, ALU.mult, ALU.add))
                for j in range(1, 4):
                    run(V.tensor_tensor(dst[:, :, j:j + 1], dst[:, :, j:j + 1], seen, ALU.mult))
                    run(V.tensor_tensor(seen, seen, dst[:, :, j:j + 1], ALU.subtract))

            goh = small[:, 464:480].rearrange("p (a n) -> p a n", a=ST)
            run(V.tensor_reduce(small[:, 452:456], gl_e, AX.X, ALU.max))
            first_of(goh, gl_e, r2)
            sel = small[:, 480:496].rearrange("p (a n) -> p a n", a=ST)
            t16 = small[:, 496:512].rearrange("p (a n) -> p a n", a=ST)
            for g in range(4):
                dst = sel if g == 0 else t16
                run(V.tensor_tensor(dst, lg[:, :, 4 + 4 * g:8 + 4 * g], goh[:, :, g:g + 1].to_broadcast([P, ST, 4]),
                                    ALU.mult))
                if g:
                    run(V.tensor_tensor(sel, sel, t16, ALU.add))
            e1 = small[:, 512:528].rearrange("p (a n) -> p a n", a=ST)
            e2 = small[:, 528:544].rearrange("p (a n) -> p a n", a=ST)
            run(V.tensor_reduce(small[:, 448:452], sel, AX.X, ALU.max))
            first_of(e1, sel, r1)
            run(V.scalar_tensor_tensor(t16, e1, -3e38, sel, op0=ALU.mult, op1=ALU.add))
            run(V.tensor_reduce(small[:, 452:456], t16, AX.X, ALU.max))
            first_of(e2, t16, r2)
            dif = stat[:, 8:12]
            run(V.tensor_tensor(dif, small[:, 452:456], small[:, 448:452], ALU.subtract), "route_diff")
            dve.wait_ge(sem("route_exp"), 2)
            w1_ = small[:, 448:452]
            run(V.tensor_scalar(w1_, dif, 1.0, None, ALU.add))
            run(V.reciprocal(w1_, w1_))
            run(V.tensor_tensor(w1_, w1_, pg, ALU.mult))
            run(V.tensor_tensor(dif, dif, w1_, ALU.mult))
            run(V.tensor_tensor(e1, e1, w1_.unsqueeze(2).to_broadcast([P, ST, 4]), ALU.mult))
            run(V.tensor_tensor(e2, e2, dif.unsqueeze(2).to_broadcast([P, ST, 4]), ALU.mult))
            run(V.tensor_tensor(e1, e1, e2, ALU.add))
            comb = scol[:, 0:64].rearrange("p (a g e) -> p a g e", a=ST, g=4)
            for g in range(4):
                run(V.tensor_tensor(comb[:, :, g, :], e1, goh[:, :, g:g + 1].to_broadcast([P, ST, 4]), ALU.mult),
                    "combined" if g == 3 else "step")
            finished(dve, "combT")
            run(V.tensor_copy(combT, ps[0:16, bank_of["combT"], :]), "combT_read")

            for g in range(EXPERTS // EPG):
                def gated(i, dst, g=g):
                    e, m = EPG * g + i // 2, i % 2
                    finished(dve, (("eu", e), m))
                    dve.wait_ge(sem("silu_read"), 2 * e + m + 1)
                    run(V.tensor_tensor(dst, bank((("eu", e), m)), sil[m], ALU.mult), "eu_read")
                    dve.wait_ge(sem("comb_read"), e + 1)
                    run(V.tensor_tensor(dst, dst, combs[e % 2], ALU.mult), "unsplit")

                split(f"moe{g}", KD, gated, ahi, alo)
                for k in range(KD):
                    finished(dve, (("ed", g), k))
                    if g == 0:
                        run(V.tensor_copy(Y[:, k, :], bank((("ed", g), k))), "ed_read")
                    else:
                        run(V.tensor_tensor(Y[:, k, :], bank((("ed", g), k)), Y[:, k, :], ALU.add), "ed_read")
                    if g == EXPERTS // EPG - 1:
                        run(V.scalar_tensor_tensor(X[:, k, :], Y[:, k, :], mod[:, 40 + k:41 + k], X[:, k, :],
                                                   op0=ALU.mult, op1=ALU.add), "ffn1_added")
            def norm_gain(n):
                return lambda k: col("norms", 8 * n + k)

            wait_rstd()
            split("n0", KD, normed(KD, lambda k: X[:, k, :], norm_gain(0)), hhi, hlo)
            for j in range(4):
                finished(dve, ("conv", 3 * j + 1))
                dve.wait_ge(sem("cc_read"), j + 1)
                u, y = tmp
                run(V.tensor_tensor(u, bank(("conv", 3 * j + 1)), convc, ALU.mult), "conv_read")
                run(V.tensor_scalar(y, u, col("conv_w", j), None, ALU.mult))
                for t in (1, 2):
                    run(V.scalar_tensor_tensor(y[:, t:S], u[:, 0:S - t], col("conv_w", 4 * t + j), y[:, t:S],
                                               op0=ALU.mult, op1=ALU.add))
                finished(dve, ("conv", 3 * j + 2))
                run(V.tensor_tensor(convo[:, j, :], bank(("conv", 3 * j + 2)), y, ALU.mult), "conv_read")
                run(V.memset(small[:, 361:362], 0.0), "conv_out")
            wait_rstd()
            split("conv", 4, normed(4, lambda k: convo[:, k, :], lambda k: col("gn_conv", k)), ahi, alo, 4)
            finished(dve, "glT")
            run(V.tensor_copy(glt, tiles(bank("glT"), ST)[:, :, 0:24]), "glT_read")

            def nsa_bias(job, o, pb):
                kind, T, (j, g), nt, w = job
                with_bias(bt2[:, 4 * g + j, :], 1.0, o, pb, nt, "nsa_logits_read")
                if kind == "win" and nt == 3:
                    run(V.tensor_tensor(pb[:, 0:P], pb[:, 0:P], band, ALU.add))

            def nsa_gate(job):
                kind, T, (j, g), nt, w = job
                if kind == "cmp":
                    return glt[:, T, 12 * g:12 * g + 10:3]
                n = (4 * g + j) * 3 + ("cmp", "sel", "win").index(kind)
                return glt[:, T, n:n + 1]

            dve.wait_ge(sem("bias2_in"), 16 * 8)
            attention(jobs2, "nsa", nsa_bias, nsa_gate)
            wait_rstd()
            split("nsa", 4, normed(4, lambda k: onsa[:, k, :], lambda k: col("gn_nsa", k)), ahi, alo)

            def residual(n, name):
                wait_rstd()
                for k in range(KD):
                    t = tmp[k % 2]
                    run(V.scalar_tensor_tensor(t, Y[:, k, :], col("norms", 8 * n + k), rstd, op0=ALU.mult, op1=ALU.mult),
                        "rstd_used" if k == KD - 1 else "step")
                    run(V.tensor_tensor(X[:, k, :], X[:, k, :], t, ALU.add), name)

            residual(1, "res1")
            wait_rstd()
            split("mem", KD, normed(KD, lambda k: memx[:, k, :], lambda k: col("mem_norm", k), MEM), ahi, alo, w=MEM)
            wait_rstd()
            split("n2", KD, normed(KD, lambda k: X[:, k, :], norm_gain(2)), hhi, hlo)

            attention(jobs3, "mem", None)
            for k in range(2):
                lo_of("mo", k, alo[:, k, :], ahi[:, k, :], om[:, k, :])
            residual(3, "res3")
            wait_rstd()
            split("n4", KD, normed(KD, lambda k: X[:, k, :], norm_gain(4)), hhi, hlo)
            done_tiles = [0]
            for g, nt in enumerate(FFN_TILES):
                def gated2(i, dst, g=g):
                    finished(dve, (("fu", g), i))
                    n = done_tiles[0]
                    done_tiles[0] += 1
                    dve.wait_ge(sem("silu_read"), 2 * EXPERTS + n + 1)
                    run(V.tensor_tensor(dst, bank((("fu", g), i)), sil[n % 2], ALU.mult), "fu_read")

                split(f"ffn{g}", nt, gated2, ahi, alo)
                for k in range(KD):
                    finished(dve, (("fd", g), k))
                    if g == 0:
                        run(V.tensor_copy(Y[:, k, :], bank((("fd", g), k))), "fd_read")
                    else:
                        run(V.tensor_tensor(Y[:, k, :], bank((("fd", g), k)), Y[:, k, :], ALU.add), "fd_read")
            residual(5, "res5")

        @block.gpsimd
        def _(pool):
            n = 0
            for i, kind in enumerate(KIND):
                if kind == "mod":
                    continue
                r, s = i % RAW_SLOTS, n % SPLIT_SLOTS
                pool.wait_ge(sem(f"raw_in{r}"), 16 * (i // RAW_SLOTS + 1))
                if n >= SPLIT_SLOTS:
                    pool.wait_ge(sem("matmuls_done"), piece_end[n - SPLIT_SLOTS])
                nc.gpsimd.tensor_scalar(whi[:, s, :], raw[:, r, :], 1.0, 1.0, ALU.mult, ALU.mult)\
                    .then_inc(sem("weights_hi"), 1)
                pool.wait_ge(sem("weights_hi"), n + 1)
                nc.gpsimd.tensor_tensor(wlo[:, s, :], raw[:, r, :], whi[:, s, :].bitcast(F32), ALU.subtract)\
                    .then_inc(sem("weights_split"), 1)
                n += 1

        @block.sync
        def _(sp):
            sp.dma_start(cols[:, :], cols_d).then_inc(sem("cols_in"), 16)
            sp.dma_start(Yf[0:33, 2048:2060], relT).then_inc(sem("tables_in"), 16)
            sp.dma_start(Yf[0:33, 2060:2060 + VEC], onehot).then_inc(sem("tables_in"), 16)
            sp.dma_start(con[:, :], const_d).then_inc(sem("const_in"), 16)
            sp.dma_start(X[:, :, :], xT).then_inc(sem("x_in"), 16)
            used = {"mod": 0, "split": 0}
            slot_free = []
            for i, kind in enumerate(KIND):
                if i == RAW_SLOTS:
                    sp.dma_start(rows, rows_d.partition_broadcast(P)).then_inc(sem("rows_in"), 16)
                    sp.dma_start(wsm[:, :, :], wsT).then_inc(sem("ws_in"), 16)
                    sp.dma_start(g2[:, :], gate2_d).then_inc(sem("gate2_in"), 16)
                    sp.dma_start(router[:, :, :], router_d).then_inc(sem("router_in"), 16)
                if i >= RAW_SLOTS:
                    sp.wait_ge(sem(slot_free[i - RAW_SLOTS][0]), slot_free[i - RAW_SLOTS][1])
                used[kind] += 1
                slot_free.append(("mod_used" if kind == "mod" else "weights_split", used[kind]))
                sp.dma_start(raw[:, i % RAW_SLOTS, :], stream[i]).then_inc(sem(f"raw_in{i % RAW_SLOTS}"), 16)
            for k in range(KD):
                sp.wait_ge(sem("res5"), k + 1)
                sp.dma_start(out[:, k, :], X[:, k, :]).then_inc(sem("out_written"), 16)
            sp.wait_ge(sem("out_written"), 16 * KD)
    return done


def columns(a):
    return np.ascontiguousarray(np.asarray(a, np.float32).reshape(-1, P).T)


def moving_tiles(w):
    k, n = w.shape
    return w.reshape(k // P, P, n // P, P).transpose(2, 0, 1, 3).reshape(-1, P, P)


def moving_rows(w):
    k, n = w.shape
    return w.reshape(k // P, P, n // P, P).transpose(0, 2, 1, 3).reshape(-1, P, P)


def constants():
    i = np.arange(P)
    c = np.zeros((P, NCONST), np.float32)

    def put(name, a):
        c[:, CON[name]:CON[name] + a.shape[1]] = a

    put("ident", np.eye(P))
    put("ones", np.ones((P, P)))
    put("causal", i[:, None] <= i[None, :])
    put("noadm", np.where(i[None, :] > i[:, None], NOT_ADMITTED, 0.0))
    put("band", np.where(i[None, :] <= i[:, None], NEG, 0.0))
    s, t = i[:, None], i[None, :]
    lv = [(s >> (n + 1) == t >> (n + 1)) & ((s >> n) & 1 == 0) & ((t >> n) & 1 == 1) for n in range(7)] + [s == t]
    put("levels", np.concatenate(lv, 1))
    n = np.arange(32)
    put("cmpmask", np.concatenate([(T * P + i[:, None] >= 16 * n[None, :] + 31) for T in range(ST)], 1))
    return c


def bucket_onehot():
    dist = np.concatenate([255 - np.arange(REV), np.arange(FWD) - 511])
    n = np.maximum(dist, 0)
    large = 16 + (np.log(np.maximum(n, 16).astype(np.float32) / 16) / np.log(8.0) * 16).astype(np.int32)
    b = np.where(n < 16, n, np.minimum(large, 31))
    rows = np.zeros((NBUCKET + 1, VEC), np.float32)
    ok = dist >= 0
    rows[b[ok], np.nonzero(ok)[0]] = 1.0
    rows[NBUCKET, ~ok] = 1.0
    return rows


def layout(x):
    f = {k: np.asarray(v) for k, v in x.items()}
    z = {k: v[0] for k, v in f.items() if k not in ("rel_bias", "rel_bias_2", "x", "c", "mem_2")}
    sizes = (512, 512, 256, 256, 512, 512, 16, 512, 512, 512, 256, 64, 4, 3072)
    cut = np.cumsum(sizes)[:-1]
    a_u, a_v, gq, gk, gv, gr, ga, dq, dk, dv, iq, ik, iw, gates = np.split(z["w_in"], cut, axis=1)
    misc = np.concatenate([iq, ik, ik, ga, iw, np.zeros((D, P - 20), np.float32)], 1)
    parts = {}
    wm = moving_rows(z["w_mod"][:, :0]) if False else None
    mods = [moving_rows(z["w_mod"][:, n * 512:(n + 1) * 512]) for n in range(12)]
    parts["mod0"], parts["mod1"] = mods[:4], mods[4:]
    parts["av"], parts["au"] = [moving_rows(a_v)], [moving_tiles(a_u)]
    parts["gqk"] = [moving_tiles(gq), moving_tiles(gk)]
    parts["misc"] = [moving_tiles(misc)]
    parts["gv"], parts["gr"] = [moving_rows(gv)], [moving_tiles(gr)]
    parts["dq"], parts["dk"], parts["dv"] = [moving_tiles(dq)], [moving_tiles(dk)], [moving_rows(dv)]
    for n in range(3):
        g, u = moving_tiles(gates[:, n * D:(n + 1) * D]), moving_tiles(z["w_branch"][n])
        parts[f"merge{n}"] = [g[0:16], u[0:16], g[16:32], g[32:48], u[16:32], g[48:64]]
    parts["wout"] = [moving_tiles(z["w_out"])]
    for g in range(4):
        es = range(4 * g, 4 * g + 4)
        p = []
        for e in es:
            p += [moving_tiles(z["w_exp_gate"][e]), moving_tiles(z["w_exp_up"][e])]
        p.append(moving_tiles(z["w_exp_down"][4 * g:4 * g + 4].reshape(1024, D)))
        parts[f"moe{g}"] = p
    q, kc, vc, ks, vs, kw, vw, gl, cb, cc, cx = np.split(
        z["w_in_2"], np.cumsum((512,) + (128,) * 6 + (24, 512, 512))[:], axis=1)
    q = q.reshape(D, 2, 4, 64).transpose(0, 2, 1, 3).reshape(D, 512)
    parts["kcvc"] = [moving_tiles(kc), moving_tiles(vc)]
    parts["kskw"] = [moving_tiles(ks), moving_tiles(kw)]
    parts["vsvw"] = [moving_rows(np.concatenate([vs, vw], 1))]
    parts["conv"] = [moving_tiles(w[:, j * P:(j + 1) * P]) for j in range(4) for w in (cc, cx, cb)]
    parts["q"] = [moving_tiles(q)]
    parts["gl"] = [moving_tiles(np.concatenate([gl, np.zeros((D, 2 * P - 24), np.float32)], 1))]
    wo2 = z["w_out_2"]
    wo2 = np.concatenate([wo2[:512].reshape(2, 4, 64, D).transpose(1, 0, 2, 3).reshape(512, D), wo2[512:]], 0)
    parts["wout2"] = [moving_tiles(wo2)]
    parts["memk"] = [moving_tiles(z["mem_wkv_2"][:, :256])]
    parts["memv"] = [moving_rows(z["mem_wkv_2"][:, 256:])]
    parts["memq"], parts["memo"] = [moving_tiles(z["mem_wq_2"])], [moving_tiles(z["mem_wo_2"])]
    at = 0
    for g, nt in enumerate(FFN_TILES):
        p = []
        for m in range(0, nt, 2):
            c = slice((at + m) * P, (at + m + 2) * P)
            p += [moving_tiles(z["ffn_wg_2"][:, c]), moving_tiles(z["ffn_wu_2"][:, c])]
        p.append(moving_tiles(z["ffn_wd_2"][at * P:(at + nt) * P]))
        parts[f"ffn{g}"] = p
        at += nt
    all_tiles = np.concatenate([t for name, _ in STREAM for t in parts[name]], 0)
    assert all_tiles.shape[0] == NPIECES * PIECE, all_tiles.shape
    stream = all_tiles.reshape(NPIECES, PIECE, P, P).transpose(0, 2, 1, 3).reshape(NPIECES, P, PIECE * P)

    cv = {"c": columns(f["c"][0]), "b_mod": columns(z["b_mod"]), "g1": columns(z["g_norm1"]),
          "g2": columns(z["g_norm2"]), "gla_b": columns(z["gla_b_gate"]), "gla_g": columns(z["gla_norm_g"]),
          "qn": columns(z["dsa_qnorm_g"]), "kn": columns(z["dsa_knorm_g"]), "b_gate": columns(z["b_branch_gate"]),
          "norms": columns(z["norms_2"]), "mem_norm": columns(z["mem_norm_2"]),
          "gn_nsa": columns(z["gn_nsa_2"].reshape(2, 4, 64).transpose(1, 0, 2)), "gn_conv": columns(z["gn_conv_2"]),
          "conv_w": columns(z["conv_w_2"]), "eps": np.full((P, 1), 1e-6, np.float32)}
    cols = np.concatenate([cv[k] for k in COLS], 1)
    rows = np.concatenate([z["gmlp_ln_g"], z["gmlp_ln_b"], z["gmlp_b_s"].reshape(-1), z["b_group"], z["b_router"]])
    rel = np.concatenate([np.concatenate([f["rel_bias"], f["rel_bias_2"].T], 1),
                          np.full((1, 12), NEG, np.float32)], 0)
    router = np.concatenate([z["w_group"], z["w_router"]], 1)
    pe = z["cmp_pe_2"].reshape(-1)
    return {
        "stream": stream,
        "xT": f["x"][0].T.reshape(KD, P, S).transpose(1, 0, 2),
        "memT": f["mem_2"][0].T.reshape(KD, P, MEM).transpose(1, 0, 2),
        "cols": cols, "rows": rows, "const": constants(),
        "wsT": z["gmlp_w_s"].transpose(2, 0, 1), "gate2": z["gla_w_gate2"], "rel": rel, "onehot": bucket_onehot(),
        "router": router.reshape(KD, P, 20).transpose(1, 0, 2),
        "cw1": np.stack([z["cmp_k_w1_2"], z["cmp_v_w1_2"]]).reshape(2, PIECE, P, P).transpose(2, 0, 1, 3)
        .reshape(P, 2, PIECE * P),
        "cw2": np.concatenate([z["cmp_k_w2_2"], z["cmp_v_w2_2"]], 1),
        "pe": columns(pe),
    }


_ORDER = ["stream", "xT", "memT", "cols", "rows", "const", "wsT", "gate2", "rel", "onehot", "router", "cw1", "cw2", "pe"]


def kernel(**inputs):
    import concourse.bacc as _bacc
    from concourse.bass_utils import run_bass_kernel_spmd as _run

    nc = _bacc.Bacc("TRN2", target_bir_lowering=False, num_devices=1)
    arrays, args = {}, []
    laid = layout(inputs)
    for name in _ORDER:
        a = np.ascontiguousarray(laid[name])
        arrays[f"in_{name}"] = a
        args.append(nc.dram_tensor(f"in_{name}", a.shape, mybir.dt.from_np(a.dtype), kind="ExternalInput").ap())
    args.append(nc.dram_tensor("out_0", (P, KD, S), F32, kind="ExternalOutput").ap())
    build(nc, *args)
    r = _run(nc, [arrays], core_ids=[0])
    got = np.asarray(r.results[0]["out_0"])
    return np.ascontiguousarray(got.transpose(1, 0, 2).reshape(1, D, S).transpose(0, 2, 1))
```

```python
from contextlib import ExitStack

import numpy as np
import concourse.bass as bass
from concourse import mybir
from concourse.alu_op_type import AluOpType as ALU

ACT = mybir.ActivationFunctionType
F32 = mybir.dt.float32
F32R = mybir.dt.float32r
U32 = mybir.dt.uint32
AX = mybir.AxisListType

P = 128
S = 512
ST = S // P
D = 1024
KD = D // P
NEG = -1e30
NOT_ADMITTED = -3e38
PIECE = 16
RAW_SLOTS = 3
SPLIT_SLOTS = 2
BANKS = 6
MEM = 256
HID = 2816
NBUCKET = 32
TOPK = 128
NCMP = S // 16 - 1
LEVELS = 8
EXPERTS, EPG = 16, 4

COLS = {"c": 8, "b_mod": 48, "g1": 8, "g2": 8, "gla_b": 2, "gla_g": 1, "qn": 1, "kn": 1,
        "b_gate": 24, "norms": 48, "mem_norm": 8, "gn_nsa": 4, "gn_conv": 4, "conv_w": 12, "eps": 1}
ROWS = {"ln_g": 512, "ln_b": 512, "b_s": 512, "b_router": 20}
CONST = {"ident": 128, "ones": 128, "causal": 128, "noadm": 128, "band": 128, "levels": 8 * 128, "cmpmask": ST * 32}


def offsets(sizes):
    at, out = 0, {}
    for name, n in sizes.items():
        out[name] = at
        at += n
    return out, at


COL, NCOL = offsets(COLS)
ROW, NROW = offsets(ROWS)
CON, NCONST = offsets(CONST)

REV = 384
FWD = 1024
VEC = REV + FWD

STREAM = ([(f"mod{n}", 2) for n in range(4)]
          + [("av", 2), ("au", 2), ("mod4", 2), ("gqk0", 1), ("mod5", 2), ("gqk1", 1), ("mod6", 2), ("misc0", 1),
             ("mod7", 2), ("misc1", 1), ("mod8", 2), ("gv0", 1), ("mod9", 2), ("gv1", 1), ("merge0", 6), ("gr", 2),
             ("dq", 2), ("dk", 2), ("dv", 2), ("mod10", 2), ("merge1a", 2), ("mod11", 2), ("merge1b", 4),
             ("merge2", 6), ("wout", 4)]
          + [(f"moe{g}", 12) for g in range(4)]
          + [("kcvc", 1), ("kskw", 1), ("vsvw", 1), ("conv", 6), ("q", 2), ("gl", 1), ("wout2", 4),
             ("memk", 1), ("memv", 1), ("memq", 1), ("memo", 1), ("ffn0", 12), ("ffn1", 12), ("ffn2", 9)])
NPIECES = sum(n for _, n in STREAM)
KIND = []
for _name, _n in STREAM:
    for _ in range(_n):
        KIND.append("mod" if _name.startswith("mod") else "split")

SPLITS, NSPLITS = offsets({"h1": 8, "ya": 4, "yb": 4, "yc": 4, "merged": 8, "h2": 8,
                           "moe0": 8, "moe1": 8, "moe2": 8, "moe3": 8, "n0": 8, "conv": 4, "nsa": 4,
                           "mem": 8, "n2": 8, "mo": 2, "n4": 8, "ffn0": 8, "ffn1": 8, "ffn2": 6})
FFN_TILES = [8, 8, 6]


def build(nc, stream, xT, memT, cols_d, rows_d, const_d, wsT, gate2_d, relT, onehot, router_d,
          cw1_d, cw2_d, peT, out):
    ctx = ExitStack()
    with ctx:
        sems = {}

        def sem(name):
            if name not in sems:
                sems[name] = ctx.enter_context(nc.semaphore("s_" + name))
            return sems[name]

        def sb(name, shape, dt=F32):
            return ctx.enter_context(nc.sbuf_tensor("b_" + name, shape, dt))

        raw = sb("raw", [P, RAW_SLOTS, PIECE * P])
        whi = sb("whi", [P, SPLIT_SLOTS, PIECE * P], F32R)
        wlo = sb("wlo", [P, SPLIT_SLOTS, PIECE * P], F32R)
        hhi = sb("hhi", [P, KD, S], F32R)
        hlo = sb("hlo", [P, KD, S], F32R)
        ahi = sb("ahi", [P, KD, S], F32R)
        alo = sb("alo", [P, KD, S], F32R)
        X = sb("x", [P, KD, S])
        Y = sb("y", [P, KD, S])
        con = sb("con", [P, NCONST])
        cols = sb("cols", [P, NCOL])
        mod = sb("mod", [P, 48])
        cact = sb("cact", [P, 8])
        gain = sb("gain", [P, 8])
        rhi = sb("rhi", [P, 8, 20], F32R)
        rlo = sb("rlo", [P, 8, 20], F32R)
        small = sb("small", [P, 544])
        ARENA = 11264
        arena = sb("arena", [P, ARENA])
        ps = ctx.enter_context(nc.psum_tensor("ps", [P, BANKS + 2, 512], F32))
        vec_d = nc.dram_tensor("bias_vectors", (12, VEC), F32, kind="Internal").ap()
        near_d = nc.dram_tensor("bias_near", (12, P, REV), F32, kind="Internal").ap()
        comp_d = nc.dram_tensor("bias_compressed", (8, NCMP, FWD), F32, kind="Internal").ap()

        def ar(off, n):
            assert off + n <= ARENA, (off, n)
            return arena[:, off:off + n]

        def tiles(ap, n):
            return ap.rearrange("p (a n) -> p a n", a=n)

        Xf = X[:, :, :].rearrange("p k s -> p (k s)")
        Yf = Y[:, :, :].rearrange("p k s -> p (k s)")
        ident = con[:, CON["ident"]:CON["ident"] + P]
        ones = con[:, CON["ones"]:CON["ones"] + P]
        causal = con[:, CON["causal"]:CON["causal"] + P]
        noadm = con[:, CON["noadm"]:CON["noadm"] + P]
        band = con[:, CON["band"]:CON["band"] + P]
        levelmask = tiles(con[:, CON["levels"]:CON["levels"] + LEVELS * P], LEVELS)
        cmpmask = tiles(con[:, CON["cmpmask"]:CON["cmpmask"] + ST * 32], ST)
        eps = cols[:, COL["eps"]:COL["eps"] + 1]

        def col(name, i=0, n=1):
            return cols[:, COL[name] + i:COL[name] + i + n]

        bn = small[:, 0:24].rearrange("p (c n) -> p c n", c=4)
        mv = small[:, 24:32].rearrange("p (c n) -> p c n", c=4)
        lnr = small[:, 32:36]
        iwt = small[:, 36:52].rearrange("p (a h) -> p a h", a=ST)
        max8 = small[:, 52:60]
        cnt = small[:, 60:61]
        stat = small[:, 64:80]
        kcmp = small[:, 80:112]
        glt = small[:, 112:208].rearrange("p (a h) -> p a h", a=ST)
        pos_hid = small[:, 208:210]
        scol = small[:, 216:344]
        sq = [ar(8704, 512), ar(9216, 512)]
        rstd = ar(9728, 512)
        tmp = [ar(10240, 512), ar(10752, 512)]
        rstds = [rstd, ar(8192, 512)]
        vecs = arena[0:12, 4608:4608 + VEC]
        ebl = stat[:, 0:8]
        gv_ = tiles(ar(0, 2048), ST)
        gu_ = tiles(ar(2048, 2048), ST)
        wsm = tiles(ar(4096, 512), 4)
        rows = Yf[:, 0:NROW]
        g2 = Yf[0:16, 1600:1856]
        router = tiles(Yf[:, 1856:2016], KD)
        qg = tiles(ar(4608, 1024), 2)
        kg = tiles(ar(5632, 1024), 2)
        vg = tiles(Xf[:, 0:2048], ST)
        rg = tiles(Xf[:, 2048:4096], 4)
        bcum = ar(0, 1024)
        edec = ar(1024, 1024)
        qs = tiles(ar(2048, 1024), 2)
        ksc = tiles(ar(3072, 1024), 2)
        ktok = tiles(ar(1024, 1024), ST)
        state = tiles(ar(4096, 768), 3)
        attn = ar(8192, 2048)
        og = tiles(ar(0, 2048), 4)
        iq = tiles(ar(6656, 1024), 2)
        ik = ar(7680, 512)
        misc = ar(8192, 512)
        dq = tiles(ar(2048, 2048), 4)
        dk = tiles(ar(0, 2048), 4)
        dv = tiles(Xf[:, 0:2048], ST)
        selmask = [None, ar(4096, 256), ar(4352, 384), ar(4736, 512)]
        work = ar(5248, 512)
        eqm = Xf[:, 3072:3584]
        cum = Xf[:, 3584:4096]
        bt1 = tiles(Xf[:, 2048:3072], 4)
        p1 = [Xf[:, 3072:3584], Xf[:, 3584:4096], ar(6272, 512), ar(6784, 512)]
        pt1 = [ar(5248, 512), ar(5760, 512), ar(7296, 512)]
        accs = [ar(8192, 512), ar(7168, 512), Xf[:, 3072:3584], Xf[:, 3584:4096]]

        def accmod(n):
            return accs[n % 2] if n < 4 else accs[2 + n % 2]

        gate3 = [ar(8192 + 512 * m, 512) for m in range(4)]
        rout = ar(2560, 512)
        combT = arena[0:16, 0:512]
        sil = [ar(512, 512), ar(1024, 512)]
        combs = [ar(1536, 512), ar(2048, 512)]
        kc2 = ar(0, 1024).rearrange("p (g t) -> p g t", g=2)
        vc2 = ar(1024, 1024).rearrange("p (g t) -> p g t", g=2)
        kcvc = tiles(ar(2048, 1024), 2)
        ks2 = ar(4096, 512)
        kw2 = ar(4608, 512)
        vsw = tiles(ar(5120, 1024), ST)
        cw1 = tiles(ar(6144, 4096), 2)
        chid = ar(3072, 128)
        cw2 = ar(3200, 128)
        pe_s = ar(3328, 16)
        pe_acc = ar(3344, 256)
        vcmp = small[0:NCMP, 216:344]
        convc = ar(8192, 512)
        convo = tiles(ar(6144, 2048), 4)
        glf = ar(8192, 512)
        q2 = tiles(ar(0, 2048), 4)
        bt2 = tiles(ar(2048, 2048), 8)
        bct = Yf[:, 0:2048].rearrange("p (j t) -> p j t", j=4)
        p2 = [ar(8192, 512), ar(10240, 512), ar(10752, 512), rstd]
        pt2 = [ar(8704, 512), ar(9216, 512), Yf[:, 2048:2560]]
        onsa = tiles(ar(6144, 2048), 4)
        memx = tiles(ar(0, 2048), 8)
        mk = tiles(ar(2048, 512), 2)
        mv_ = tiles(ar(2560, 512), 2)
        mq = tiles(ar(3072, 1024), 2)
        om = tiles(ar(4096, 1024), 2)
        p3 = [ar(5120, 512), ar(5632, 512), ar(6144, 512), ar(6656, 512)]
        pt3 = [ar(7168, 512), ar(7680, 512), ar(8192, 512)]
        probs = {"dsa": p1, "nsa": p2, "mem": p3}
        probsT = {"dsa": pt1, "nsa": pt2, "mem": pt3}


        done = {}
        marks = [0]
        opened = []
        bank_of = {}
        handed = {}
        piece_end = []
        squares = []
        square_base = {}
        adds = [0]
        here = {"piece": -1, "tile": PIECE}

        def mark(ins, *keys):
            marks[0] += 1
            ins.then_inc(sem("matmuls_done"), 1)
            for k in keys:
                done[k] = marks[0]

        jobs1 = [("dsa", T, h, T + 1, (T + 1) * P) for T in range(ST) for h in range(4)]
        jobs2 = []
        for T in reversed(range(ST)):
            n = min(T, 2) + 1
            of_tile = [job for j in range(4) for g in range(2)
                       for job in (("win", T, (j, g), n, n * P), ("sel", T, (j, g), T + 1, (T + 1) * P))]
            for g, at in ((0, 3), (1, 6)):
                of_tile.insert(at, ("cmp", T, (0, g), 4, NCMP))
            jobs2 += of_tile
        jobs3 = [("mem", T, h, 2, MEM) for T in range(ST) for h in range(4)]
        last_job = {name: {job[1]: i for i, job in enumerate(jobs)}
                    for name, jobs in (("dsa", jobs1), ("nsa", jobs2), ("mem", jobs3))}
        TLAG = 3

        def heads(ap):
            return tiles(ap[:, 0:P], 4)[:, :, 0:NCMP]

        block = ctx.enter_context(nc.Block())

        @block.tensor
        def _(pe):
            def open_bank(key, frees):
                n = len(opened)
                if n >= BANKS:
                    pe.wait_ge(sem(opened[n - BANKS][0]), opened[n - BANKS][1])
                handed[frees] = handed.get(frees, 0) + 1
                opened.append((frees, handed[frees]))
                bank_of[key] = n % BANKS
                return ps[:, n % BANKS, :]

            def open_output(key, frees):
                n = handed.get(frees, 0)
                if n >= 2:
                    pe.wait_ge(sem(frees), n - 1)
                handed[frees] = n + 1
                bank_of[key] = BANKS + n % 2
                return ps[:, BANKS + n % 2, :]

            def weight_tile():
                if here["tile"] == PIECE:
                    here["tile"] = 0
                    here["piece"] += 1
                    pe.wait_ge(sem("weights_split"), here["piece"] + 1)
                n, slot = here["tile"], here["piece"] % SPLIT_SLOTS
                here["tile"] += 1
                return slot, n * P

            def piece_over(ins, *keys):
                mark(ins, *keys)
                piece_end.append(marks[0])

            def three(o, ahi_, alo_, bhi_, blo_, start, stop):
                pe.matmul(o, ahi_, bhi_, start=start, stop=False)
                pe.matmul(o, ahi_, blo_, start=False, stop=False)
                return pe.matmul(o, alo_, bhi_, start=False, stop=stop)

            def linear(key, outs, nk, hi, lo, k0, frees, split_key=None, n=S, ready=0):
                outs = list(outs)
                if split_key and 2 * nk == PIECE:
                    here["piece"] += 1
                    pe.wait_ge(sem("weights_split"), here["piece"] + 1)
                    slot = here["piece"] % SPLIT_SLOTS
                    o = [open_bank((key, m), frees(m) if callable(frees) else frees) for m in outs[:2]]
                    for k in range(nk):
                        if k >= ready:
                            pe.wait_ge(sem("lo"), SPLITS[split_key] + k - ready + 1)
                        for i in range(2):
                            c = (i * nk + k) * P
                            ins = three(o[i][:, 0:n], whi[:, slot, c:c + P], wlo[:, slot, c:c + P],
                                        hi[:, k0 + k, 0:n], lo[:, k0 + k, 0:n], k == 0, k == nk - 1)
                            if k == nk - 1:
                                (piece_over if i else mark)(ins, (key, outs[i]))
                    outs, split_key = outs[2:], None
                for m in outs:
                    o = open_bank((key, m), frees(m) if callable(frees) else frees)
                    for k in range(nk):
                        if split_key and m == outs[0]:
                            pe.wait_ge(sem("lo"), SPLITS[split_key] + k + 1)
                        slot, c = weight_tile()
                        ins = three(o[:, 0:n], whi[:, slot, c:c + P], wlo[:, slot, c:c + P],
                                    hi[:, k0 + k, 0:n], lo[:, k0 + k, 0:n], k == 0, k == nk - 1)
                        keys = [(key, m)] if k == nk - 1 else []
                        if here["tile"] == PIECE:
                            piece_over(ins, *keys)
                        elif keys:
                            mark(ins, *keys)

            def rest_unused(key):
                piece_end.append(done[key])
                here["tile"] = PIECE

            def linear_tokens(key, width, hi, lo, frees, split_key=None, nt=ST):
                per = PIECE * P // width
                o = [open_bank((key, t), frees) for t in range(nt)]
                for k0 in range(0, KD, per):
                    here["piece"] += 1
                    pe.wait_ge(sem("weights_split"), here["piece"] + 1)
                    slot = here["piece"] % SPLIT_SLOTS
                    for k in range(k0, k0 + per):
                        if split_key:
                            pe.wait_ge(sem("lo"), SPLITS[split_key] + k + 1)
                        for t in range(nt):
                            c = (k - k0) * width
                            ts = slice(t * P, t * P + P)
                            ins = three(o[t][:, 0:width], hi[:, k, ts], lo[:, k, ts],
                                        whi[:, slot, c:c + width], wlo[:, slot, c:c + width],
                                        k == 0, k == KD - 1)
                            if t == nt - 1 and k == k0 + per - 1:
                                piece_over(ins, *([(key, t)] if k == KD - 1 else []))
                            elif k == KD - 1:
                                mark(ins, (key, t))

            def norm_sum(key, n, width=S):
                o = open_bank(key, "mean_square_read")
                for k in range(n):
                    pe.wait_ge(sem("squares"), len(squares) + 1)
                    ins = pe.matmul(o[:, 0:width], ones, sq[len(squares) % 2][:, 0:width],
                                    start=k == 0, stop=k == n - 1)
                    mark(ins, *([key] if k == n - 1 else []))
                    squares.append(marks[0])

            def norm_product(key, n):
                square_base[key] = len(squares), adds[0]
                assert len(squares) % 2 == 0
                adds[0] += n - 1
                pe.wait_ge(sem("squares_added"), adds[0])
                o = open_bank(key, "mean_square_read")
                mark(pe.matmul(o[:, :], ones, sq[0], start=True, stop=True), key)
                squares.extend([marks[0]] * n)

            def mod_products(lo_, hi_):
                for n in range(lo_, hi_):
                    pe.wait_ge(sem("mod_used"), 2 * n + 2)
                    o = open_bank(("mod", n), "mod_read")
                    for m in range(4):
                        ins = pe.matmul(o[:, m:m + 1], accmod(n)[:, m * P:(m + 1) * P], ones[:, 0:1],
                                        start=True, stop=True)
                    mark(ins, ("mod", n))

            pe.wait_ge(sem("const_in"), 16)
            mod_products(0, 2)
            norm_sum("sum_h1", KD)
            mod_products(2, 4)

            linear_tokens("av", 512, hhi, hlo, "gelu_v", "h1")
            pe.wait_ge(sem("tables_in"), 16 * 2)
            for i, (c0, n) in enumerate(((0, REV), (REV, 512), (REV + 512, 512))):
                o = open_bank(("vec", i), "vec_read")
                mark(pe.matmul(o[0:12, 0:n], Yf[0:33, 2048:2060], Yf[0:33, 2060 + c0:2060 + c0 + n],
                               start=True, stop=True), ("vec", i))
            linear("au", range(4), KD, hhi, hlo, 0, "gelu_u")
            linear("gqk", range(2), KD, hhi, hlo, 0, "gla_qk")
            mod_products(4, 5)
            linear("gqk", range(2, 4), KD, hhi, hlo, 0, "gla_qk")
            mod_products(5, 6)
            linear("misc", range(2), KD, hhi, hlo, 0, "misc_read")
            mod_products(6, 7)
            linear("misc", range(2, 4), KD, hhi, hlo, 0, "misc_read")
            mod_products(7, 8)
            pe.wait_ge(sem("misc_read"), 4)
            pe.wait_ge(sem("gate2_in"), 16)
            for a in range(2):
                o = open_bank(("z", a), "z_read")
                mark(pe.matmul(o[:, 0:S], g2[:, a * P:(a + 1) * P], misc[0:16, :], start=True, stop=True), ("z", a))
            o = open_bank("iw", "iw_read")
            for T in range(ST):
                ins = pe.transpose(o[:, T * P:(T + 1) * P], misc[:, T * P:(T + 1) * P], ident)
            mark(ins, "iw")
            linear_tokens("gv", 512, hhi, hlo, "gla_v")
            mod_products(8, 10)
            for g in range(4):
                if g == 0:
                    pe.wait_ge(sem("ln_done"), 4)
                    pe.wait_ge(sem("spatial_masked"), 1)
                o = open_bank(("mix", g), "mix_read")
                for c in range(ST):
                    ins = pe.matmul(o[:, c * P:(c + 1) * P], gv_[:, c, g * P:(g + 1) * P], wsm[:, g, :],
                                    start=True, stop=True)
                mark(ins, ("mix", g))

            def merge(n, hi, lo, k0, split_key, between=()):
                step = dict(between)
                for half in range(2):
                    m = 4 * half
                    for i in (0, 2):
                        linear(("gate", n), range(m + i, m + i + 2), KD, hhi, hlo, 0, "gate_read")
                        if (half, i) in step:
                            step[half, i]()
                    if half == 0:
                        pe.wait_ge(sem("lo"), SPLITS[split_key] + 4)
                    linear(("up", n), range(m, m + 4), 4, hi, lo, k0, "up_read")
                    if (half, 4) in step:
                        step[half, 4]()

            def attn_of(h, c):
                at_ = ((h % 2) * 8 + 2 * c + h // 2) * P
                return attn[:, at_:at_ + P]

            def level(lv):
                if lv < LEVELS - 1:
                    pe.wait_ge(sem("level_scaled"), 2 * (lv + 1))
                qk_q, qk_k = (qs, ksc) if lv < LEVELS - 1 else (qg, kg)
                for n in range(4):
                    o = open_bank(("level", lv, n), "level_read")
                    r = slice(64 * (n % 2), 64 * (n % 2) + 64)
                    for i in range(4):
                        cs = slice((2 * (n // 2) + i // 2) * P, (2 * (n // 2) + i // 2 + 1) * P)
                        ins = pe.matmul(o[:, i * P:(i + 1) * P], qk_k[r, i % 2, cs], qk_q[r, i % 2, cs],
                                        start=True, stop=True)
                    mark(ins, ("level", lv, n))

            merge(0, ahi, alo, 0, "ya", {(0, 2): lambda: level(0), (0, 4): lambda: level(1), (1, 0): lambda: level(2),
                                         (1, 2): lambda: level(3), (1, 4): lambda: level(4)})
            linear("gr", range(2), KD, hhi, hlo, 0, "gla_r")
            level(5)
            linear("gr", range(2, 4), KD, hhi, hlo, 0, "gla_r")
            level(6)
            level(7)
            pe.wait_ge(sem("khat"), 1)
            for c in range(ST - 1):
                o = open_bank(("khat", c), "ktok")
                for a in range(2):
                    ins = pe.transpose(o[:, a * P:(a + 1) * P], ksc[:, a, c * P:(c + 1) * P], ident)
                mark(ins, ("khat", c))
            for c in range(ST - 1):
                pe.wait_ge(sem("ktok"), c + 1)
                o = open_bank(("upd", c), "state")
                for h in range(4):
                    r = slice(64 * (h % 2), 64 * (h % 2) + 64)
                    c0 = (h // 2) * P
                    ins = pe.matmul(o[r, c0:c0 + P], ktok[:, c, c0 + 64 * (h % 2):c0 + 64 * (h % 2) + 64],
                                    vg[:, c, h * P:(h + 1) * P], start=True, stop=True)
                mark(ins, ("upd", c))
            pe.wait_ge(sem("state"), 3)
            pe.wait_ge(sem("level_read"), 4 * LEVELS)
            for h in range(4):
                r = slice(64 * (h % 2), 64 * (h % 2) + 64)
                o = open_bank(("og", h), "og_read")
                for c in range(ST):
                    cs = slice(c * P, (c + 1) * P)
                    ins = pe.matmul(o[:, cs], vg[:, c, h * P:(h + 1) * P], attn_of(h, c),
                                    start=True, stop=c == 0)
                    if c:
                        ins = pe.matmul(o[:, cs], state[r, c - 1, (h // 2) * P:(h // 2 + 1) * P],
                                        qs[r, h // 2, cs], start=False, stop=True)
                mark(ins, ("og", h))

            def index_products(T):
                for h in range(4):
                    r = slice(64 * (h % 2), 64 * (h % 2) + 64)
                    o = open_bank(("idx", T, h), "index_read")
                    mark(pe.matmul(o[:, 0:(T + 1) * P], iq[r, h // 2, T * P:(T + 1) * P], ik[r, 0:(T + 1) * P],
                                   start=True, stop=True), ("idx", T, h))

            for a in range(2):
                linear("dq", range(2 * a, 2 * a + 2), KD, hhi, hlo, 0, "dq_read")
                for h in (2 * a, 2 * a + 1):
                    norm_sum(("sum_og", h), 1)
            index_products(1)
            linear("dk", range(2), KD, hhi, hlo, 0, "dk_read")
            index_products(2)
            linear("dk", range(2, 4), KD, hhi, hlo, 0, "dk_read")
            index_products(3)
            linear_tokens("dv", 512, hhi, hlo, "dv_read")

            def qk_norms(h):
                norm_sum(("sum_dq", h), 1)
                norm_sum(("sum_dk", h), 1)
                if h == 0:
                    mod_products(10, 12)

            merge(1, ahi, alo, 4, "yb", {(0, 0): lambda: qk_norms(0), (0, 2): lambda: qk_norms(1),
                                         (0, 4): lambda: qk_norms(2), (1, 0): lambda: qk_norms(3)})

            def attention(jobs, name, logits, values, out_key, out_open):
                outs = {}
                for i in range(len(jobs) + TLAG + 1):
                    if i < len(jobs):
                        o = open_bank((name, i), name + "_logits_read")
                        mark(logits(o, jobs[i]), (name, i))
                    if 0 <= i - TLAG < len(jobs):
                        n = i - TLAG
                        kind, T, h, nt, w = jobs[n]
                        pe.wait_ge(sem(name + "_probs"), n + 1)
                        o = open_bank((name + "T", n), name + "_probsT")
                        pb = probs[name][n % len(probs[name])]
                        for j in range(nt):
                            c, wj = (32 * j, NCMP) if kind == "cmp" else (j * P, P)
                            ins = pe.transpose(o[0:wj, j * P:(j + 1) * P], pb[:, c:c + wj], ident)
                        mark(ins, (name + "T", n))
                    if i > TLAG:
                        n = i - TLAG - 1
                        key = out_key(jobs[n])
                        if key not in outs:
                            outs[key] = open_output(key, out_open)
                        pe.wait_ge(sem(name + "_probsT"), n + 1)
                        ins = values(outs[key], jobs[n], probsT[name][n % len(probsT[name])])
                        mark(ins, key, (name + "V", n))

            def dsa_logits(o, job):
                _, T, h, nt, w = job
                return pe.matmul(o[:, 0:w], dq[:, h, T * P:(T + 1) * P], dk[:, h, 0:w], start=True, stop=True)

            def dsa_values(o, job, pt):
                _, T, h, nt, w = job
                for j in range(nt):
                    ins = pe.matmul(o[:, h * P:(h + 1) * P], dv[:, j, h * P:(h + 1) * P], pt[:, j * P:(j + 1) * P],
                                    start=j == 0, stop=j == nt - 1)
                return ins

            linear(("gate", 2), range(3), KD, hhi, hlo, 0, "gate_read")
            pe.wait_ge(sem("rstd_used"), 1 + 4 + 8)
            attention(jobs1, "dsa", dsa_logits, dsa_values, lambda job: ("dsa_out", job[1]), "dsa_out_read")
            linear(("gate", 2), range(3, 4), KD, hhi, hlo, 0, "gate_read")
            pe.wait_ge(sem("lo"), SPLITS["yc"] + 4)
            linear(("up", 2), range(4), 4, ahi, alo, 0, "up_read")
            linear(("gate", 2), range(4, KD), KD, hhi, hlo, 0, "gate_read")
            linear(("up", 2), range(4, KD), 4, ahi, alo, 0, "up_read")
            linear("wout", range(KD), KD, hhi, hlo, 0, "wout_read", "merged")

            norm_product("sum_h2", KD)

            def expert_gate(e):
                linear(("eg", e), range(2), KD, hhi, hlo, 0, "silu_read", "h2" if e == 0 else None)

            def expert_up(e):
                linear(("eu", e), range(2), KD, hhi, hlo, 0, "eu_read")

            def expert_weight(e):
                o = open_bank(("comb", e), "comb_read")
                mark(pe.matmul(o[:, :], ident[0:16, e:e + 1].to_broadcast([16, P]), combT[:, :],
                               start=True, stop=True), ("comb", e))

            expert_gate(0)
            o = open_bank("router", "router_T")
            pe.wait_ge(sem("router_split"), 1)
            for k in range(KD):
                ins = three(o[0:20, :], rhi[:, k, :], rlo[:, k, :], hhi[:, k, :], hlo[:, k, :], k == 0, k == KD - 1)
            mark(ins, "router")
            pe.wait_ge(sem("router_T"), 1)
            o = open_bank("routerT", "router_read")
            for T in range(ST):
                ins = pe.transpose(o[:, T * 32:T * 32 + 20], rout[0:20, T * P:(T + 1) * P], ident[0:20, 0:20])
            mark(ins, "routerT")
            expert_up(0)
            expert_gate(1)
            pe.wait_ge(sem("combined"), 1)
            o = open_bank("combT", "combT_read")
            for T in range(ST):
                ins = pe.transpose(o[0:16, T * P:(T + 1) * P], scol[:, T * 16:(T + 1) * 16], ident)
            mark(ins, "combT")
            pe.wait_ge(sem("combT_read"), 1)
            for g in range(EXPERTS // EPG):
                for e in range(EPG * g, EPG * g + EPG):
                    if e > 1:
                        expert_gate(e)
                    if e > 0:
                        expert_up(e)
                    expert_weight(e)
                linear(("ed", g), range(KD), KD, ahi, alo, 0, "ed_read", f"moe{g}")

            norm_product("sum_n0", KD)
            linear("kcvc", range(2), KD, hhi, hlo, 0, "kcvc_read", "n0")
            linear("kskw", range(2), KD, hhi, hlo, 0, "kskw_read")
            linear_tokens("vsvw", 256, hhi, hlo, "vsvw_read")
            pe.wait_ge(sem("comp_in"), 16 * 3)
            pe.wait_ge(sem("pe_sum"), 2)
            for i in range(2):
                o = open_bank(("pe", i), "pe_read")
                mark(pe.matmul(o[:, 0:1], pe_acc[:, i * P:(i + 1) * P], ones[:, 0:1], start=True, stop=True), ("pe", i))
            pe.wait_ge(sem("pairs_in"), 16 * 8)
            for i, src in enumerate((kc2, vc2)):
                o = open_bank(("hid", i), "chid")
                for m in range(PIECE):
                    ins = pe.matmul(tiles(o[:, 0:64], 2)[:, :, 0:NCMP], cw1[:, i, m * P:(m + 1) * P],
                                    src[:, :, 2 * m:2 * m + 16 * (NCMP - 1) + 1:16],
                                    start=m == 0, stop=m == PIECE - 1)
                mark(ins, ("hid", i))
            pe.wait_ge(sem("chid"), 2)
            o = open_bank("kcmp", "kcmp_read")
            for g in range(2):
                ins = pe.matmul(o[64 * g:64 * g + 64, 0:NCMP], cw2[:, 0:64], chid[:, g * 32:g * 32 + NCMP],
                                start=True, stop=True)
            mark(ins, "kcmp")
            o = open_bank("vcmp", "vcmp_read")
            for g in range(2):
                ins = pe.matmul(o[0:NCMP, g * 64:g * 64 + 64], chid[:, 64 + g * 32:64 + g * 32 + NCMP],
                                cw2[:, 64:128], start=True, stop=True)
            mark(ins, "vcmp")
            linear("conv", range(12), KD, hhi, hlo, 0, lambda m: "cc_read" if m % 3 == 0 else "conv_read")
            norm_sum("sum_conv", 4)
            linear("q2", range(4), KD, hhi, hlo, 0, "q2_read")
            linear("gl", range(1), KD, hhi, hlo, 0, "gl_read")
            rest_unused(("gl", 0))
            pe.wait_ge(sem("gl_read"), 1)
            o = open_bank("glT", "glT_read")
            for T in range(ST):
                ins = pe.transpose(o[:, T * P:T * P + 32], glf[0:32, T * P:(T + 1) * P], ident[0:32, 0:32])
            mark(ins, "glT")

            def nsa_logits(o, job):
                kind, T, (j, g), nt, w = job
                r = slice(64 * g, 64 * g + 64)
                if kind == "cmp":
                    for j in range(4):
                        pe.matmul(o[:, 32 * j:32 * j + NCMP], q2[r, j, T * P:(T + 1) * P], kcmp[r, 0:NCMP],
                                  start=True, stop=False)
                        rb = slice(64 * g, 64 * g + NCMP)
                        ins = pe.matmul(o[:, 32 * j:32 * j + NCMP], bct[rb, j, T * P:(T + 1) * P],
                                        ident[rb, 64 * g:64 * g + NCMP], start=False, stop=True)
                    return ins
                key, j0 = (ks2, 0) if kind == "sel" else (kw2, T + 1 - nt)
                return pe.matmul(o[:, 0:w], q2[r, j, T * P:(T + 1) * P], key[r, j0 * P:j0 * P + w],
                                 start=True, stop=True)

            def nsa_values(o, job, pt):
                kind, T, (j, g), nt, w = job
                r = slice(64 * g, 64 * g + 64)
                if kind == "cmp":
                    for j in range(4):
                        ins = pe.matmul(o[r, j * P:(j + 1) * P], vcmp[:, 64 * g:64 * g + 64],
                                        pt[0:NCMP, j * P:(j + 1) * P], start=False, stop=False)
                    return ins
                c0 = (0 if kind == "sel" else P) + 64 * g
                first = kind == "win" and j == 0
                for n in range(nt):
                    ins = pe.matmul(o[r, j * P:(j + 1) * P], vsw[:, T + 1 - nt + n, c0:c0 + 64],
                                    pt[:, n * P:(n + 1) * P], start=first and n == 0, stop=kind == "sel" and j == 3 and n == nt - 1)
                return ins

            pe.wait_ge(sem("q2_read"), 4)
            pe.wait_ge(sem("bias_cmp_in"), 16 * 8)
            pe.wait_ge(sem("kcmp_read"), 1)
            pe.wait_ge(sem("vcmp_read"), 1)
            attention(jobs2, "nsa", nsa_logits, nsa_values, lambda job: ("nsa_out", job[1]), "nsa_out_read")
            norm_sum("sum_nsa", 4)
            linear("wout2", range(2), KD, ahi, alo, 0, "wout2_read", "nsa", ready=4)
            norm_sum("sum_mem", KD, MEM)
            linear("wout2", range(2, KD), KD, ahi, alo, 0, "wout2_read")

            linear("memk", range(2), KD, hhi, hlo, 0, "memk_read", "mem", n=MEM)
            norm_product("sum_w2", KD)
            linear_tokens("memv", 256, hhi, hlo, "memv_read", nt=2)
            norm_sum("sum_n2", KD)
            linear("memq", range(2), KD, hhi, hlo, 0, "memq_read", "n2")

            def mem_logits(o, job):
                _, T, h, nt, w = job
                r = slice(64 * (h % 2), 64 * (h % 2) + 64)
                return pe.matmul(o[:, 0:w], mq[r, h // 2, T * P:(T + 1) * P], mk[r, h // 2, :], start=True, stop=True)

            def mem_values(o, job, pt):
                _, T, h, nt, w = job
                r = slice(64 * (h % 2), 64 * (h % 2) + 64)
                for j in range(nt):
                    ins = pe.matmul(o[r, (h // 2) * P:(h // 2 + 1) * P], mv_[:, j, 64 * h:64 * h + 64],
                                    pt[:, j * P:(j + 1) * P], start=j == 0, stop=j == nt - 1)
                return ins

            pe.wait_ge(sem("memq_read"), 2)
            pe.wait_ge(sem("memk_read"), 2)
            pe.wait_ge(sem("memv_read"), 2)
            attention(jobs3, "mem", mem_logits, mem_values, lambda job: ("mem_out", job[1]), "mem_out_read")
            pe.wait_ge(sem("lo"), SPLITS["mo"] + 2)
            linear("memo", range(KD), 2, ahi, alo, 0, "memo_read")
            norm_product("sum_mo", KD)

            norm_sum("sum_n4", KD)
            for g, nt in enumerate(FFN_TILES):
                for m in range(0, nt, 2):
                    linear(("fg", g), range(m, m + 2), KD, hhi, hlo, 0, "silu_read", "n4" if g == 0 and m == 0 else None)
                    linear(("fu", g), range(m, m + 2), KD, hhi, hlo, 0, "fu_read")
                linear(("fd", g), range(KD), nt, ahi, alo, 0, "fd_read", f"ffn{g}")
            norm_product("sum_fd", KD)
            assert here["piece"] + 1 == KIND.count("split") == len(piece_end), (here, KIND.count("split"), len(piece_end))

        def bank(key, w=512):
            return ps[:, bank_of[key], 0:w]

        def finished(eng, key):
            eng.wait_ge(sem("matmuls_done"), done[key])

        PRODUCED = ("h1", "ya", "yb", "merged", "h2", "moe0", "moe1", "moe2", "moe3", "n0", "conv", "nsa", "mem",
                    "n2", "n4")
        SIZE = {k: (list(SPLITS.values()) + [NSPLITS])[n + 1] - SPLITS[k] for n, k in enumerate(SPLITS)}
        UNSPLIT, at = {}, 0
        for k in SPLITS:
            if k in PRODUCED:
                UNSPLIT[k] = at
                at += SIZE[k]

        @block.scalar
        def _(act):
            count = {}

            slots = []
            table = [None]

            def log_exp_table():
                if table[0] is None:
                    nc.scalar.preload_act_table_set("natural_log_exp_and_others")
                    table[0] = "log_exp"


            def run(ins, name, wait=False):
                count[name] = count.get(name, 0) + 1
                ins.then_inc(sem(name), 1)
                if wait:
                    act.wait_ge(sem(name), count[name])

            def squares_of(n, src, ready=None, width=S):
                log_exp_table()
                for k in range(n):
                    i = count.get("squares", 0)
                    if i >= 2:
                        act.wait_ge(sem("matmuls_done"), squares[i - 2])
                    if ready:
                        act.wait_ge(sem(ready[0]), ready[1] + k)
                    run(nc.scalar.activation(sq[i % 2][:, 0:width], src(k), ACT.Square), "squares")

            def square_for(key, k, src):
                base, added = square_base[key]
                log_exp_table()
                assert count.get("squares", 0) == base + k
                if k < 2:
                    act.wait_ge(sem("matmuls_done"), squares[base + k - 2])
                else:
                    act.wait_ge(sem("squares_added"), added + k - 1)
                run(nc.scalar.activation(sq[min(k, 1)], src, ACT.Square), "squares")

            def rstd_of(key, dim, width=S, slot=0):
                n = count.get("rstd", 0)
                log_exp_table()
                finished(act, key)
                last_use = n if slots[-1:] == [slot] else n - 1
                slots.append(slot)
                if last_use > 0:
                    act.wait_ge(sem("rstd_used"), last_use)
                dst = rstds[slot][:, 0:width]
                run(nc.scalar.activation(dst, bank(key, width), ACT.Ln, bias=eps, scale=1.0 / dim),
                    "mean_square_read", True)
                run(nc.scalar.activation(dst, dst, ACT.Exp, scale=-0.5), "rstd")

            def hi_of(key, i, dst, src=None, bias=None, ready=None, free=None):
                n = SPLITS[key] + i
                assert n == count.get("hi", 0), (key, i, count.get("hi"))
                if ready:
                    act.wait_ge(sem(ready[0]), ready[1])
                else:
                    act.wait_ge(sem("unsplit"), UNSPLIT[key] + i + 1)
                if free:
                    finished(act, free)
                src = tmp[n % 2] if src is None else src
                if bias is None:
                    run(nc.scalar.activation(dst, src, ACT.Copy), "hi")
                else:
                    run(nc.scalar.activation(dst, src, ACT.Identity, bias=bias), "hi")

            def evacuate(key, dst, name, func=ACT.Copy, scale=1.0, bias=0.0, w=512, src=None):
                finished(act, key)
                src = bank(key, w) if src is None else src
                if func != ACT.Copy:
                    table[0] = None
                run(nc.scalar.activation(dst, src, func, scale=scale, bias=bias), name)

            act.wait_ge(sem("cols_in"), 16)
            run(nc.scalar.activation(cact[:, :], col("c", 0, 8), ACT.Silu), "c_act")
            act.wait_ge(sem("x_in"), 16)
            squares_of(KD, lambda k: X[:, k, :])
            rstd_of("sum_h1", D)
            for k in range(KD):
                hi_of("h1", k, hhi[:, k, :], bias=mod[:, k:k + 1])
            for T in range(ST):
                evacuate(("av", T), gv_[:, T, :], "gelu_v", ACT.Gelu_apprx_tanh)
            for i, (c0, n) in enumerate(((0, REV), (REV, 512), (REV + 512, 512))):
                evacuate(("vec", i), vecs[:, c0:c0 + n], "vec_read", src=ps[0:12, bank_of[("vec", i)], 0:n])
            act.wait_ge(sem("vec_read"), 3)
            act.dma_start(vec_d, vecs).then_inc(sem("vec_out"), 16)
            act.wait_ge(sem("vec_out"), 16)
            for m in range(4):
                evacuate(("au", m), gu_[:, m, :], "gelu_u", ACT.Gelu_apprx_tanh)
            log_exp_table()
            act.wait_ge(sem("ln_stats"), 4)
            run(nc.scalar.activation(lnr, mv[:, :, 1], ACT.Ln, bias=eps), "ln_log", True)
            run(nc.scalar.activation(lnr, lnr, ACT.Exp, scale=-0.5), "ln_rstd")
            for m in range(4):
                evacuate(("gqk", m), qg[:, m, :] if m < 2 else kg[:, m - 2, :], "gla_qk", scale=0.125 if m < 2 else 1.0)
            for m in range(4):
                finished(act, ("misc", m))
                evacuate(("misc", m), [iq[:, 0, :], iq[:, 1, :], ik, misc][m], "misc_read")
            act.wait_ge(sem("lo"), SPLITS["h1"] + KD)
            for T in range(ST):
                evacuate(("gv", T), vg[:, T, :], "gla_v")
            for g in range(4):
                hi_of("ya", g, ahi[:, g, :])

            def gates(n, ms):
                for m in ms:
                    if n == 0:
                        evacuate((("gate", n), m), Y[:, m, :], "gate_read", ACT.Sigmoid, bias=col("b_gate", m))
                        continue
                    if n == 2:
                        if m >= 4:
                            act.wait_ge(sem("up_read"), 2 * KD + m - 3)
                        evacuate((("gate", n), m), gate3[m % 4], "gate_read", ACT.Sigmoid, bias=col("b_gate", 16 + m))
                        continue
                    if m >= 2:
                        act.wait_ge(sem("merged_in"), m - 1)
                    evacuate((("gate", n), m), tmp[m % 2], "gate_read", ACT.Sigmoid, bias=col("b_gate", 8 * n + m))

            act.dma_start(near_d[:, :, 0:REV - 1], bass.AP(tensor=vec_d.tensor, offset=vec_d.offset,
                                                           ap=[[VEC, 12], [0, P], [1, REV - 1]])).then_inc(sem("near_out"), 16)
            act.dma_start(comp_d[:, :, 0:FWD - 32], bass.AP(tensor=vec_d.tensor, offset=vec_d.offset + 4 * VEC + REV,
                                                            ap=[[VEC, 8], [0, NCMP], [1, FWD - 32]])).then_inc(sem("comp_out"), 16)
            log_exp_table()
            act.wait_ge(sem("lo"), SPLITS["ya"] + 4)
            act.wait_ge(sem("z_read"), 2)
            run(nc.scalar.activation(edec, ar(8704, 1024), ACT.Abs), "softplus", True)
            run(nc.scalar.activation(edec, edec, ACT.Exp, scale=-1.0), "softplus", True)
            run(nc.scalar.activation(edec, edec, ACT.Ln, bias=ones[:, 0:1]), "softplus")

            def decay(lv):
                log_exp_table()
                act.wait_ge(sem("decay_diff"), lv + 1)
                half = 1 << lv
                e = edec.rearrange("p (n b) -> p n b", b=2 * half)
                run(nc.scalar.activation(e[:, :, 0:half], e[:, :, 0:half], ACT.Exp, scale=-1.0), "decay_lower")
                run(nc.scalar.activation(e[:, :, half:2 * half], e[:, :, half:2 * half], ACT.Exp), "decay")

            gates(0, range(2))
            decay(0)
            gates(0, range(2, 4))
            decay(1)
            decay(2)
            gates(0, range(4, 6))
            decay(3)
            gates(0, range(6, 8))
            decay(4)
            decay(5)
            for m in range(2):
                evacuate(("gr", m), rg[:, m, :], "gla_r", ACT.Silu)
            decay(6)
            for m in range(2, 4):
                evacuate(("gr", m), rg[:, m, :], "gla_r", ACT.Silu)
            act.wait_ge(sem("level_scaled"), 2 * (LEVELS - 1))
            run(nc.scalar.activation(ebl, bcum.rearrange("p (n b) -> p n b", b=P)[:, :, P - 1], ACT.Exp), "decay_last")
            run(nc.scalar.activation(edec, bcum, ACT.Exp), "decay")
            act.wait_ge(sem("decay_diff"), LEVELS)
            run(nc.scalar.activation(edec, edec, ACT.Exp), "decay")
            act.wait_ge(sem("khat"), 1)
            for c in range(ST - 1):
                evacuate(("khat", c), ktok[:, c, :], "ktok", w=256)
            for h in range(4):
                evacuate(("og", h), og[:, h, :], "og_read")
            finished(act, ("og", 3))
            for a in range(2):
                act.wait_ge(sem("og_read"), 4)
                squares_of(2, lambda k: og[:, 2 * a + k, :])
                for m in (2 * a, 2 * a + 1):
                    evacuate(("dq", m), dq[:, m, :], "dq_read")
                for h in (2 * a, 2 * a + 1):
                    rstd_of(("sum_og", h), P, slot=h % 2)
                    hi_of("yb", h, ahi[:, 4 + h, :])
            act.wait_ge(sem("lo"), SPLITS["yb"] + 4)
            act.wait_ge(sem("near_out"), 16)
            for h in range(4):
                src = bass.AP(tensor=near_d.tensor, offset=near_d.offset + h * P * REV + 127, ap=[[REV - 1, P], [1, 256]])
                act.dma_start(bt1[:, h, :], src).then_inc(sem("bias1_in"), 16)
            for m in range(4):
                evacuate(("dk", m), dk[:, m, :], "dk_read")
            for T in range(ST):
                evacuate(("dv", T), dv[:, T, :], "dv_read")
            act.wait_ge(sem("dq_read"), 4)
            act.wait_ge(sem("dk_read"), 4)

            def qk_squares(h):
                squares_of(1, lambda k: dq[:, h, :])
                squares_of(1, lambda k: dk[:, h, :])

            def qk_rstds(h):
                rstd_of(("sum_dq", h), P, slot=0)
                rstd_of(("sum_dk", h), P, slot=1)

            qk_squares(0)
            gates(1, range(2))
            qk_rstds(0)
            qk_squares(1)
            qk_rstds(1)
            qk_squares(2)
            gates(1, range(2, 4))
            qk_rstds(2)
            qk_squares(3)
            gates(1, range(4, 6))
            qk_rstds(3)
            gates(1, range(6, 8))

            def attention(jobs, name, out_of):
                log_exp_table()
                for i in range(len(jobs) + TLAG + 2):
                    if 0 <= i - TLAG < len(jobs):
                        n = i - TLAG
                        kind, T, h, nt, w = jobs[n]
                        ring = probsT[name]
                        if n >= len(ring):
                            finished(act, (name + "V", n - len(ring)))
                        rows_ = NCMP if kind == "cmp" else P
                        evacuate((name + "T", n), ring[n % len(ring)][0:rows_, 0:nt * P], name + "_probsT",
                                 src=ps[0:rows_, bank_of[(name + "T", n)], 0:nt * P])
                    if i < len(jobs):
                        kind, T, h, nt, w = jobs[i]
                        st = stat[:, 4 * (i % 4):4 * (i % 4) + 4]
                        pb = probs[name][i % len(probs[name])]
                        if kind != "cmp":
                            act.wait_ge(sem(name + "_max"), sum(job[0] != "cmp" for job in jobs[:i + 1]))
                        if kind == "cmp":
                            act.wait_ge(sem(name + "_logits_read"), i + 1)
                            run(nc.scalar.activation(heads(pb), heads(pb), ACT.Exp), name + "_exp")
                        elif kind == "mem":
                            run(nc.scalar.activation(pb[:, 0:w], bank((name, i), w), ACT.Exp, bias=st[:, 0:1],
                                                     accum_out=st[:, 2:3]), name + "_logits_read")
                        else:
                            run(nc.scalar.activation(pb[:, 0:w], pb[:, 0:w], ACT.Exp, bias=st[:, 0:1],
                                                     accum_out=st[:, 2:3]), name + "_exp")
                    n = i - TLAG - 2
                    if n >= 0 and last_job[name][jobs[n][1]] == n:
                        out_of(jobs[n][1])

            def dsa_out(T):
                n = SPLITS["yc"] + T
                act.wait_ge(sem("lo"), n - 1)
                evacuate(("dsa_out", T), tmp[n % 2], "dsa_out_read")
                t4 = tmp[n % 2].rearrange("p (h t) -> p h t", h=4)
                hi_of("yc", T, ahi[:, 0:4, T * P:(T + 1) * P], src=t4, ready=("dsa_out_read", T + 1))

            gates(2, range(3))
            attention(jobs1, "dsa", dsa_out)
            finished(act, ("dsa_out", ST - 1))
            act.wait_ge(sem("dsa_probs"), len(jobs1))
            act.dma_start(X[:, :, :], xT).then_inc(sem("x_in"), 16)
            act.wait_ge(sem("lo"), SPLITS["yc"] + 4)
            gates(2, range(3, KD))
            for k in range(KD):
                hi_of("merged", k, hhi[:, k, :], src=Y[:, k, :], free=(("gate", 2), 7))
            for k in range(KD):
                act.wait_ge(sem("wout_read"), k + 1)
                square_for("sum_h2", k, X[:, k, :])
            rstd_of("sum_h2", D)
            for k in range(KD):
                hi_of("h2", k, hhi[:, k, :], bias=mod[:, 24 + k:25 + k])
            evacuate("router", rout[0:20, :], "router_T", src=ps[0:20, bank_of["router"], :])
            act.wait_ge(sem("route_max"), 1)
            gl_e = small[:, 344:360]
            run(nc.scalar.activation(gl_e, gl_e, ACT.Exp), "route_exp")
            act.wait_ge(sem("route_diff"), 1)
            run(nc.scalar.activation(stat[:, 8:12], stat[:, 8:12], ACT.Exp), "route_exp")
            for g in range(EXPERTS // EPG):
                for e in range(EPG * g, EPG * g + EPG):
                    for m in range(2):
                        if 2 * e + m >= 2:
                            act.wait_ge(sem("eu_read"), 2 * e + m - 1)
                        evacuate((("eg", e), m), sil[m], "silu_read", ACT.Silu)
                    if e >= 2:
                        act.wait_ge(sem("unsplit"), UNSPLIT["moe0"] + 2 * (e - 1))
                    evacuate(("comb", e), combs[e % 2], "comb_read")
                    for m in range(2):
                        i = 2 * (e % EPG) + m
                        hi_of(f"moe{g}", i, ahi[:, i, :], free=(("ed", g - 1), 7) if g else None)
            for k in range(KD):
                act.wait_ge(sem("ffn1_added"), k + 1)
                square_for("sum_n0", k, X[:, k, :])
            rstd_of("sum_n0", D)
            for k in range(KD):
                hi_of("n0", k, hhi[:, k, :])
            act.wait_ge(sem("lo"), SPLITS["n0"] + KD)
            act.dma_start(cw1[:, :, :], cw1_d).then_inc(sem("comp_in"), 16)
            act.dma_start(cw2, cw2_d).then_inc(sem("comp_in"), 16)
            act.dma_start(pe_s, peT).then_inc(sem("comp_in"), 16)
            act.wait_ge(sem("comp_out"), 16)
            for h in range(8):
                src = bass.AP(tensor=comp_d.tensor, offset=comp_d.offset + h * NCMP * FWD + 480,
                              ap=[[FWD - 16, NCMP], [1, S]])
                act.dma_start(bct[64 * (h // 4):64 * (h // 4) + NCMP, h % 4, :], src).then_inc(sem("bias_cmp_in"), 16)
            for m in range(2):
                evacuate(("kcvc", m), kcvc[:, m, :], "kcvc_read")
            act.wait_ge(sem("kcvc_read"), 2)
            for i, dst in enumerate((kc2, vc2)):
                for g in range(2):
                    r = slice(64 * g, 64 * g + 64)
                    act.dma_start(dst[0:64, g, :], kcvc[r, i, :]).then_inc(sem("pairs_in"), 16)
                    act.dma_start(dst[64:128, g, 0:S - 1], kcvc[r, i, 1:S]).then_inc(sem("pairs_in"), 16)
            for m in range(2):
                evacuate(("kskw", m), [ks2, kw2][m], "kskw_read")
            for T in range(ST):
                evacuate(("vsvw", T), vsw[:, T, :], "vsvw_read", w=256)
            for i in range(2):
                evacuate(("pe", i), pos_hid[:, i:i + 1], "pe_read", w=1)
            act.wait_ge(sem("pe_read"), 2)
            for i in range(2):
                finished(act, ("hid", i))
                src = ps[:, bank_of[("hid", i)], 0:64].rearrange("p (g n) -> p g n", g=2)[:, :, 0:NCMP]
                dst = chid[:, 64 * i:64 * i + 64].rearrange("p (g n) -> p g n", g=2)[:, :, 0:NCMP]
                run(nc.scalar.activation(dst, src, ACT.Gelu_apprx_tanh, bias=pos_hid[:, i:i + 1]), "chid")
            table[0] = None
            evacuate("kcmp", kcmp[:, 0:NCMP], "kcmp_read", w=NCMP)
            evacuate("vcmp", vcmp, "vcmp_read", src=ps[0:NCMP, bank_of["vcmp"], 0:128])
            for h in range(8):
                src = bass.AP(tensor=near_d.tensor, offset=near_d.offset + (4 + h) * P * REV + 127,
                              ap=[[REV - 1, P], [1, 256]])
                act.dma_start(bt2[:, h, :], src).then_inc(sem("bias2_in"), 16)
            for j in range(4):
                if j:
                    act.wait_ge(sem("conv_read"), 2 * j - 1)
                evacuate(("conv", 3 * j), convc, "cc_read")
            squares_of(4, lambda k: convo[:, k, :], ("conv_out", 1))
            rstd_of("sum_conv", 512)
            for k in range(4):
                hi_of("conv", k, ahi[:, k, :])
            for m in range(4):
                evacuate(("q2", m), q2[:, m, :], "q2_read", scale=0.125)
            evacuate(("gl", 0), glf, "gl_read", ACT.Sigmoid)

            def nsa_out(T):
                evacuate(("nsa_out", T), onsa[:, :, T * P:(T + 1) * P], "nsa_out_read",
                         src=bank(("nsa_out", T)).rearrange("p (a t) -> p a t", a=4))

            act.wait_ge(sem("lo"), SPLITS["conv"] + 4)
            attention(jobs2, "nsa", nsa_out)
            act.wait_ge(sem("nsa_out_read"), ST)
            squares_of(4, lambda k: onsa[:, k, :])
            rstd_of("sum_nsa", 512)
            for k in range(4):
                hi_of("nsa", k, ahi[:, 4 + k, :])
            finished(act, ("nsa_out", ST - 1))
            act.dma_start(memx, memT).then_inc(sem("mem_in"), 16)
            for k in range(2):
                evacuate(("wout2", k), Y[:, k, :], "wout2_read")
            act.wait_ge(sem("mem_in"), 16)
            squares_of(KD, lambda k: memx[:, k, :], width=MEM)
            rstd_of("sum_mem", D, MEM)
            for k in range(KD):
                hi_of("mem", k, hhi[:, k, 0:MEM], src=tmp[(SPLITS["mem"] + k) % 2][:, 0:MEM])
            for k in range(KD):
                if k >= 2:
                    evacuate(("wout2", k), Y[:, k, :], "wout2_read")
                act.wait_ge(sem("wout2_read"), k + 1)
                square_for("sum_w2", k, Y[:, k, :])
            for m in range(2):
                evacuate(("memk", m), mk[:, m, :], "memk_read", w=MEM)
            rstd_of("sum_w2", D)
            for T in range(2):
                evacuate(("memv", T), mv_[:, T, :], "memv_read", w=MEM)
            squares_of(KD, lambda k: X[:, k, :], ("res1", 1))
            rstd_of("sum_n2", D)
            for k in range(KD):
                hi_of("n2", k, hhi[:, k, :], free=("memv", 1))
            for m in range(2):
                evacuate(("memq", m), mq[:, m, :], "memq_read", scale=0.125)

            def mem_out(T):
                evacuate(("mem_out", T), om[:, :, T * P:(T + 1) * P], "mem_out_read",
                         src=bank(("mem_out", T), 256).rearrange("p (a t) -> p a t", a=2))

            attention(jobs3, "mem", mem_out)
            for k in range(2):
                hi_of("mo", k, ahi[:, k, :], src=om[:, k, :], ready=("mem_out_read", ST))
            for k in range(KD):
                evacuate(("memo", k), Y[:, k, :], "memo_read")
                act.wait_ge(sem("memo_read"), k + 1)
                square_for("sum_mo", k, Y[:, k, :])
            rstd_of("sum_mo", D)
            squares_of(KD, lambda k: X[:, k, :], ("res3", 1))
            rstd_of("sum_n4", D)
            for k in range(KD):
                hi_of("n4", k, hhi[:, k, :])
            n = 0
            for g, nt in enumerate(FFN_TILES):
                for m in range(nt):
                    i = 2 * EXPERTS + n
                    if n < 2:
                        act.wait_ge(sem("eu_read"), 2 * EXPERTS)
                    else:
                        act.wait_ge(sem("fu_read"), n - 1)
                    evacuate((("fg", g), m), sil[n % 2], "silu_read", ACT.Silu)
                    hi_of(f"ffn{g}", m, ahi[:, m, :], ready=("fu_read", n + 1),
                          free=(("fd", g - 1), 7) if g else None)
                    n += 1
            for k in range(KD):
                act.wait_ge(sem("fd_read"), 2 * KD + k + 1)
                square_for("sum_fd", k, Y[:, k, :])
            rstd_of("sum_fd", D)

        @block.vector
        def _(dve):
            count = {}

            def run(ins, name="step", wait=True):
                count[name] = count.get(name, 0) + 1
                ins.then_inc(sem("dve_" + name if name == "step" else name), 1)
                if wait:
                    dve.wait_ge(sem("dve_" + name if name == "step" else name), count[name])

            V = nc.vector

            def lo_of(key, i, dst, dst_hi, src=None, bias=None):
                n = SPLITS[key] + i
                assert n == count.get("lo", 0)
                dve.wait_ge(sem("hi"), n + 1)
                src = tmp[n % 2] if src is None else src
                hi32 = dst_hi.bitcast(F32)
                if bias is None:
                    run(V.tensor_tensor(dst, src, hi32, ALU.subtract), "lo")
                else:
                    run(V.scalar_tensor_tensor(dst, src, bias, hi32, op0=ALU.add, op1=ALU.subtract), "lo")

            def split(key, n, produce, hi, lo, k0=0, bias=None, w=S):
                for i in range(n + 1):
                    if i < n:
                        produce(i, tmp[(SPLITS[key] + i) % 2][:, 0:w])
                    if i:
                        j = i - 1
                        lo_of(key, j, lo[:, k0 + j, 0:w], hi[:, k0 + j, 0:w], tmp[(SPLITS[key] + j) % 2][:, 0:w],
                              bias(j) if bias else None)

            def add_square(key, k):
                dve.wait_ge(sem("squares"), square_base[key][0] + k + 1)
                run(V.tensor_tensor(sq[0], sq[0], sq[1], ALU.add), "squares_added")

            def add_squares_behind(key, k):
                if k >= 2:
                    add_square(key, k - 1)
                if k == KD - 1:
                    add_square(key, k)

            def wait_rstd():
                count["norms"] = count.get("norms", 0) + 1
                dve.wait_ge(sem("rstd"), count["norms"])

            def normed(n, src, g, w=S):
                def produce(i, dst):
                    run(V.scalar_tensor_tensor(dst, src(i), g(i), rstd[:, 0:w], op0=ALU.mult, op1=ALU.mult),
                        "unsplit")
                    if i == n - 1:
                        run(V.memset(small[:, 360:361], 0.0), "rstd_used")
                return produce

            first = {}
            for i, (name, n) in enumerate(STREAM):
                first[name] = sum(x for _, x in STREAM[:i])

            def mod_sum(n):
                if n >= 2:
                    finished(dve, ("mod", n - 2))
                acc = accmod(n)
                for half in range(2):
                    i = first[f"mod{n}"] + half
                    dve.wait_ge(sem(f"raw_in{i % RAW_SLOTS}"), 16 * (i // RAW_SLOTS + 1))
                    for k in range(4):
                        w_ = raw[:, i % RAW_SLOTS, k * 512:(k + 1) * 512]
                        c_ = cact[:, 4 * half + k:4 * half + k + 1]
                        name = "mod_used" if k == 3 else "step"
                        if half == 0 and k == 0:
                            run(V.tensor_scalar(acc, w_, c_, None, ALU.mult), name)
                        else:
                            run(V.scalar_tensor_tensor(acc, w_, c_, acc, op0=ALU.mult, op1=ALU.add), name)

            def mod_read(n):
                finished(dve, ("mod", n))
                run(V.tensor_tensor(mod[:, 4 * n:4 * n + 4], bank(("mod", n), 4), col("b_mod", 4 * n, 4), ALU.add),
                    "mod_read")

            dve.wait_ge(sem("c_act"), 1)
            for n in range(4):
                mod_sum(n)
            for n in range(4):
                mod_read(n)
            run(V.scalar_tensor_tensor(gain[:, :], mod[:, 8:16], 1.0, col("g1", 0, 8), op0=ALU.add, op1=ALU.mult))
            wait_rstd()
            split("h1", KD, normed(KD, lambda k: X[:, k, :], lambda k: gain[:, k:k + 1]), hhi, hlo,
                  bias=lambda k: mod[:, k:k + 1])
            dve.wait_ge(sem("ws_in"), 16)
            dve.wait_ge(sem("masks_in"), 16)
            run(V.tensor_tensor(wsm, wsm, causal.unsqueeze(1).to_broadcast([P, 4, P]), ALU.mult), "spatial_masked")
            mod_sum(4)
            mod_sum(5)
            for c in range(ST):
                dve.wait_ge(sem("gelu_v"), c + 1)
                run(V.bn_stats(bn[:, c, :], gv_[:, c, :]))
                run(V.bn_aggr(mv[:, c, :], bn[:, c, :]), "ln_stats")
            dve.wait_ge(sem("ln_rstd"), 1)
            dve.wait_ge(sem("rows_in"), 16)
            for c in range(ST):
                v = gv_[:, c, :]
                run(V.tensor_scalar(v, v, mv[:, c, 0:1], lnr[:, c:c + 1], ALU.subtract, ALU.mult))
                run(V.tensor_tensor(v, v, rows[:, ROW["ln_g"]:ROW["ln_g"] + 512], ALU.mult))
                run(V.tensor_tensor(v, v, rows[:, ROW["ln_b"]:ROW["ln_b"] + 512], ALU.add), "ln_done")
            dve.wait_ge(sem("router_in"), 16)
            run(V.tensor_copy(rhi[:, :, :], router))
            run(V.tensor_tensor(rlo[:, :, :], router, rhi[:, :, :].bitcast(F32), ALU.subtract), "router_split")
            run(V.tensor_copy(scol[:, 0:20], rows[:, ROW["b_router"]:ROW["b_router"] + 20]))
            mod_read(4)
            mod_sum(6)
            mod_read(5)
            mod_sum(7)
            mod_read(6)
            mod_sum(8)
            mod_read(7)
            zb = ar(8704, 1024)
            for a in range(2):
                finished(dve, ("z", a))
                run(V.tensor_scalar(zb[:, a * S:(a + 1) * S], bank(("z", a)), col("gla_b", a), None, ALU.add), "z_read")
            finished(dve, "iw")
            run(V.tensor_copy(iwt, tiles(bank("iw"), 4)[:, :, 16:20]), "iw_read")
            mod_sum(9)
            mod_read(8)
            mod_read(9)

            def mixed(g, dst):
                finished(dve, ("mix", g))
                dve.wait_ge(sem("gelu_u"), 4)
                b_ = rows[:, ROW["b_s"] + g * P:ROW["b_s"] + (g + 1) * P].unsqueeze(1).to_broadcast([P, ST, P])
                run(V.tensor_tensor(tiles(dst, ST), tiles(bank(("mix", g)), ST), b_, ALU.add), "mix_read")
                run(V.tensor_tensor(dst, dst, gu_[:, g, :], ALU.mult), "unsplit")

            split("ya", 4, mixed, ahi, alo)
            dve.wait_ge(sem("softplus"), 3)
            run(V.scalar_tensor_tensor(edec, zb, 0.0, edec, op0=ALU.min, op1=ALU.subtract))
            run(V.tensor_scalar(edec, edec, 1.0 / 16.0, None, ALU.mult))
            for n in range(8):
                c_ = slice(n * P, (n + 1) * P)
                run(V.tensor_tensor_scan(bcum[:, c_], ones, edec[:, c_], 0.0, ALU.mult, ALU.add), wait=n == 7)

            def ups(n, ms):
                for m in ms:
                    finished(dve, (("up", n), m))
                    dve.wait_ge(sem("gate_read"), 8 * n + m + 1)
                    if n == 0:
                        run(V.tensor_tensor(Y[:, m, :], bank((("up", n), m)), Y[:, m, :], ALU.mult), "up_read")
                    else:
                        gate = gate3[m % 4] if n == 2 else tmp[m % 2]
                        run(V.tensor_tensor(tmp[m % 2], bank((("up", n), m)), gate, ALU.mult), "up_read")
                        run(V.tensor_tensor(Y[:, m, :], Y[:, m, :], tmp[m % 2], ALU.add),
                            "merged_in" if n == 1 else "unsplit")

            def difference(lv):
                half = 1 << lv
                b_ = bcum.rearrange("p (n b) -> p n b", b=2 * half)
                ref = b_[:, :, half - 1:half].to_broadcast([P, 1024 // (2 * half), 2 * half])
                run(V.tensor_tensor(edec.rearrange("p (n b) -> p n b", b=2 * half), b_, ref, ALU.subtract), "decay_diff")

            difference(0)
            finished(dve, "iw")
            run(V.memset(attn, 0.0))
            dve.wait_ge(sem("gla_qk"), 4)

            def flat(t):
                return t.rearrange("p a t -> p (a t)")

            for lv in range(LEVELS):
                if lv < LEVELS - 1:
                    dve.wait_ge(sem("decay"), lv + 1)
                    dve.wait_ge(sem("decay_lower"), lv + 1)
                    if lv:
                        finished(dve, ("level", lv - 1, ST - 1))
                    run(V.tensor_tensor(flat(qs), flat(qg), edec, ALU.mult), "level_scaled", False)
                    run(V.tensor_tensor(flat(ksc), flat(kg), edec, ALU.mult), "level_scaled")
                if lv < LEVELS - 2:
                    difference(lv + 1)
                if lv == LEVELS - 1:
                    dve.wait_ge(sem("decay"), LEVELS)
                    run(V.tensor_tensor(flat(qs), flat(qg), edec, ALU.mult))
                    b_ = bcum.rearrange("p (n b) -> p n b", b=P)
                    run(V.tensor_tensor(edec.rearrange("p (n b) -> p n b", b=P), b_[:, :, P - 1:P].to_broadcast([P, 8, P]), b_,
                                        ALU.subtract), "decay_diff")
                for n in range(4):
                    finished(dve, ("level", lv, n))
                    mask = levelmask[:, lv, :].bitcast(U32).unsqueeze(1).to_broadcast([P, 4, P])
                    at_ = (n % 2) * 1024 + (n // 2) * 512
                    run(V.copy_predicated(attn[:, at_:at_ + 512].rearrange("p (h t) -> p h t", h=4), mask,
                                          tiles(bank(("level", lv, n)), 4)), "level_read")
                if lv in (0, 3):
                    ups(0, range(4) if lv == 0 else range(4, 8))
            dve.wait_ge(sem("decay"), LEVELS + 1)
            run(V.tensor_tensor(flat(ksc), flat(kg), edec, ALU.mult), "khat")
            dve.wait_ge(sem("decay_last"), 1)
            for c in range(ST - 1):
                finished(dve, ("upd", c))
                if c == 0:
                    run(V.tensor_copy(state[:, 0, :], bank(("upd", 0), 256)), "state")
                else:
                    for a in range(2):
                        a_ = slice(a * P, (a + 1) * P)
                        run(V.scalar_tensor_tensor(state[:, c, a_], state[:, c - 1, a_], ebl[:, 4 * a + c:4 * a + c + 1],
                                                   bank(("upd", c), 256)[:, a_], op0=ALU.mult, op1=ALU.add),
                            "state" if a else "step")

            def gla_out(h, dst):
                wait_rstd()
                run(V.scalar_tensor_tensor(dst, og[:, h, :], col("gla_g"), rstds[h % 2], op0=ALU.mult, op1=ALU.mult),
                    "rstd_used")
                dve.wait_ge(sem("gla_r"), h + 1)
                run(V.tensor_tensor(dst, dst, rg[:, h, :], ALU.mult), "unsplit")

            split("yb", 4, gla_out, ahi, alo, 4)

            def index(T):
                w = (T + 1) * P
                sc = selmask[T]
                for h in range(4):
                    finished(dve, ("idx", T, h))
                    dst = sc if h == 0 else eqm[:, 0:w]
                    run(V.tensor_scalar(dst, bank(("idx", T, h), w), 0.0, iwt[:, T, h:h + 1], ALU.max, ALU.mult),
                        "index_read")
                    if h:
                        run(V.tensor_tensor(sc, sc, eqm[:, 0:w], ALU.add))
                run(V.tensor_tensor(sc[:, T * P:w], sc[:, T * P:w], noadm, ALU.add))

            def qk_normed(h):
                for t, g, r_ in ((dq, "qn", rstds[0]), (dk, "kn", rstds[1])):
                    wait_rstd()
                    run(V.scalar_tensor_tensor(t[:, h, :], t[:, h, :], col(g), r_, op0=ALU.mult, op1=ALU.mult),
                        "rstd_used")

            def largest(T, rounds):
                sc, wk = selmask[T], work[:, 0:(T + 1) * P]
                for r in rounds:
                    run(V.max(max8, wk if r else sc))
                    if r < TOPK // 8 - 1:
                        run(V.match_replace(wk, max8, wk if r else sc, -3.4e38))

            def select(T):
                w = (T + 1) * P
                sc, wk, eq_, cu = selmask[T], work[:, 0:w], eqm[:, 0:w], cum[:, 0:w]
                thr = max8[:, 7:8]
                run(V.tensor_scalar(wk, sc, thr, None, ALU.is_gt))
                run(V.tensor_reduce(cnt, wk, AX.X, ALU.add))
                run(V.tensor_scalar(cnt, cnt, -1.0, float(TOPK), ALU.mult, ALU.add))
                run(V.tensor_scalar(eq_, sc, thr, None, ALU.is_equal))
                run(V.tensor_tensor_scan(cu, ones[:, 0:1].to_broadcast([P, w]), eq_, 0.0, ALU.mult, ALU.add))
                run(V.scalar_tensor_tensor(eq_, cu, cnt, eq_, op0=ALU.is_le, op1=ALU.mult))
                run(V.tensor_tensor(wk, wk, eq_, ALU.add))
                run(V.tensor_scalar(sc, wk, -1.0, -NEG, ALU.add, ALU.mult))

            rounds = TOPK // 8
            index(1)
            index(2)
            largest(1, range(8))
            index(3)
            largest(1, range(8, rounds))
            select(1)
            mod_sum(10)
            largest(2, range(8))
            mod_sum(11)
            largest(2, range(8, rounds))
            mod_read(10)
            mod_read(11)
            select(2)
            qk_normed(0)
            qk_normed(1)
            ups(1, range(4))
            qk_normed(2)
            largest(3, range(8))
            qk_normed(3)
            ups(1, range(4, 6))
            largest(3, range(8, 12))
            ups(1, range(6, 8))
            largest(3, range(12, rounds))
            select(3)

            def attention(jobs, name, bias_of, gate_of=None, after=None):
                ring = probs[name]
                exp_done = name + ("_logits_read" if name == "mem" else "_exp")

                def then():
                    dve.wait_ge(sem("dve_step"), count["step"])

                for i in range(len(jobs) + 1):
                    if i < len(jobs):
                        kind, T, h, nt, w = jobs[i]
                        st = stat[:, 4 * (i % 4):4 * (i % 4) + 4]
                        pb = ring[i % len(ring)]
                        if i >= len(ring):
                            finished(dve, (name + "T", i - len(ring)))
                        finished(dve, (name, i))
                        if kind == "cmp":
                            lg = heads(bank((name, i)))
                            m4 = small[:, 4 * h[1]:4 * h[1] + 4]
                            run(V.tensor_reduce(m4, lg, AX.X, ALU.max))
                            run(V.tensor_tensor(heads(pb), lg, m4.unsqueeze(2).to_broadcast([P, 4, NCMP]),
                                                ALU.subtract), name + "_logits_read", False)
                        elif kind == "mem":
                            run(V.tensor_reduce(st[:, 0:1], bank((name, i), w), AX.X, ALU.max, negate=True),
                                name + "_max", False)
                        else:
                            bias_of(jobs[i], bank((name, i)), pb)
                    if i:
                        n = i - 1
                        kind1, T1, h1, nt1, w1 = jobs[n]
                        st1 = stat[:, 4 * (n % 4):4 * (n % 4) + 4]
                        pb1 = ring[n % len(ring)]
                        dve.wait_ge(sem(exp_done), n + 1)
                        if kind1 == "cmp":
                            s4 = small[:, 8 + 4 * h1[1]:12 + 4 * h1[1]]
                            pv = heads(pb1)
                            run(V.tensor_tensor(pv, pv, cmpmask[:, T1, 0:NCMP].unsqueeze(1).to_broadcast([P, 4, NCMP]),
                                                ALU.mult))
                            run(V.tensor_reduce(s4, pv, AX.X, ALU.add))
                            run(V.tensor_scalar(s4, s4, 1e-30, None, ALU.max))
                            run(V.reciprocal(s4, s4))
                            run(V.tensor_tensor(s4, s4, gate_of(jobs[n]), ALU.mult))
                        else:
                            run(V.reciprocal(st1[:, 3:4], st1[:, 2:3]), "step", False)
                    if i < len(jobs) and kind not in ("cmp", "mem"):
                        run(V.tensor_reduce(st[:, 0:1], pb[:, 0:w], AX.X, ALU.max, negate=True), name + "_max", False)
                    if i:
                        then()
                        if kind1 == "cmp":
                            run(V.tensor_tensor(pv, pv, s4.unsqueeze(2).to_broadcast([P, 4, NCMP]), ALU.mult),
                                name + "_probs", False)
                        elif gate_of:
                            run(V.tensor_scalar(pb1[:, 0:w1], pb1[:, 0:w1], st1[:, 3:4], gate_of(jobs[n]),
                                                ALU.mult, ALU.mult), name + "_probs", False)
                        else:
                            run(V.tensor_scalar(pb1[:, 0:w1], pb1[:, 0:w1], st1[:, 3:4], None, ALU.mult),
                                name + "_probs", False)
                    if after:
                        after(i)

            def with_bias(bt, scale, o, pb, nt, sem_name):
                w = nt * P
                if nt == 1:
                    run(V.scalar_tensor_tensor(pb[:, 0:P], o[:, 0:P], scale, bt[:, P:2 * P], op0=ALU.mult, op1=ALU.add),
                        sem_name)
                    return
                if nt > 2:
                    run(V.tensor_scalar(pb[:, 0:w - 2 * P], o[:, 0:w - 2 * P], scale, bt[:, 0:1], ALU.mult, ALU.add),
                        "step", False)
                run(V.scalar_tensor_tensor(pb[:, w - 2 * P:w], o[:, w - 2 * P:w], scale, bt, op0=ALU.mult, op1=ALU.add),
                    sem_name)
                dve.wait_ge(sem("dve_step"), count["step"])

            def dsa_bias(job, o, pb):
                _, T, h, nt, w = job
                with_bias(bt1[:, h, :], P ** -0.5, o, pb, nt, "dsa_logits_read")
                if T:
                    run(V.tensor_tensor(pb[:, 0:w], pb[:, 0:w], selmask[T], ALU.add))

            dve.wait_ge(sem("bias1_in"), 16 * 4)
            def dsa_low(i):
                T = (i - 9) // 4
                if i < 9 or (i - 9) % 4:
                    return
                n = SPLITS["yc"] + T
                t4 = tmp[n % 2].rearrange("p (h t) -> p h t", h=4)
                ts = slice(T * P, (T + 1) * P)
                lo_of("yc", T, alo[:, 0:4, ts], ahi[:, 0:4, ts], t4)

            attention(jobs1, "dsa", dsa_bias, after=dsa_low)
            dsa_low(17)
            dsa_low(21)
            ups(2, range(KD))
            for k in range(KD):
                lo_of("merged", k, hlo[:, k, :], hhi[:, k, :], Y[:, k, :])
            dve.wait_ge(sem("x_in"), 32)
            for k in range(KD):
                finished(dve, ("wout", k))
                run(V.scalar_tensor_tensor(X[:, k, :], bank(("wout", k)), mod[:, 16 + k:17 + k], X[:, k, :],
                                           op0=ALU.mult, op1=ALU.add), "wout_read")
                add_squares_behind("sum_h2", k)
            run(V.scalar_tensor_tensor(gain[:, :], mod[:, 32:40], 1.0, col("g2", 0, 8), op0=ALU.add, op1=ALU.mult))
            wait_rstd()
            split("h2", KD, normed(KD, lambda k: X[:, k, :], lambda k: gain[:, k:k + 1]), hhi, hlo,
                  bias=lambda k: mod[:, 24 + k:25 + k])

            finished(dve, "routerT")
            lg = small[:, 368:368 + 80].rearrange("p (a n) -> p a n", a=ST)
            gl_e = small[:, 344:360].rearrange("p (a n) -> p a n", a=ST)
            bias_ = scol[:, 0:20].unsqueeze(1).to_broadcast([P, ST, 20])
            run(V.tensor_tensor(lg, tiles(bank("routerT", 128), ST)[:, :, 0:20], bias_, ALU.add), "router_read")
            r1 = small[:, 448:452].unsqueeze(2)
            r2 = small[:, 452:456].unsqueeze(2)
            run(V.tensor_reduce(small[:, 448:452], lg[:, :, 0:4], AX.X, ALU.max))
            run(V.tensor_tensor(gl_e, lg[:, :, 0:4], r1.to_broadcast([P, ST, 4]), ALU.subtract), "route_max")
            dve.wait_ge(sem("route_exp"), 1)
            pg = small[:, 456:460]
            run(V.tensor_reduce(pg, gl_e, AX.X, ALU.add))
            run(V.reciprocal(pg, pg))

            def first_of(dst, src, best):
                run(V.tensor_tensor(dst, src, best.to_broadcast([P, ST, 4]), ALU.is_equal))
                seen = small[:, 460:464].unsqueeze(2)
                run(V.tensor_scalar(seen, dst[:, :, 0:1], -1.0, 1.0, ALU.mult, ALU.add))
                for j in range(1, 4):
                    run(V.tensor_tensor(dst[:, :, j:j + 1], dst[:, :, j:j + 1], seen, ALU.mult))
                    run(V.tensor_tensor(seen, seen, dst[:, :, j:j + 1], ALU.subtract))

            goh = small[:, 464:480].rearrange("p (a n) -> p a n", a=ST)
            run(V.tensor_reduce(small[:, 452:456], gl_e, AX.X, ALU.max))
            first_of(goh, gl_e, r2)
            sel = small[:, 480:496].rearrange("p (a n) -> p a n", a=ST)
            t16 = small[:, 496:512].rearrange("p (a n) -> p a n", a=ST)
            for g in range(4):
                dst = sel if g == 0 else t16
                run(V.tensor_tensor(dst, lg[:, :, 4 + 4 * g:8 + 4 * g], goh[:, :, g:g + 1].to_broadcast([P, ST, 4]),
                                    ALU.mult))
                if g:
                    run(V.tensor_tensor(sel, sel, t16, ALU.add))
            e1 = small[:, 512:528].rearrange("p (a n) -> p a n", a=ST)
            e2 = small[:, 528:544].rearrange("p (a n) -> p a n", a=ST)
            run(V.tensor_reduce(small[:, 448:452], sel, AX.X, ALU.max))
            first_of(e1, sel, r1)
            run(V.scalar_tensor_tensor(t16, e1, -3e38, sel, op0=ALU.mult, op1=ALU.add))
            run(V.tensor_reduce(small[:, 452:456], t16, AX.X, ALU.max))
            first_of(e2, t16, r2)
            dif = stat[:, 8:12]
            run(V.tensor_tensor(dif, small[:, 452:456], small[:, 448:452], ALU.subtract), "route_diff")
            dve.wait_ge(sem("route_exp"), 2)
            w1_ = small[:, 448:452]
            run(V.tensor_scalar(w1_, dif, 1.0, None, ALU.add))
            run(V.reciprocal(w1_, w1_))
            run(V.tensor_tensor(w1_, w1_, pg, ALU.mult))
            run(V.tensor_tensor(dif, dif, w1_, ALU.mult))
            run(V.tensor_tensor(e1, e1, w1_.unsqueeze(2).to_broadcast([P, ST, 4]), ALU.mult))
            run(V.tensor_tensor(e2, e2, dif.unsqueeze(2).to_broadcast([P, ST, 4]), ALU.mult))
            run(V.tensor_tensor(e1, e1, e2, ALU.add))
            comb = scol[:, 0:64].rearrange("p (a g e) -> p a g e", a=ST, g=4)
            for g in range(4):
                run(V.tensor_tensor(comb[:, :, g, :], e1, goh[:, :, g:g + 1].to_broadcast([P, ST, 4]), ALU.mult),
                    "combined" if g == 3 else "step")
            finished(dve, "combT")
            run(V.tensor_copy(combT, ps[0:16, bank_of["combT"], :]), "combT_read")

            for g in range(EXPERTS // EPG):
                def gated(i, dst, g=g):
                    e, m = EPG * g + i // 2, i % 2
                    finished(dve, (("eu", e), m))
                    dve.wait_ge(sem("silu_read"), 2 * e + m + 1)
                    run(V.tensor_tensor(dst, bank((("eu", e), m)), sil[m], ALU.mult), "eu_read")
                    dve.wait_ge(sem("comb_read"), e + 1)
                    run(V.tensor_tensor(dst, dst, combs[e % 2], ALU.mult), "unsplit")

                split(f"moe{g}", KD, gated, ahi, alo)
                for k in range(KD):
                    finished(dve, (("ed", g), k))
                    if g == 0:
                        run(V.tensor_copy(Y[:, k, :], bank((("ed", g), k))), "ed_read")
                    else:
                        run(V.tensor_tensor(Y[:, k, :], bank((("ed", g), k)), Y[:, k, :], ALU.add), "ed_read")
                    if g == EXPERTS // EPG - 1:
                        run(V.scalar_tensor_tensor(X[:, k, :], Y[:, k, :], mod[:, 40 + k:41 + k], X[:, k, :],
                                                   op0=ALU.mult, op1=ALU.add), "ffn1_added")
                        add_squares_behind("sum_n0", k)
            def norm_gain(n):
                return lambda k: col("norms", 8 * n + k)

            wait_rstd()
            split("n0", KD, normed(KD, lambda k: X[:, k, :], norm_gain(0)), hhi, hlo)
            dve.wait_ge(sem("comp_in"), 16 * 3)
            for m in range(PIECE):
                for i in range(2):
                    a_, w_ = pe_acc[:, i * P:(i + 1) * P], cw1[:, i, m * P:(m + 1) * P]
                    if m == 0:
                        run(V.tensor_scalar(a_, w_, pe_s[:, 0:1], None, ALU.mult))
                    else:
                        run(V.scalar_tensor_tensor(a_, w_, pe_s[:, m:m + 1], a_, op0=ALU.mult, op1=ALU.add),
                            "pe_sum" if m == PIECE - 1 else "step")
            for j in range(4):
                finished(dve, ("conv", 3 * j + 1))
                dve.wait_ge(sem("cc_read"), j + 1)
                u, y = tmp
                run(V.tensor_tensor(u, bank(("conv", 3 * j + 1)), convc, ALU.mult), "conv_read")
                run(V.tensor_scalar(y, u, col("conv_w", j), None, ALU.mult))
                for t in (1, 2):
                    run(V.scalar_tensor_tensor(y[:, t:S], u[:, 0:S - t], col("conv_w", 4 * t + j), y[:, t:S],
                                               op0=ALU.mult, op1=ALU.add))
                finished(dve, ("conv", 3 * j + 2))
                run(V.tensor_tensor(convo[:, j, :], bank(("conv", 3 * j + 2)), y, ALU.mult), "conv_read")
                run(V.memset(small[:, 361:362], 0.0), "conv_out")
            wait_rstd()
            split("conv", 4, normed(4, lambda k: convo[:, k, :], lambda k: col("gn_conv", k)), ahi, alo)
            finished(dve, "glT")
            run(V.tensor_copy(glt, tiles(bank("glT"), ST)[:, :, 0:24]), "glT_read")

            def nsa_bias(job, o, pb):
                kind, T, (j, g), nt, w = job
                with_bias(bt2[:, 4 * g + j, :], 1.0, o, pb, nt, "nsa_logits_read")
                if kind == "win" and nt == 3:
                    run(V.tensor_tensor(pb[:, 0:P], pb[:, 0:P], band, ALU.add))

            def nsa_gate(job):
                kind, T, (j, g), nt, w = job
                if kind == "cmp":
                    return glt[:, T, 12 * g:12 * g + 10:3]
                n = (4 * g + j) * 3 + ("cmp", "sel", "win").index(kind)
                return glt[:, T, n:n + 1]

            dve.wait_ge(sem("bias2_in"), 16 * 8)
            attention(jobs2, "nsa", nsa_bias, nsa_gate)
            wait_rstd()
            split("nsa", 4, normed(4, lambda k: onsa[:, k, :], lambda k: col("gn_nsa", k)), ahi, alo, 4)

            def residual(n, name):
                wait_rstd()
                for k in range(KD):
                    t = tmp[k % 2]
                    run(V.scalar_tensor_tensor(t, Y[:, k, :], col("norms", 8 * n + k), rstd, op0=ALU.mult, op1=ALU.mult),
                        "rstd_used" if k == KD - 1 else "step")
                    run(V.tensor_tensor(X[:, k, :], X[:, k, :], t, ALU.add), name)

            wait_rstd()
            split("mem", KD, normed(KD, lambda k: memx[:, k, :], lambda k: col("mem_norm", k), MEM), hhi, hlo, w=MEM)
            for k in range(KD):
                add_squares_behind("sum_w2", k)
            residual(1, "res1")
            wait_rstd()
            split("n2", KD, normed(KD, lambda k: X[:, k, :], norm_gain(2)), hhi, hlo)

            attention(jobs3, "mem", None)
            for k in range(2):
                lo_of("mo", k, alo[:, k, :], ahi[:, k, :], om[:, k, :])
            for k in range(KD):
                add_squares_behind("sum_mo", k)
            residual(3, "res3")
            wait_rstd()
            split("n4", KD, normed(KD, lambda k: X[:, k, :], norm_gain(4)), hhi, hlo)
            done_tiles = [0]
            for g, nt in enumerate(FFN_TILES):
                def gated2(i, dst, g=g):
                    finished(dve, (("fu", g), i))
                    n = done_tiles[0]
                    done_tiles[0] += 1
                    dve.wait_ge(sem("silu_read"), 2 * EXPERTS + n + 1)
                    run(V.tensor_tensor(dst, bank((("fu", g), i)), sil[n % 2], ALU.mult), "fu_read")

                split(f"ffn{g}", nt, gated2, ahi, alo)
                for k in range(KD):
                    finished(dve, (("fd", g), k))
                    if g == 0:
                        run(V.tensor_copy(Y[:, k, :], bank((("fd", g), k))), "fd_read")
                    else:
                        run(V.tensor_tensor(Y[:, k, :], bank((("fd", g), k)), Y[:, k, :], ALU.add), "fd_read")
                    if g == len(FFN_TILES) - 1:
                        add_squares_behind("sum_fd", k)
            residual(5, "res5")

        @block.gpsimd
        def _(pool):
            n = 0
            for i, kind in enumerate(KIND):
                if kind == "mod":
                    continue
                r, s = i % RAW_SLOTS, n % SPLIT_SLOTS
                pool.wait_ge(sem(f"raw_in{r}"), 16 * (i // RAW_SLOTS + 1))
                if n >= SPLIT_SLOTS:
                    pool.wait_ge(sem("matmuls_done"), piece_end[n - SPLIT_SLOTS])
                nc.gpsimd.tensor_scalar(whi[:, s, :], raw[:, r, :], 1.0, 1.0, ALU.mult, ALU.mult)\
                    .then_inc(sem("weights_hi"), 1)
                pool.wait_ge(sem("weights_hi"), n + 1)
                nc.gpsimd.tensor_tensor(wlo[:, s, :], raw[:, r, :], whi[:, s, :].bitcast(F32), ALU.subtract)\
                    .then_inc(sem("weights_split"), 1)
                n += 1

        @block.sync
        def _(sp):
            sp.dma_start(cols[:, :], cols_d).then_inc(sem("cols_in"), 16)
            used = {"mod": 0, "split": 0}
            slot_free = []
            for i, kind in enumerate(KIND):
                if i == RAW_SLOTS:
                    sp.dma_start(con[:, 0:2 * P], const_d[:, 0:2 * P]).then_inc(sem("const_in"), 16)
                    sp.dma_start(X[:, :, :], xT).then_inc(sem("x_in"), 16)
                if i == 3 * RAW_SLOTS + 2:
                    sp.dma_start(Yf[0:33, 2048:2060], relT).then_inc(sem("tables_in"), 16)
                    sp.dma_start(Yf[0:33, 2060:2060 + VEC], onehot).then_inc(sem("tables_in"), 16)
                    sp.dma_start(con[:, 2 * P:], const_d[:, 2 * P:]).then_inc(sem("masks_in"), 16)
                    sp.dma_start(rows, rows_d.partition_broadcast(P)).then_inc(sem("rows_in"), 16)
                    sp.dma_start(wsm[:, :, :], wsT).then_inc(sem("ws_in"), 16)
                    sp.dma_start(g2, gate2_d).then_inc(sem("gate2_in"), 16)
                    sp.dma_start(router, router_d).then_inc(sem("router_in"), 16)
                if i >= RAW_SLOTS:
                    sp.wait_ge(sem(slot_free[i - RAW_SLOTS][0]), slot_free[i - RAW_SLOTS][1])
                used[kind] += 1
                slot_free.append(("mod_used" if kind == "mod" else "weights_split", used[kind]))
                sp.dma_start(raw[:, i % RAW_SLOTS, :], stream[i]).then_inc(sem(f"raw_in{i % RAW_SLOTS}"), 16)
            for k in range(KD):
                sp.wait_ge(sem("res5"), k + 1)
                sp.dma_start(out[:, k, :], X[:, k, :]).then_inc(sem("out_written"), 16)
            sp.wait_ge(sem("out_written"), 16 * KD)
    return done


def columns(a):
    return np.ascontiguousarray(np.asarray(a, np.float32).reshape(-1, P).T)


def moving_tiles(w):
    k, n = w.shape
    return w.reshape(k // P, P, n // P, P).transpose(2, 0, 1, 3).reshape(-1, P, P)


def moving_rows(w):
    k, n = w.shape
    return w.reshape(k // P, P, n // P, P).transpose(0, 2, 1, 3).reshape(-1, P, P)


def constants():
    i = np.arange(P)
    c = np.zeros((P, NCONST), np.float32)

    def put(name, a):
        c[:, CON[name]:CON[name] + a.shape[1]] = a

    put("ident", np.eye(P))
    put("ones", np.ones((P, P)))
    put("causal", i[:, None] <= i[None, :])
    put("noadm", np.where(i[None, :] > i[:, None], NOT_ADMITTED, 0.0))
    put("band", np.where(i[None, :] <= i[:, None], NEG, 0.0))
    s, t = i[:, None], i[None, :]
    lv = [(s >> (n + 1) == t >> (n + 1)) & ((s >> n) & 1 == 0) & ((t >> n) & 1 == 1) for n in range(7)] + [s == t]
    put("levels", np.concatenate(lv, 1))
    n = np.arange(32)
    put("cmpmask", np.concatenate([(T * P + i[:, None] >= 16 * n[None, :] + 31) for T in range(ST)], 1))
    return c


def bucket_onehot():
    dist = np.concatenate([255 - np.arange(REV), np.arange(FWD) - 511])
    n = np.maximum(dist, 0)
    large = 16 + (np.log(np.maximum(n, 16).astype(np.float32) / 16) / np.log(8.0) * 16).astype(np.int32)
    b = np.where(n < 16, n, np.minimum(large, 31))
    rows = np.zeros((NBUCKET + 1, VEC), np.float32)
    ok = dist >= 0
    rows[b[ok], np.nonzero(ok)[0]] = 1.0
    rows[NBUCKET, ~ok] = 1.0
    return rows


def layout(x):
    f = {k: np.asarray(v) for k, v in x.items()}
    z = {k: v[0] for k, v in f.items() if k not in ("rel_bias", "rel_bias_2", "x", "c", "mem_2")}
    sizes = (512, 512, 256, 256, 512, 512, 16, 512, 512, 512, 256, 64, 4, 3072)
    cut = np.cumsum(sizes)[:-1]
    a_u, a_v, gq, gk, gv, gr, ga, dq, dk, dv, iq, ik, iw, gates = np.split(z["w_in"], cut, axis=1)
    misc = np.concatenate([iq, ik, ik, ga, iw, np.zeros((D, P - 20), np.float32)], 1)
    parts = {}
    for n in range(12):
        parts[f"mod{n}"] = [moving_rows(z["w_mod"][:, n * 512:(n + 1) * 512])]
    parts["av"], parts["au"] = [moving_rows(a_v)], [moving_tiles(a_u)]
    parts["gr"] = [moving_tiles(gr)]
    parts["dq"], parts["dk"], parts["dv"] = [moving_tiles(dq)], [moving_tiles(dk)], [moving_rows(dv)]
    for name, w in (("gqk", moving_tiles(np.concatenate([gq, gk], 1))), ("misc", moving_tiles(misc)),
                    ("gv", moving_rows(gv))):
        parts[name + "0"], parts[name + "1"] = [w[:PIECE]], [w[PIECE:]]
    for n in range(3):
        g, u = moving_tiles(gates[:, n * D:(n + 1) * D]), moving_tiles(z["w_branch"][n])
        parts[f"merge{n}"] = [g[0:32], u[0:16], g[32:64], u[16:32]]
        if n == 1:
            parts["merge1a"], parts["merge1b"] = [g[0:32]], [u[0:16], g[32:64], u[16:32]]
    parts["wout"] = [moving_tiles(z["w_out"])]
    for g in range(4):
        es = range(4 * g, 4 * g + 4)
        p = []
        for e in es:
            p += [moving_tiles(z["w_exp_gate"][e]), moving_tiles(z["w_exp_up"][e])]
        p.append(moving_tiles(z["w_exp_down"][4 * g:4 * g + 4].reshape(1024, D)))
        parts[f"moe{g}"] = p
    q, kc, vc, ks, vs, kw, vw, gl, cb, cc, cx = np.split(
        z["w_in_2"], np.cumsum((512,) + (128,) * 6 + (24, 512, 512))[:], axis=1)
    q = q.reshape(D, 2, 4, 64).transpose(0, 2, 1, 3).reshape(D, 512)
    parts["kcvc"] = [moving_tiles(kc), moving_tiles(vc)]
    parts["kskw"] = [moving_tiles(ks), moving_tiles(kw)]
    parts["vsvw"] = [moving_rows(np.concatenate([vs, vw], 1))]
    parts["conv"] = [moving_tiles(w[:, j * P:(j + 1) * P]) for j in range(4) for w in (cc, cx, cb)]
    parts["q"] = [moving_tiles(q)]
    parts["gl"] = [moving_tiles(np.concatenate([gl, np.zeros((D, 2 * P - 24), np.float32)], 1))]
    wo2 = z["w_out_2"]
    wo2 = np.concatenate([wo2[512:], wo2[:512].reshape(2, 4, 64, D).transpose(1, 0, 2, 3).reshape(512, D)], 0)
    parts["wout2"] = [moving_tiles(wo2)]
    parts["memk"] = [moving_tiles(z["mem_wkv_2"][:, :256])]
    parts["memv"] = [moving_rows(z["mem_wkv_2"][:, 256:])]
    parts["memq"], parts["memo"] = [moving_tiles(z["mem_wq_2"])], [moving_tiles(z["mem_wo_2"])]
    at = 0
    for g, nt in enumerate(FFN_TILES):
        p = []
        for m in range(0, nt, 2):
            c = slice((at + m) * P, (at + m + 2) * P)
            p += [moving_tiles(z["ffn_wg_2"][:, c]), moving_tiles(z["ffn_wu_2"][:, c])]
        p.append(moving_tiles(z["ffn_wd_2"][at * P:(at + nt) * P]))
        parts[f"ffn{g}"] = p
        at += nt
    all_tiles = np.concatenate([t for name, _ in STREAM for t in parts[name]], 0)
    assert all_tiles.shape[0] == NPIECES * PIECE, all_tiles.shape
    stream = all_tiles.reshape(NPIECES, PIECE, P, P).transpose(0, 2, 1, 3).reshape(NPIECES, P, PIECE * P)

    cv = {"c": columns(f["c"][0]), "b_mod": columns(z["b_mod"]), "g1": columns(z["g_norm1"]),
          "g2": columns(z["g_norm2"]), "gla_b": columns(z["gla_b_gate"]), "gla_g": columns(z["gla_norm_g"]),
          "qn": columns(z["dsa_qnorm_g"]), "kn": columns(z["dsa_knorm_g"]), "b_gate": columns(z["b_branch_gate"]),
          "norms": columns(z["norms_2"]), "mem_norm": columns(z["mem_norm_2"]),
          "gn_nsa": columns(z["gn_nsa_2"].reshape(2, 4, 64).transpose(1, 0, 2)), "gn_conv": columns(z["gn_conv_2"]),
          "conv_w": columns(z["conv_w_2"]), "eps": np.full((P, 1), 1e-6, np.float32)}
    cols = np.concatenate([cv[k] for k in COLS], 1)
    rows = np.concatenate([z["gmlp_ln_g"], z["gmlp_ln_b"], z["gmlp_b_s"].reshape(-1), z["b_group"], z["b_router"]])
    rel = np.concatenate([np.concatenate([f["rel_bias"], f["rel_bias_2"].T], 1),
                          np.full((1, 12), NEG, np.float32)], 0)
    router = np.concatenate([z["w_group"], z["w_router"]], 1)
    pe = z["cmp_pe_2"].reshape(-1)
    return {
        "stream": stream,
        "xT": f["x"][0].T.reshape(KD, P, S).transpose(1, 0, 2),
        "memT": f["mem_2"][0].T.reshape(KD, P, MEM).transpose(1, 0, 2),
        "cols": cols, "rows": rows, "const": constants(),
        "wsT": z["gmlp_w_s"].transpose(2, 0, 1), "gate2": z["gla_w_gate2"], "rel": rel, "onehot": bucket_onehot(),
        "router": router.reshape(KD, P, 20).transpose(1, 0, 2),
        "cw1": np.stack([z["cmp_k_w1_2"], z["cmp_v_w1_2"]]).reshape(2, PIECE, P, P).transpose(2, 0, 1, 3)
        .reshape(P, 2, PIECE * P),
        "cw2": np.concatenate([z["cmp_k_w2_2"], z["cmp_v_w2_2"]], 1),
        "pe": columns(pe),
    }


_ORDER = ["stream", "xT", "memT", "cols", "rows", "const", "wsT", "gate2", "rel", "onehot", "router", "cw1", "cw2", "pe"]


def kernel(**inputs):
    import concourse.bacc as _bacc
    from concourse.bass_utils import run_bass_kernel_spmd as _run

    nc = _bacc.Bacc("TRN2", target_bir_lowering=False, num_devices=1)
    arrays, args = {}, []
    laid = layout(inputs)
    for name in _ORDER:
        a = np.ascontiguousarray(laid[name])
        arrays[f"in_{name}"] = a
        args.append(nc.dram_tensor(f"in_{name}", a.shape, mybir.dt.from_np(a.dtype), kind="ExternalInput").ap())
    args.append(nc.dram_tensor("out_0", (P, KD, S), F32, kind="ExternalOutput").ap())
    build(nc, *args)
    r = _run(nc, [arrays], core_ids=[0])
    got = np.asarray(r.results[0]["out_0"])
    return np.ascontiguousarray(got.transpose(1, 0, 2).reshape(1, D, S).transpose(0, 2, 1))
```
